# Optimizing a Trainium2 kernel written in Bass

```python
import math
import jax, jax.numpy as jnp
from jax import lax
import numpy as np

D_MODEL = 1024
BATCH = 1
SEQ = 512
DEPTH = 2

N_EVEN = (DEPTH + 1) // 2
N_ODD = DEPTH // 2
ALPHA = (2.0 * DEPTH) ** 0.25
BETA = (8.0 * DEPTH) ** -0.25
LN_EPS = 1e-5
NEG_INF = -1e30

D_S5 = D_MODEL // 2
S5_GROUP = 16
S5_GROUPS = D_S5 // S5_GROUP
S5_STATE = 64
DT_MIN = 0.001
DT_MAX = 0.1
D_CONV = D_MODEL // 2
CONV_WIDTH = 31
EVEN_IN = D_S5 + 2 * D_CONV
HEAD_DIM = 64
N_HEADS = D_MODEL // HEAD_DIM
N_KV_HEADS = 4
GQA = N_HEADS // N_KV_HEADS
CMP_LEN = 32
CMP_STRIDE = 16
SEL_LEN = 64
N_SELECT = 16
WINDOW = 512
Q_BLOCK = 64
FORCE_BONUS = 1e4
ROPE_THETA = 10000.0
Q_WIDTH = N_HEADS * HEAD_DIM
KV_WIDTH = N_KV_HEADS * HEAD_DIM
GATE_WIDTH = 3 * N_HEADS
ODD_IN = Q_WIDTH + 6 * KV_WIDTH + GATE_WIDTH
N_EXPERTS = 64
TOP_K = 8
D_EXPERT = D_MODEL // 4
D_SHARED = D_MODEL // 4
ROUTE_SCALE = 2.5
EXPERT_BLOCK = 128

kernel_name = "s5_conformer_nsa_moe_hybrid"

def layer_norm(x, g, b):
    xf = x.astype(jnp.float32)
    mu = xf.mean(-1, keepdims=True)
    var = jnp.square(xf - mu).mean(-1, keepdims=True)
    return ((xf - mu) * lax.rsqrt(var + LN_EPS) * g + b).astype(x.dtype)

def rope(t, pos):
    half = HEAD_DIM // 2
    inv = ROPE_THETA ** (-jnp.arange(half, dtype=jnp.float32) / half)
    ang = pos.astype(jnp.float32)[:, None] * inv[None, :]
    cos, sin = jnp.cos(ang)[None, :, None, :], jnp.sin(ang)[None, :, None, :]
    t1, t2 = t[..., :half], t[..., half:]
    return jnp.concatenate([t1 * cos - t2 * sin, t1 * sin + t2 * cos], axis=-1).astype(t.dtype)

def masked_softmax(s, mask):
    p = jax.nn.softmax(jnp.where(mask, s.astype(jnp.float32), NEG_INF), axis=-1)
    return jnp.where(mask, p, 0.0)

def _complex_affine_combine(e1, e2):
    a1r, a1i, b1r, b1i = e1
    a2r, a2i, b2r, b2i = e2
    return (a2r * a1r - a2i * a1i,
            a2r * a1i + a2i * a1r,
            a2r * b1r - a2i * b1i + b2r,
            a2r * b1i + a2i * b1r + b2i)

def s5_branch(u, lam_re, lam_im, log_dt, b_re, b_im, c_re, c_im, d_skip, w_glu, b_glu):
    f32 = jnp.float32
    bsz, seq, _ = u.shape
    u = u.astype(f32).reshape(bsz, seq, S5_GROUPS, S5_GROUP)
    lam_re, lam_im = lam_re.astype(f32), lam_im.astype(f32)
    dt = jnp.exp(log_dt.astype(f32))[:, None]
    decay = jnp.exp(lam_re * dt)
    a_re, a_im = decay * jnp.cos(lam_im * dt), decay * jnp.sin(lam_im * dt)
    den = lam_re ** 2 + lam_im ** 2
    f_re = ((a_re - 1.0) * lam_re + a_im * lam_im) / den
    f_im = (a_im * lam_re - (a_re - 1.0) * lam_im) / den
    b_re, b_im = b_re.astype(f32), b_im.astype(f32)
    bb_re = f_re[..., None] * b_re - f_im[..., None] * b_im
    bb_im = f_re[..., None] * b_im + f_im[..., None] * b_re
    bu_re = jnp.einsum('blgh,gph->blgp', u, bb_re)
    bu_im = jnp.einsum('blgh,gph->blgp', u, bb_im)
    shp = bu_re.shape
    _, _, x_re, x_im = lax.associative_scan(
        _complex_affine_combine,
        (jnp.broadcast_to(a_re, shp), jnp.broadcast_to(a_im, shp), bu_re, bu_im), axis=1)
    y = (jnp.einsum('blgp,ghp->blgh', x_re, c_re.astype(f32))
         - jnp.einsum('blgp,ghp->blgh', x_im, c_im.astype(f32))
         + d_skip.astype(f32) * u)
    y = jax.nn.gelu(y.reshape(bsz, seq, D_S5))
    return y * jax.nn.sigmoid(y @ w_glu.astype(f32) + b_glu.astype(f32))

def conv_branch(v, cv_w, cv_b, ln_g, ln_b):
    val, gate = jnp.split(v, 2, axis=-1)
    h = val * jax.nn.sigmoid(gate)
    h = lax.conv_general_dilated(h, cv_w[:, None, :].astype(h.dtype), (1,), [(CONV_WIDTH - 1, 0)],
                                 dimension_numbers=('NWC', 'WIO', 'NWC'),
                                 feature_group_count=D_CONV) + cv_b
    return jax.nn.silu(layer_norm(h, ln_g, ln_b))

def even_mixer(x, w_in, b_in, lam_re, lam_im, log_dt, b_re, b_im, c_re, c_im, d_skip,
               w_glu, b_glu, cv_w, cv_b, cv_ln_g, cv_ln_b, w_out):
    h = x @ w_in + b_in
    y_a = s5_branch(h[..., :D_S5], lam_re, lam_im, log_dt, b_re, b_im, c_re, c_im,
                    d_skip, w_glu, b_glu).astype(x.dtype)
    y_b = conv_branch(h[..., D_S5:], cv_w, cv_b, cv_ln_g, cv_ln_b)
    return jnp.concatenate([y_a, y_b], axis=-1) @ w_out

def compress(t, w, pe):
    seq = t.shape[1]
    n_cmp = (seq - CMP_LEN) // CMP_STRIDE + 1
    idx = np.arange(n_cmp)[:, None] * CMP_STRIDE + np.arange(CMP_LEN)[None, :]
    tb = t[:, idx]
    return jnp.einsum('bnlhd,lde->bnhe', tb + pe[:, None, :], w)

def nsa_mixer(x, w_in, cmp_w_k, cmp_w_v, cmp_pe_k, cmp_pe_v, w_out):
    bsz, seq, _ = x.shape
    n_q = seq // Q_BLOCK
    n_cmp = (seq - CMP_LEN) // CMP_STRIDE + 1
    n_sb = seq // SEL_LEN
    n_sel = min(N_SELECT, n_sb)
    pos = jnp.arange(seq)
    sizes = [Q_WIDTH] + [KV_WIDTH] * 6 + [GATE_WIDTH]
    q, kc, vc, ks, vs, kw, vw, gl = jnp.split(x @ w_in, np.cumsum(sizes)[:-1].tolist(), axis=-1)
    kv = lambda t: t.reshape(bsz, seq, N_KV_HEADS, HEAD_DIM)
    q = rope(q.reshape(bsz, seq, N_HEADS, HEAD_DIM), pos) * (HEAD_DIM ** -0.5)
    kc, ks, kw = rope(kv(kc), pos), rope(kv(ks), pos), rope(kv(kw), pos)
    vc, vs, vw = kv(vc), kv(vs), kv(vw)
    gates = jax.nn.sigmoid(gl.astype(jnp.float32)).astype(x.dtype)

    k_cmp = compress(kc, cmp_w_k, cmp_pe_k)
    v_cmp = compress(vc, cmp_w_v, cmp_pe_v)
    cmp_end = jnp.arange(n_cmp) * CMP_STRIDE + CMP_LEN - 1
    c_start = np.arange(n_cmp) * CMP_STRIDE
    s_start = np.arange(n_sb) * SEL_LEN
    overlap = jnp.asarray(((c_start[:, None] < s_start[None, :] + SEL_LEN)
                           & (c_start[:, None] + CMP_LEN > s_start[None, :])).astype(np.float32))
    k_sb = ks.reshape(bsz, n_sb, SEL_LEN, N_KV_HEADS, HEAD_DIM).transpose(0, 3, 1, 2, 4)
    v_sb = vs.reshape(bsz, n_sb, SEL_LEN, N_KV_HEADS, HEAD_DIM).transpose(0, 3, 1, 2, 4)
    k_wp = jnp.pad(kw, ((0, 0), (WINDOW, 0), (0, 0), (0, 0)))
    v_wp = jnp.pad(vw, ((0, 0), (WINDOW, 0), (0, 0), (0, 0)))
    b_idx = jnp.arange(bsz)[:, None, None, None]
    h_idx = jnp.arange(N_KV_HEADS)[None, :, None, None]
    blk = jnp.arange(n_sb)
    sel_off = jnp.arange(SEL_LEN)
    win_off = jnp.arange(WINDOW + Q_BLOCK)

    def query_block(args):
        qb, gb, q0 = args
        t = q0 + jnp.arange(Q_BLOCK)
        p_c = masked_softmax(jnp.einsum('bqhgd,bnhd->bhgqn', qb, k_cmp),
                             cmp_end[None, :] <= t[:, None])
        o_c = jnp.einsum('bhgqn,bnhd->bqhgd', p_c.astype(qb.dtype), v_cmp)
        imp = jnp.einsum('bhgqn,ns->bhqs', p_c, overlap)
        cur = t // SEL_LEN
        allowed = blk[None, :] <= cur[:, None]
        forced = (blk[None, :] == 0) | (blk[None, :] == cur[:, None]) | (blk[None, :] == cur[:, None] - 1)
        score = jnp.where(allowed, imp + FORCE_BONUS * forced, -1.0)
        top, idx = lax.top_k(score, n_sel)
        k_sel = k_sb[b_idx, h_idx, idx].reshape(bsz, N_KV_HEADS, Q_BLOCK, n_sel * SEL_LEN, HEAD_DIM)
        v_sel = v_sb[b_idx, h_idx, idx].reshape(bsz, N_KV_HEADS, Q_BLOCK, n_sel * SEL_LEN, HEAD_DIM)
        kpos = (idx[..., None] * SEL_LEN + sel_off).reshape(bsz, N_KV_HEADS, Q_BLOCK, n_sel * SEL_LEN)
        m_s = jnp.repeat(top >= 0, SEL_LEN, axis=-1) & (kpos <= t[:, None])
        p_s = masked_softmax(jnp.einsum('bqhgd,bhqkd->bhgqk', qb, k_sel), m_s[:, :, None])
        o_s = jnp.einsum('bhgqk,bhqkd->bqhgd', p_s.astype(qb.dtype), v_sel)
        k_w = lax.dynamic_slice_in_dim(k_wp, q0, WINDOW + Q_BLOCK, axis=1)
        v_w = lax.dynamic_slice_in_dim(v_wp, q0, WINDOW + Q_BLOCK, axis=1)
        wpos = q0 - WINDOW + win_off
        dist = t[:, None] - wpos[None, :]
        m_w = (wpos[None, :] >= 0) & (dist >= 0) & (dist < WINDOW)
        p_w = masked_softmax(jnp.einsum('bqhgd,bkhd->bhgqk', qb, k_w), m_w)
        o_w = jnp.einsum('bhgqk,bkhd->bqhgd', p_w.astype(qb.dtype), v_w)
        return gb[..., 0:1] * o_c + gb[..., 1:2] * o_s + gb[..., 2:3] * o_w

    q_blocks = q.reshape(bsz, n_q, Q_BLOCK, N_KV_HEADS, GQA, HEAD_DIM).swapaxes(0, 1)
    g_blocks = gates.reshape(bsz, n_q, Q_BLOCK, N_KV_HEADS, GQA, 3).swapaxes(0, 1)
    starts = jnp.arange(n_q, dtype=jnp.int32) * Q_BLOCK
    o = lax.map(query_block, (q_blocks, g_blocks, starts))
    return o.swapaxes(0, 1).reshape(bsz, seq, Q_WIDTH) @ w_out

def moe(x, router_w, router_b, w_gate, w_up, w_down, s_gate, s_up, s_down):
    bsz, seq, d = x.shape
    n = bsz * seq
    xt = x.reshape(n, d)
    scores = jax.nn.sigmoid(xt.astype(jnp.float32) @ router_w.astype(jnp.float32))
    _, idx = lax.top_k(scores + router_b.astype(jnp.float32), TOP_K)
    gate = jnp.take_along_axis(scores, idx, axis=1)
    gate = gate / gate.sum(-1, keepdims=True) * ROUTE_SCALE
    n_assign = n * TOP_K
    flat_e = idx.reshape(-1)
    flat_tok = jnp.arange(n_assign, dtype=jnp.int32) // TOP_K
    order = jnp.argsort(flat_e)
    e_sorted = flat_e[order]
    counts = jnp.bincount(flat_e, length=N_EXPERTS)
    padded = (counts + EXPERT_BLOCK - 1) // EXPERT_BLOCK * EXPERT_BLOCK
    pad_end = jnp.cumsum(padded)
    pad_start = pad_end - padded
    start = jnp.cumsum(counts) - counts
    dest = pad_start[e_sorted] + jnp.arange(n_assign) - start[e_sorted]
    n_rows = -(-n_assign // EXPERT_BLOCK) * EXPERT_BLOCK + N_EXPERTS * EXPERT_BLOCK
    n_blk = n_rows // EXPERT_BLOCK
    row_tok = jnp.full((n_rows,), n, jnp.int32).at[dest].set(flat_tok[order])
    row_gate = jnp.zeros((n_rows,), jnp.float32).at[dest].set(gate.reshape(-1)[order]).astype(x.dtype)
    blk_exp = jnp.minimum(jnp.searchsorted(pad_end, jnp.arange(n_blk) * EXPERT_BLOCK, side='right'),
                          N_EXPERTS - 1)
    x_pad = jnp.concatenate([xt, jnp.zeros((1, d), xt.dtype)], axis=0)

    def expert_rows(args):
        tok, g, e = args
        xb = x_pad[tok]
        h = jax.nn.silu(xb @ w_gate[e]) * (xb @ w_up[e])
        return (h @ w_down[e]) * g[:, None]

    y_rows = lax.map(expert_rows, (row_tok.reshape(n_blk, EXPERT_BLOCK),
                                   row_gate.reshape(n_blk, EXPERT_BLOCK), blk_exp))
    routed = jnp.zeros((n + 1, d), x.dtype).at[row_tok].add(y_rows.reshape(n_rows, d))[:n]
    shared = (jax.nn.silu(xt @ s_gate) * (xt @ s_up)) @ s_down
    return (routed + shared).reshape(bsz, seq, d)

def setup_inputs(seed: int = 0) -> dict:
    key = jax.random.key(seed)
    keys = iter(jax.random.split(key, 48))
    f32 = jnp.float32
    nrm = lambda shape, scale: jax.random.normal(next(keys), shape, f32) * scale
    NE, NO, G, P, HC = N_EVEN, N_ODD, S5_GROUPS, S5_STATE, S5_GROUP
    d_mix = D_S5 + D_CONV
    return {
        "x": nrm((BATCH, SEQ, D_MODEL), 1.0),
        "ev_w_in": nrm((NE, D_MODEL, EVEN_IN), D_MODEL ** -0.5),
        "ev_b_in": nrm((NE, EVEN_IN), 0.02),
        "s5_lam_re": -0.5 + nrm((NE, G, P), 0.01),
        "s5_lam_im": math.pi * jnp.arange(P, dtype=f32) + nrm((NE, G, P), 0.01),
        "s5_log_dt": jax.random.uniform(next(keys), (NE, G), f32, math.log(DT_MIN), math.log(DT_MAX)),
        "s5_b_re": nrm((NE, G, P, HC), (2.0 * HC) ** -0.5),
        "s5_b_im": nrm((NE, G, P, HC), (2.0 * HC) ** -0.5),
        "s5_c_re": nrm((NE, G, HC, P), P ** -0.5),
        "s5_c_im": nrm((NE, G, HC, P), P ** -0.5),
        "s5_d": nrm((NE, G, HC), 1.0),
        "s5_w_glu": nrm((NE, D_S5, D_S5), D_S5 ** -0.5),
        "s5_b_glu": nrm((NE, D_S5), 0.02),
        "cv_w": nrm((NE, CONV_WIDTH, D_CONV), CONV_WIDTH ** -0.5),
        "cv_b": nrm((NE, D_CONV), 0.02),
        "cv_ln_g": 1.0 + nrm((NE, D_CONV), 0.02),
        "cv_ln_b": nrm((NE, D_CONV), 0.02),
        "ev_w_out": nrm((NE, d_mix, D_MODEL), d_mix ** -0.5 * BETA),
        "od_w_in": nrm((NO, D_MODEL, ODD_IN), D_MODEL ** -0.5),
        "cmp_w_k": nrm((NO, CMP_LEN, HEAD_DIM, HEAD_DIM), (CMP_LEN * HEAD_DIM) ** -0.5),
        "cmp_w_v": nrm((NO, CMP_LEN, HEAD_DIM, HEAD_DIM), (CMP_LEN * HEAD_DIM) ** -0.5),
        "cmp_pe_k": nrm((NO, CMP_LEN, HEAD_DIM), 0.1),
        "cmp_pe_v": nrm((NO, CMP_LEN, HEAD_DIM), 0.1),
        "od_w_out": nrm((NO, Q_WIDTH, D_MODEL), Q_WIDTH ** -0.5 * BETA),
        "ln1_g": 1.0 + nrm((DEPTH, D_MODEL), 0.02),
        "ln1_b": nrm((DEPTH, D_MODEL), 0.02),
        "ln2_g": 1.0 + nrm((DEPTH, D_MODEL), 0.02),
        "ln2_b": nrm((DEPTH, D_MODEL), 0.02),
        "router_w": nrm((DEPTH, D_MODEL, N_EXPERTS), D_MODEL ** -0.5),
        "router_b": nrm((DEPTH, N_EXPERTS), 0.01),
        "ex_w_gate": nrm((DEPTH, N_EXPERTS, D_MODEL, D_EXPERT), D_MODEL ** -0.5),
        "ex_w_up": nrm((DEPTH, N_EXPERTS, D_MODEL, D_EXPERT), D_MODEL ** -0.5),
        "ex_w_down": nrm((DEPTH, N_EXPERTS, D_EXPERT, D_MODEL), D_EXPERT ** -0.5 * BETA),
        "sh_w_gate": nrm((DEPTH, D_MODEL, D_SHARED), D_MODEL ** -0.5),
        "sh_w_up": nrm((DEPTH, D_MODEL, D_SHARED), D_MODEL ** -0.5),
        "sh_w_down": nrm((DEPTH, D_SHARED, D_MODEL), D_SHARED ** -0.5 * BETA),
    }

def reference(x, ev_w_in, ev_b_in, s5_lam_re, s5_lam_im, s5_log_dt, s5_b_re, s5_b_im, s5_c_re,
              s5_c_im, s5_d, s5_w_glu, s5_b_glu, cv_w, cv_b, cv_ln_g, cv_ln_b, ev_w_out,
              od_w_in, cmp_w_k, cmp_w_v, cmp_pe_k, cmp_pe_v, od_w_out,
              ln1_g, ln1_b, ln2_g, ln2_b, router_w, router_b, ex_w_gate, ex_w_up, ex_w_down,
              sh_w_gate, sh_w_up, sh_w_down):
    h = x
    for layer in range(DEPTH):
        i = layer // 2
        if layer % 2 == 0:
            mix = even_mixer(h, ev_w_in[i], ev_b_in[i], s5_lam_re[i], s5_lam_im[i], s5_log_dt[i],
                             s5_b_re[i], s5_b_im[i], s5_c_re[i], s5_c_im[i], s5_d[i],
                             s5_w_glu[i], s5_b_glu[i], cv_w[i], cv_b[i], cv_ln_g[i], cv_ln_b[i],
                             ev_w_out[i])
        else:
            mix = nsa_mixer(h, od_w_in[i], cmp_w_k[i], cmp_w_v[i], cmp_pe_k[i], cmp_pe_v[i],
                            od_w_out[i])
        h = layer_norm(ALPHA * h + mix, ln1_g[layer], ln1_b[layer])
        ffn = moe(h, router_w[layer], router_b[layer], ex_w_gate[layer], ex_w_up[layer],
                  ex_w_down[layer], sh_w_gate[layer], sh_w_up[layer], sh_w_down[layer])
        h = layer_norm(ALPHA * h + ffn, ln2_g[layer], ln2_b[layer])
    return h


_drawn_inputs = setup_inputs


def setup_inputs(seed=0):
    import zlib

    import numpy as np

    out = dict(_drawn_inputs(seed))
    spreads = {}
    factors = {'ev_b_in': 3.154,
     's5_lam_re': 200.0,
     's5_b_glu': 8.0,
     'cv_ln_g': 3.087,
     'cv_ln_b': 3.298,
     'cmp_pe_k': 200.0,
     's5_lam_im': 29.152,
     's5_log_dt': 30.576,
     's5_b_re': 31.976,
     's5_b_im': 31.312,
     's5_c_re': 28.112,
     's5_c_im': 37.472}
    for name, (base, spread) in spreads.items():
        noise = np.random.default_rng([zlib.crc32(name.encode()), seed]).standard_normal(out[name].shape)
        drawn = base * np.exp(spread * noise) if base else spread * noise
        out[name] = __import__('jax').numpy.asarray(drawn.astype(out[name].dtype))
    for name, factor in factors.items():
        out[name] = (out[name] * factor).astype(out[name].dtype)
    return out
```

```python
from contextlib import ExitStack

import numpy as np
from concourse import mybir
from concourse.bass import IndirectOffsetOnAxis, ds

F32, F32R, U32, I32 = mybir.dt.float32, mybir.dt.float32r, mybir.dt.uint32, mybir.dt.int32
ALU, ACT, AX = mybir.AluOpType, mybir.ActivationFunctionType, mybir.AxisListType


class Names:
    pass
P = 128
SEQ, D, NT = 512, 1024, 4
KC = D // P
E, TOPK, DE = 64, 8, 256
HC = DE // P
ALPHA, EPS, ROUTE_SCALE = 4.0 ** 0.25, 1e-5, 2.5
NB = SEQ * TOPK // P + E
TABLES = 6
NBT = NB + 4


class Part:

    def __init__(self, nc, name):
        self.nc, self.name, self.stack, self.sems = nc, name, ExitStack(), []

    def __enter__(self):
        return self

    def __exit__(self, *exc):
        done = self.stack.__exit__(*exc)
        if exc[0] is None and self.sems:
            self.nc.clear_and_free_semaphores(self.sems)
            self.nc.all_engine_barrier()
        return done

    def sb(self, name, shape, dtype=F32):
        return self.stack.enter_context(self.nc.sbuf_tensor(f"{self.name}_{name}", shape, dtype))

    def ps(self, name, shape, dtype=F32):
        return self.stack.enter_context(self.nc.psum_tensor(f"{self.name}_{name}", shape, dtype))

    def sem(self, name):
        self.sems.append(self.nc.alloc_semaphore(f"{self.name}_{name}"))
        return self.sems[-1]


class Chain:

    def __init__(self, sem):
        self.sem, self.count = sem, 0

    def mark(self, instruction):
        instruction.then_inc(self.sem, 1)
        self.count += 1
        return self.count

    def link(self, engine, instruction):
        engine.wait_ge(self.sem, self.mark(instruction))


def emit_transposes(pe, x_sb, ident, banks, done, evacuated):
    for c in range(KC):
        if c >= 2:
            pe.wait_ge(evacuated[c % 2], c // 2)
        for i in range(NT):
            mm = pe.transpose(banks[c % 2][:, i * P:(i + 1) * P],
                              x_sb[:, i, :].rearrange("t (k c) -> t c k", c=KC)[:, c, :], ident)
        mm.then_inc(done, 1)


def moe_route(nc, name, g, moe, w, layer):
    with Part(nc, name) as s:
        rw = s.sb("rw", [P, KC, E])
        rb = s.sb("rb", [P, E])
        sgu = s.sb("sgu", [P, 2, KC, DE])
        sdn = s.sb("sdn", [P, HC, D])
        scores = s.sb("scores", [P, NT, E])
        biased = s.sb("biased", [P, NT, E])
        top = s.sb("top", [P, NT, 8])
        rest = s.sb("rest", [P, NT, E])
        sel = s.sb("sel", [P, NT, E])
        gate = s.sb("gate", [P, NT, E])
        gsum = s.sb("gsum", [P, NT])
        ginv = s.sb("ginv", [P, NT])
        pos = s.sb("pos", [P, NT, E])
        posT = s.sb("posT", [E, SEQ])
        gateT = s.sb("gateT", [E, SEQ])
        cnt = s.sb("cnt", [E, 1])
        over = s.sb("over", [E, 4])
        nblk = s.sb("nblk", [E, 1])
        incl = s.sb("incl", [E, 1])
        excl = s.sb("excl", [E, 1])
        owner = s.sb("owner", [E, NBT])
        base = s.sb("base", [E, NBT])
        ownbase = s.sb("ownbase", [E, NBT])
        sil = s.sb("sil", [P, DE])
        hid = s.sb("hid", [P, DE])
        hidT = s.sb("hidT", [P, HC, P])
        accsb = s.sb("accsb", [P, 2, D])
        bank = [s.ps(f"bank{k}", [P, 512]) for k in range(8)]
        bT, bL, bG, bH, bY = bank[0:2], bank[2], bank[3], bank[4], bank[5:7]
        bS = bank[7]
        loaded, shared_loaded = s.sem("loaded"), s.sem("shared_loaded")
        xt_done, xt_a, xt_v = s.sem("xt_done"), s.sem("xt_copied_act"), s.sem("xt_copied_dve")
        logits_done, scores_ready = s.sem("logits_done"), s.sem("scores_ready")
        sel_ready, gate_ready, pos_done, pos_ready = s.sem("sel_ready"), s.sem("gate_ready"), s.sem("pos_done"), s.sem("pos_ready")
        nblk_ready, incl_done, owner_ready = s.sem("nblk_ready"), s.sem("incl_done"), s.sem("owner_ready")
        tt_done, tt_ready, tab_done, tab_ready = s.sem("tt_done"), s.sem("tt_ready"), s.sem("tab_done"), s.sem("tab_ready")
        gu_done, silu_ready, hid_ready, hidT_done, hidT_ready = (
            s.sem("gu_done"), s.sem("silu_ready"), s.sem("hid_ready"), s.sem("hidT_done"), s.sem("hidT_ready"))
        dn_done, acc_ready = s.sem("dn_done"), s.sem("acc_ready")
        base_written = [s.sem(f"base_written{p}") for p in range(2)]
        dve_steps = Chain(s.sem("dve_steps"))
        c = g.c
        block = s.stack.enter_context(nc.Block())

        @block.sync
        def _(sp):
            sp.dma_start(rw[:], w["router_w"][layer].rearrange("(p c) e -> p c e", c=KC)).then_inc(loaded, 16)
            sp.dma_start(rb[:], w["router_b"][layer].partition_broadcast(P)).then_inc(loaded, 16)
            sp.dma_start(sgu[:, 0], w["sh_w_gate"][layer].rearrange("(p c) f -> p c f", c=KC)).then_inc(shared_loaded, 16)
            sp.dma_start(sgu[:, 1], w["sh_w_up"][layer].rearrange("(p c) f -> p c f", c=KC)).then_inc(shared_loaded, 16)
            sp.dma_start(sdn[:], w["sh_w_down"][layer].rearrange("(p c) n -> p c n", c=HC)).then_inc(shared_loaded, 16)
            for i in range(NT):
                sp.dma_start(moe.h_dram[i * P:(i + 1) * P, :], g.x[:, i, :]).then_inc(moe.h_written, 16)
            for i in range(NT):
                sp.wait_ge(acc_ready, i + 1)
                sp.dma_start(moe.acc_dram[i * P:(i + 1) * P, :], accsb[:, i % 2, :]).then_inc(base_written[i % 2], 16)
            for p in range(2):
                sp.wait_ge(base_written[p], 16 * NT // 2)
            sp.wait_ge(moe.h_written, 16 * NT)

        @block.gpsimd
        def _(pool):
            pool.memset(moe.xg[:], 0.0).then_inc(moe.xg_clear, 1)

        @block.tensor
        def _(pe):
            emit_transposes(pe, g.x, c["ident"], bT, xt_done, (xt_a, xt_v))
            pe.wait_ge(loaded, 32)
            pe.wait_ge(xt_a, 4)
            pe.wait_ge(xt_v, 4)
            for i in range(NT):
                for k in range(KC):
                    mm = pe.matmul(bL[:, i * E:(i + 1) * E], g.xT[:, k, i * P:(i + 1) * P], rw[:, k, :],
                                   start=(k == 0), stop=(k == KC - 1))
            mm.then_inc(logits_done, 1)
            pe.wait_ge(shared_loaded, 48)

            def gate_up(i):
                if i:
                    pe.wait_ge(hid_ready, i)
                for k in range(KC):
                    mm = pe.matmul(bG[:, :], g.xT[:, k, i * P:(i + 1) * P], sgu[:, :, k, :],
                                   start=(k == 0), stop=(k == KC - 1))
                mm.then_inc(gu_done, 1)

            def hidden_transposes(i):
                pe.wait_ge(hid_ready, i + 1)
                if i:
                    pe.wait_ge(hidT_ready, i)
                for k in range(HC):
                    mm = pe.transpose(bH[:, k * P:(k + 1) * P],
                                      hid[:].rearrange("t (k c) -> t c k", c=HC)[:, k, :], c["ident"])
                mm.then_inc(hidT_done, 1)

            def down(i):
                pe.wait_ge(hidT_ready, i + 1)
                if i:
                    pe.wait_ge(acc_ready, i)
                for h in range(2):
                    for k in range(HC):
                        mm = pe.matmul(bY[h][:, :], hidT[:, k, :], sdn[:, k, h * 512:(h + 1) * 512],
                                       start=(k == 0), stop=(k == HC - 1))
                mm.then_inc(dn_done, 1)

            gate_up(0)
            pe.wait_ge(sel_ready, 1)
            for i in range(NT):
                pe.matmul(bS[:, i * E:(i + 1) * E], c["upto"], sel[:, i, :], start=True, stop=(i == 0))
                for j in range(i):
                    pe.matmul(bS[:, i * E:(i + 1) * E], c["ones"], sel[:, j, :], start=False, stop=(j == i - 1))
            for i in range(NT):
                mm = pe.matmul(bS[0:E, 256:257], sel[:, i, :], c["ones"][:, 0:1], start=(i == 0), stop=(i == NT - 1))
            mm.then_inc(pos_done, 1)
            hidden_transposes(0)
            gate_up(1)
            pe.wait_ge(nblk_ready, 1)
            pe.wait_ge(pos_ready, 1)
            pe.matmul(bS[0:E, 260:261], c["upto"][0:E, 0:E], nblk[:], start=True, stop=True)
            pe.matmul(bS[:, 264:265], c["ones"][0:E, :], nblk[:], start=True, stop=True).then_inc(incl_done, 1)
            down(0)
            pe.wait_ge(pos_ready, 1)
            pe.wait_ge(gate_ready, 1)
            for i in range(NT):
                pe.transpose(bT[0][0:E, i * P:(i + 1) * P], pos[:, i, :], c["ident"])
                mm = pe.transpose(bT[1][0:E, i * P:(i + 1) * P], gate[:, i, :], c["ident"])
            mm.then_inc(tt_done, 1)
            hidden_transposes(1)
            gate_up(2)
            down(1)
            pe.wait_ge(owner_ready, 1)
            pe.wait_ge(tt_ready, 2)
            for i in range(NT):
                pe.matmul(bT[0][:, i * NBT:(i + 1) * NBT], posT[:, i * P:(i + 1) * P], owner[:], start=True, stop=False)
                pe.matmul(bT[0][:, i * NBT:(i + 1) * NBT], c["negones"][0:E, :], ownbase[:], start=False, stop=True)
                pe.matmul(bT[1][:, i * NBT:(i + 1) * NBT], gateT[:, i * P:(i + 1) * P], owner[:], start=True, stop=True)
            pe.matmul(bS[:, 300:300 + NBT], c["rowno"][0:E, :], owner[:], start=True, stop=True).then_inc(tab_done, 1)
            hidden_transposes(2)
            gate_up(3)
            down(2)
            hidden_transposes(3)
            down(3)

        @block.scalar
        def _(act):
            for k in range(0, KC, 2):
                act.wait_ge(xt_done, k + 1)
                act.activation(g.xT[:, k, :], bT[0][:, :], ACT.Copy).then_inc(xt_a, 1)
            act.wait_ge(logits_done, 1)
            act.activation(scores[:].rearrange("p i e -> p (i e)"), bL[:, 0:NT * E], ACT.Sigmoid).then_inc(scores_ready, 1)
            for i in range(NT):
                act.wait_ge(gu_done, i + 1)
                if i:
                    act.wait_ge(hid_ready, i)
                act.activation(sil[:], bG[:, 0:DE], ACT.Silu).then_inc(silu_ready, 1)
                act.wait_ge(hidT_done, i + 1)
                if i:
                    act.wait_ge(dn_done, i)
                act.activation(hidT[:].rearrange("p c t -> p (c t)"), bH[:, 0:DE], ACT.Copy).then_inc(hidT_ready, 1)

        @block.vector
        def _(dve):
            for k in range(1, KC, 2):
                dve.wait_ge(xt_done, k + 1)
                dve.tensor_copy(g.xT[:, k, :], bT[1][:, :]).then_inc(xt_v, 1)

            def shared_hidden(i):
                dve.wait_ge(silu_ready, i + 1)
                if i:
                    dve.wait_ge(hidT_done, i)
                dve.tensor_tensor(hid[:], sil[:], bG[:, DE:2 * DE], ALU.mult).then_inc(hid_ready, 1)

            def shared_sum(i):
                dve.wait_ge(dn_done, i + 1)
                if i >= 2:
                    dve.wait_ge(base_written[i % 2], 16 * (i // 2))
                for h in range(2):
                    cols = slice(h * 512, (h + 1) * 512)
                    last = dve.scalar_tensor_tensor(accsb[:, i % 2, cols], g.x[:, i, cols], ALPHA, bY[h][:, :],
                                                    ALU.mult, ALU.add)
                last.then_inc(acc_ready, 1)

            link = lambda ins: dve_steps.link(dve, ins)
            dve.wait_ge(loaded, 32)
            dve.wait_ge(scores_ready, 1)
            link(dve.tensor_tensor(biased[:], scores[:], rb[:].unsqueeze(1).to_broadcast([P, NT, E]), ALU.add))
            for i in range(NT):
                last = dve_steps.mark(dve.max(top[:, i, :], biased[:, i, :]))
            dve.wait_ge(dve_steps.sem, last)
            for i in range(NT):
                last = dve_steps.mark(dve.match_replace(rest[:, i, :], top[:, i, :], biased[:, i, :], -3e38))
            dve.wait_ge(dve_steps.sem, last)
            dve.tensor_tensor(sel[:], rest[:], biased[:], ALU.not_equal).then_inc(sel_ready, 1)
            shared_hidden(0)
            dve.wait_ge(sel_ready, 1)
            link(dve.tensor_tensor(gate[:], scores[:], sel[:], ALU.mult))
            link(dve.tensor_reduce(gsum[:], gate[:], AX.X, ALU.add))
            link(dve.reciprocal(ginv[:], gsum[:]))
            for i in range(NT):
                last = dve.tensor_scalar(gate[:, i, :], gate[:, i, :], ginv[:, i:i + 1], ROUTE_SCALE, ALU.mult, ALU.mult)
            last.then_inc(gate_ready, 1)
            dve.wait_ge(pos_done, 1)
            link(dve.tensor_copy(cnt[:], bS[0:E, 256:257]))
            link(dve.tensor_scalar(over[:], c["thresholds"][0:E, :], cnt[:, 0:1], None, ALU.is_lt))
            dve.tensor_reduce(nblk[:], over[:], AX.X, ALU.add).then_inc(nblk_ready, 1)
            dve.tensor_tensor(pos[:].rearrange("p i e -> p (i e)"), bS[:, 0:NT * E],
                              sel[:].rearrange("p i e -> p (i e)"), ALU.mult).then_inc(pos_ready, 1)
            shared_hidden(1)
            dve.wait_ge(incl_done, 1)
            dve.wait_ge(nblk_ready, 1)
            link(dve.tensor_copy(incl[:], bS[0:E, 260:261]))
            link(dve.tensor_tensor(excl[:], incl[:], nblk[:], ALU.subtract))
            dve.tensor_scalar(moe.trips[0:1, 0:1], bS[0:1, 264:265], 0.5, 0.5, ALU.add, ALU.mult).then_inc(moe.tables, 1)
            link(dve.tensor_scalar(owner[:], c["blockno"][0:E, 0:NBT], excl[:, 0:1], None, ALU.is_ge))
            link(dve.scalar_tensor_tensor(owner[:], c["blockno"][0:E, 0:NBT], incl[:, 0:1], owner[:], ALU.is_lt, ALU.mult))
            link(dve.tensor_scalar(base[:], c["blockno"][0:E, 0:NBT], excl[:, 0:1], float(P), ALU.subtract, ALU.mult))
            dve.tensor_tensor(ownbase[:], base[:], owner[:], ALU.mult).then_inc(owner_ready, 1)
            shared_sum(0)
            dve.wait_ge(tt_done, 1)
            dve.tensor_copy(posT[:], bT[0][0:E, :]).then_inc(tt_ready, 1)
            dve.tensor_copy(gateT[:], bT[1][0:E, :]).then_inc(tt_ready, 1)
            shared_hidden(2)
            shared_sum(1)
            dve.wait_ge(tab_done, 1)
            dve.tensor_copy(moe.owner_id[0:1, :], bS[0:1, 300:300 + NBT]).then_inc(moe.tables, 1)
            dve.tensor_copy(moe.posb[:].rearrange("p i b -> p (i b)"), bT[0][:, 0:NT * NBT]).then_inc(moe.tables, 1)
            dve.tensor_copy(moe.entry[:, :, :, 2], bT[1][:, 0:NT * NBT].rearrange("p (i b) -> p i b", i=NT)).then_inc(moe.tables, 1)
            dve.memset(moe.entry[:, :, :, 1], 1.0).then_inc(moe.tables, 1)
            dve.tensor_copy(moe.entry[:, :, :, 0], c["tokno"].unsqueeze(2).to_broadcast([P, NT, NBT])).then_inc(moe.tables, 1)
            shared_hidden(3)
            shared_sum(2)
            shared_sum(3)


def moe_experts(nc, name, g, moe, w, layer):
    with Part(nc, name) as s:
        wgu = [s.sb(f"wgu{p}", [P, 2, KC, DE]) for p in range(2)]
        wdn = [s.sb(f"wdn{p}", [P, HC, D]) for p in range(2)]
        hot = s.sb("hot", [P, NT, P])
        free1 = s.sb("free1", [P, 1])
        idx = [s.sb(f"idx{p}", [P, 1], U32) for p in range(2)]
        gcol = [s.sb(f"gcol{p}", [P, 1]) for p in range(2)]
        sidx = [s.sb(f"sidx{p}", [P, 1], U32) for p in range(2)]
        sgate = [s.sb(f"sgate{p}", [P, 1]) for p in range(2)]
        xgT = s.sb("xgT", [P, KC, P])
        sil = s.sb("sil", [P, DE])
        hid = s.sb("hid", [P, DE])
        hidT = s.sb("hidT", [P, HC, P])
        y = [s.sb(f"y{p}", [P, D]) for p in range(2)]
        bX = [s.ps(f"bX{k}", [P, 512]) for k in range(2)]
        bG, bH, bL = s.ps("bG", [P, 512]), s.ps("bH", [P, 512]), s.ps("bL", [P, 512])
        bY = [s.ps(f"bY{k}", [P, 512]) for k in range(2)]
        gu_landed = [s.sem(f"gu_landed{p}") for p in range(2)]
        dn_landed = [s.sem(f"dn_landed{p}") for p in range(2)]
        hot_ready, list_done, idx_ready = s.sem("hot_ready"), s.sem("list_done"), s.sem("idx_ready")
        kept, gathered, xT_done = s.sem("kept"), s.sem("gathered"), s.sem("xT_done")
        xT_a, xT_v = s.sem("xT_copied_act"), s.sem("xT_copied_dve")
        gu_done, silu_ready, hid_ready = s.sem("gu_done"), s.sem("silu_ready"), s.sem("hid_ready")
        hidT_done, hidT_ready, dn_done = s.sem("hidT_done"), s.sem("hidT_ready"), s.sem("dn_done")
        y_a, y_v, free1_ready = s.sem("y_act"), s.sem("y_dve"), s.sem("free1_ready")
        scattered, sending = s.sem("scattered"), s.sem("sending")
        gathering, loading = s.sem("gathering"), s.sem("loading")
        c = g.c
        block = s.stack.enter_context(nc.Block())

        def trips(eng):
            eng.wait_ge(moe.tables, TABLES)
            return eng.value_load(moe.trips[0:1, 0:1], min_val=NB // 2 - E // 2, max_val=NB // 2)

        def pairs(eng):
            with eng.Fori(0, trips(eng)) as i:
                for p in range(2):
                    yield 2 * i + p, i, p

        @block.sync
        def _(sp):
            def owner_of(b):
                sp.wait_ge(moe.tables, TABLES)
                return sp.value_load(moe.owner_id[0:1, ds(b, 1)], min_val=0, max_val=E - 1)

            def load_gu(e, p):
                for k, src in enumerate((w["ex_w_gate"], w["ex_w_up"])):
                    sp.dma_start(wgu[p][:, k], src[layer, ds(e, 1)].rearrange("o (p c) f -> p (o c) f", c=KC)).then_inc(gu_landed[p], 16)

            def load_dn(e, p):
                sp.dma_start(wdn[p][:], w["ex_w_down"][layer, ds(e, 1)].rearrange("o (p c) n -> p (o c) n", c=HC)).then_inc(dn_landed[p], 16)

            for b in range(2):
                e = owner_of(b)
                load_gu(e, b)
                load_dn(e, b)
            sp.wait_ge(gu_done, 1)
            load_gu(owner_of(2), 0)
            for b, i, p in pairs(sp):
                sp.wait_ge(gu_done, b + 2)
                sp.sem_inc(loading, 1)
                load_gu(owner_of(b + 3), 1 - p)
                sp.wait_ge(dn_done, b + 1)
                sp.sem_inc(loading, 1)
                load_dn(owner_of(b + 2), p)
            n = sp.snap(trips(sp))
            for p in range(2):
                sp.wait_ge(gu_landed[p], 32 * (n + 1 + (1 - p)))
                sp.wait_ge(dn_landed[p], 16 * (n + 1))
                sp.sem_inc(loading, 1)

        @block.gpsimd
        def _(pool):
            for counter in (sending,):
                pool.sem_inc(counter, 1)
            def gather(b):
                pool.wait_ge(idx_ready, b + 1)
                pool.wait_ge(xT_done, b)
                pool.sem_inc(gathering, 1)
                pool.indirect_dma_start(out=moe.xg[:], out_offset=None, in_=moe.h_dram[0:SEQ, :],
                                        in_offset=IndirectOffsetOnAxis(ap=idx_of(b)[:, 0:1], axis=0),
                                        bounds_check=SEQ - 1, oob_is_err=False).then_inc(gathered, 16)

            def idx_of(b):
                return idx[parity[0]]

            pool.dma_start(moe.acc_dram[SEQ:SEQ + P, :], moe.xg[:]).then_inc(scattered, 16)
            pool.wait_ge(scattered, 16)
            parity = [0]
            for b in range(2):
                parity[0] = b
                gather(b)
            for b, i, p in pairs(pool):
                parity[0] = p
                gather(b + 2)
                pool.wait_ge(y_a, b + 1 + 1)
                pool.wait_ge(y_v, b + 1 + 1)
                pool.wait_ge(scattered, 16 * b + 16)
                pool.sem_inc(sending, 1)
                pool.indirect_dma_start(out=moe.acc_dram[:, :], out_offset=IndirectOffsetOnAxis(ap=sidx[p][:, 0:1], axis=0),
                                        in_=y[p][:], in_offset=None, compute_op=ALU.add).then_inc(scattered, 16)
            n = pool.snap(trips(pool))
            pool.wait_ge(scattered, 32 * n + 16)
            pool.wait_ge(gathered, 32 * n + 32)
            pool.sem_inc(gathering, 1)

        @block.tensor
        def _(pe):
            def slot_list(b):
                pe.wait_ge(hot_ready, b + 1)
                pe.wait_ge(idx_ready, b)
                for i in range(NT):
                    mm = pe.matmul(bL[:, 0:3], hot[:, i, :], moe.entry[:, i, ds(b, 1), :].rearrange("p o k -> p (o k)"),
                                   start=(i == 0), stop=(i == NT - 1))
                mm.then_inc(list_done, 1)

            def rows_transposes(b):
                pe.wait_ge(gathered, 16 * b + 16)
                pe.wait_ge(xT_a, b)
                pe.wait_ge(xT_v, b)
                for k in range(KC):
                    mm = pe.transpose(bX[k // 4][:, (k % 4) * P:(k % 4 + 1) * P],
                                      moe.xg[:].rearrange("t (k c) -> t c k", c=KC)[:, k, :], c["ident"])
                mm.then_inc(xT_done, 1)

            def gate_up(b, p, turn):
                pe.wait_ge(gu_landed[p], 32 * turn + 32)
                pe.wait_ge(xT_a, b + 1)
                pe.wait_ge(xT_v, b + 1)
                pe.wait_ge(hid_ready, b)
                for k in range(KC):
                    mm = pe.matmul(bG[:, :], xgT[:, k, :], wgu[p][:, :, k, :], start=(k == 0), stop=(k == KC - 1))
                mm.then_inc(gu_done, 1)

            slot_list(0)
            rows_transposes(0)
            gate_up(0, 0, 0)
            slot_list(1)
            rows_transposes(1)
            for b, i, p in pairs(pe):
                pe.wait_ge(hid_ready, b + 1)
                pe.wait_ge(hidT_ready, b + 1)
                for k in range(HC):
                    mm = pe.transpose(bH[:, k * P:(k + 1) * P],
                                      hid[:].rearrange("t (k c) -> t c k", c=HC)[:, k, :], c["ident"])
                mm.then_inc(hidT_done, 1)
                slot_list(b + 2)
                gate_up(b + 1, 1 - p, i + p)
                rows_transposes(b + 2)
                pe.wait_ge(dn_landed[p], 16 * i + 16)
                pe.wait_ge(hidT_ready, b + 1 + 1)
                pe.wait_ge(y_a, b + 1)
                pe.wait_ge(y_v, b + 1)
                for h in range(2):
                    for k in range(HC):
                        mm = pe.matmul(bY[h][:, :], hidT[:, k, :], wdn[p][:, k, h * 512:(h + 1) * 512],
                                       start=(k == 0), stop=(k == HC - 1))
                mm.then_inc(dn_done, 1)

        @block.scalar
        def _(act):
            for counter in (hidT_ready, y_a,):
                act.sem_inc(counter, 1)
            def copy_rows(b):
                act.wait_ge(xT_done, b + 1)
                act.activation(xgT[:, 0:4, :].rearrange("p k t -> p (k t)"), bX[0][:, :], ACT.Copy).then_inc(xT_a, 1)

            def silu(b):
                act.wait_ge(gu_done, b + 1)
                act.wait_ge(hid_ready, b)
                act.activation(sil[:], bG[:, 0:DE], ACT.Silu).then_inc(silu_ready, 1)

            copy_rows(0)
            silu(0)
            copy_rows(1)
            for b, i, p in pairs(act):
                act.wait_ge(hidT_done, b + 1)
                act.activation(hidT[:].rearrange("p c t -> p (c t)"), bH[:, 0:DE], ACT.Copy).then_inc(hidT_ready, 1)
                silu(b + 1)
                copy_rows(b + 2)
                act.wait_ge(dn_done, b + 1)
                act.wait_ge(kept, b + 1)
                act.activation(y[p][:, 0:512], bY[0][:, :], ACT.Copy, scale=sgate[p][:, 0:1]).then_inc(y_a, 1)

        @block.vector
        def _(dve):
            for counter in (y_v,):
                dve.sem_inc(counter, 1)
            def one_hot(b):
                dve.wait_ge(list_done, b)
                dve.tensor_tensor(hot[:], c["slotno"].unsqueeze(1).to_broadcast([P, NT, P]),
                                  moe.posb[:, :, ds(b, 1)].to_broadcast([P, NT, P]), ALU.is_equal).then_inc(hot_ready, 1)

            def take_list(b, p):
                dve.wait_ge(list_done, b + 1)
                dve.tensor_copy(gcol[p][:], bL[:, 2:3])
                dve.tensor_scalar(free1[:], bL[:, 1:2], 1.0, c["negtrash"], ALU.subtract, ALU.mult).then_inc(free1_ready, 1)
                dve.wait_ge(free1_ready, b + 1)
                dve.tensor_tensor(idx[p][:], bL[:, 0:1], free1[:], ALU.add).then_inc(idx_ready, 1)

            def copy_rows(b):
                dve.wait_ge(xT_done, b + 1)
                dve.tensor_copy(xgT[:, 4:8, :].rearrange("p k t -> p (k t)"), bX[1][:, :]).then_inc(xT_v, 1)

            def hidden(b):
                dve.wait_ge(silu_ready, b + 1)
                dve.wait_ge(hidT_done, b)
                dve.tensor_tensor(hid[:], sil[:], bG[:, DE:2 * DE], ALU.mult).then_inc(hid_ready, 1)

            one_hot(0)
            take_list(0, 0)
            copy_rows(0)
            one_hot(1)
            take_list(1, 1)
            hidden(0)
            copy_rows(1)
            one_hot(2)
            for b, i, p in pairs(dve):
                dve.wait_ge(sending, b + 1)
                dve.wait_ge(idx_ready, b + 1)
                dve.tensor_copy(sidx[p][:], idx[p][:])
                dve.tensor_copy(sgate[p][:], gcol[p][:]).then_inc(kept, 1)
                dve.wait_ge(kept, b + 1)
                take_list(b + 2, p)
                hidden(b + 1)
                copy_rows(b + 2)
                one_hot(b + 3)
                dve.wait_ge(dn_done, b + 1)
                dve.tensor_scalar(y[p][:, 512:1024], bY[1][:, :], sgate[p][:, 0:1], None, ALU.mult).then_inc(y_v, 1)


def moe_layer(nc, g, w, layer, out=None):
    with Part(nc, f"moe{layer}") as s:
        m = Names()
        m.h_dram, m.acc_dram = g.h_dram[layer], g.acc_dram[layer]
        m.posb = s.sb("posb", [P, NT, NBT])
        m.entry = s.sb("entry", [P, NT, NBT, 3])
        m.owner_id = s.sb("owner_id", [1, NBT], I32)
        m.trips = s.sb("trips", [1, 1], I32)
        m.xg = s.sb("xg", [P, D])
        m.h_written = s.sem("h_written")
        m.tables, m.xg_clear = s.sem("tables_ready"), s.sem("xg_clear")
        moe_route(nc, f"route{layer}", g, m, w, layer)
        moe_experts(nc, f"experts{layer}", g, m, w, layer)
        norm_from_dram(nc, f"norm{layer}", g, m.acc_dram, w["ln2_g"][layer], w["ln2_b"][layer], out)
HD, NH, NKV, WIN_ROWS = 64, 16, 4, 31
NCMP, CSTRIDE, CLEN = (SEQ - 32) // 16 + 1, 16, 32


def constant_table():
    p = np.arange(P)
    half = HD // 2
    inv = np.float32(10000.0) ** (-np.arange(half, dtype=np.float32) / np.float32(half))
    ang = np.arange(SEQ, dtype=np.float32)[None, :] * inv[p % half][:, None]
    rot = np.zeros((P, P), np.float32)
    for m in range(P):
        rot[m + half if m % HD < half else m - half, m] = -1.0 if m % HD < half else 1.0
    ends = np.arange(32) * CSTRIDE + CLEN - 1
    t = np.arange(NT)[None, :, None] * P + p[:, None, None]
    parts = {
        "ident": np.eye(P), "upto": p[:, None] <= p[None, :], "ones": np.ones((P, P)), "negones": -np.ones((P, P)),
        "rowno": np.repeat(p[:, None], P, 1), "slotno": np.repeat(p[None, :] + 1, P, 0),
        "thresholds": np.repeat(np.arange(4)[None, :] * P, P, 0), "blockno": np.repeat(np.arange(NBT)[None, :], P, 0),
        "tokno": np.arange(NT)[None, :] * P + p[:, None], "negtrash": -(SEQ + p[:, None]),
        "time": np.repeat(np.arange(SEQ)[None, :], P, 0), "cos": np.cos(ang), "sin": np.sin(ang), "rot": rot,
        "causal": np.where(p[None, :] > p[:, None], -1e30, 0.0),
        "cmpmask": np.where(ends[None, None, :] > t, -1e30, 0.0).reshape(P, -1),
        "anycmp": (p[:, None] >= CLEN - 1),
    }
    table = np.concatenate([np.asarray(v, np.float32) for v in parts.values()], axis=1)
    at, where = 0, {}
    for k, v in parts.items():
        where[k] = (at, at + v.shape[1])
        at += v.shape[1]
    return np.ascontiguousarray(table), where


def load_constants(nc, g, const_dram, where):
    cs = nc.alloc_sbuf_tensor("const_sb", [P, const_dram.shape[1]], F32)
    g.c = {k: cs[:, a:b] for k, (a, b) in where.items()}
    g.const_sb = cs


class Norm:

    def __init__(self, s, g, gamma, beta):
        self.g = g
        self.gamma, self.beta = s.sb("ln_g", [P, D]), s.sb("ln_b", [P, D])
        self.gamma_dram, self.beta_dram = gamma, beta
        self.stats, self.mv = s.sb("ln_stats", [P, NT, 2, 6]), s.sb("ln_mv", [P, NT, 2])
        self.std, self.rstd, self.eps = s.sb("ln_std", [P, NT]), s.sb("ln_rstd", [P, NT]), s.sb("ln_eps", [P, 1])
        self.loaded, self.eps_ready = s.sem("ln_loaded"), s.sem("ln_eps_ready")
        self.mv_ready, self.std_ready = s.sem("ln_mv_ready"), s.sem("ln_std_ready")
        self.scaled, self.times_g, self.done = s.sem("ln_scaled"), s.sem("ln_times_g"), s.sem("ln_done")
        self.steps = Chain(s.sem("ln_dve_steps"))

    def load(self, sp):
        sp.dma_start(self.gamma[:], self.gamma_dram.partition_broadcast(P)).then_inc(self.loaded, 16)
        sp.dma_start(self.beta[:], self.beta_dram.partition_broadcast(P)).then_inc(self.loaded, 16)

    def dve_begin(self, dve):
        dve.memset(self.eps[:], EPS).then_inc(self.eps_ready, 1)

    def dve_tile(self, dve, i):
        for h in range(2):
            last = self.steps.mark(dve.bn_stats(self.stats[:, i, h, :], self.g.x[:, i, h * 512:(h + 1) * 512]))
        dve.wait_ge(self.steps.sem, last)
        dve.bn_aggr(self.mv[:, i, :], self.stats[:, i, :, :]).then_inc(self.mv_ready, 1)

    def dve_scale(self, dve, i):
        dve.wait_ge(self.std_ready, i + 1)
        self.steps.link(dve, dve.reciprocal(self.rstd[:, i:i + 1], self.std[:, i:i + 1]))
        dve.wait_ge(self.mv_ready, i + 1)
        dve.tensor_scalar(self.g.x[:, i, :], self.g.x[:, i, :], self.mv[:, i, 0:1], self.rstd[:, i:i + 1],
                          ALU.subtract, ALU.mult).then_inc(self.scaled, 1)

    def act_tile(self, act, i):
        act.wait_ge(self.eps_ready, 1)
        act.wait_ge(self.mv_ready, i + 1)
        act.activation(self.std[:, i:i + 1], self.mv[:, i, 1:2], ACT.Sqrt, bias=self.eps[:, 0:1]).then_inc(self.std_ready, 1)

    def pool_tile(self, pool, i):
        pool.wait_ge(self.loaded, 32)
        pool.wait_ge(self.scaled, i + 1)
        pool.tensor_tensor(self.g.x[:, i, :], self.g.x[:, i, :], self.gamma[:], ALU.mult).then_inc(self.times_g, 1)
        pool.wait_ge(self.times_g, i + 1)
        pool.tensor_tensor(self.g.x[:, i, :], self.g.x[:, i, :], self.beta[:], ALU.add).then_inc(self.done, 1)


def norm_from_dram(nc, name, g, acc_dram, gamma, beta, out=None):
    with Part(nc, name) as s:
        norm = Norm(s, g, gamma, beta)
        landed, stored = [s.sem(f"landed{i}") for i in range(NT)], s.sem("stored")
        block = s.stack.enter_context(nc.Block())

        @block.sync
        def _(sp):
            for i in range(NT):
                sp.dma_start(g.x[:, i, :], acc_dram[i * P:(i + 1) * P, :]).then_inc(landed[i], 16)
            norm.load(sp)
            if out is not None:
                for i in range(NT):
                    sp.wait_ge(norm.done, i + 1)
                    sp.dma_start(out[i * P:(i + 1) * P, :], g.x[:, i, :]).then_inc(stored, 16)
                sp.wait_ge(stored, 16 * NT)

        @block.vector
        def _(dve):
            norm.dve_begin(dve)
            for i in range(NT):
                dve.wait_ge(landed[i], 16)
                norm.dve_tile(dve, i)
            for i in range(NT):
                norm.dve_scale(dve, i)

        @block.scalar
        def _(act):
            for i in range(NT):
                norm.act_tile(act, i)

        @block.gpsimd
        def _(pool):
            for i in range(NT):
                norm.pool_tile(pool, i)


def out_project_norm(nc, name, g, yT, wout, gamma, beta):
    with Part(nc, name) as s:
        norm = Norm(s, g, gamma, beta)
        bank = [s.ps(f"bank{k}", [P, 512]) for k in range(4)]
        done, summed = s.sem("product_done"), s.sem("summed")
        block = s.stack.enter_context(nc.Block())

        @block.sync
        def _(sp):
            norm.load(sp)

        @block.tensor
        def _(pe):
            for n in range(2 * NT):
                i, h = n // 2, n % 2
                if n >= 4:
                    pe.wait_ge(summed, n - 3)
                for k in range(KC):
                    mm = pe.matmul(bank[n % 4][:, :], yT[:, k, i * P:(i + 1) * P], wout[:, k, h * 512:(h + 1) * 512],
                                   start=(k == 0), stop=(k == KC - 1))
                mm.then_inc(done, 1)

        @block.vector
        def _(dve):
            norm.dve_begin(dve)
            for i in range(NT):
                for h in range(2):
                    n, cols = 2 * i + h, slice(h * 512, (h + 1) * 512)
                    dve.wait_ge(done, n + 1)
                    dve.scalar_tensor_tensor(g.x[:, i, cols], g.x[:, i, cols], ALPHA, bank[n % 4][:, :],
                                             ALU.mult, ALU.add).then_inc(summed, 1)
                dve.wait_ge(summed, 2 * i + 2)
                norm.dve_tile(dve, i)
                norm.dve_scale(dve, i)

        @block.scalar
        def _(act):
            for i in range(NT):
                norm.act_tile(act, i)

        @block.gpsimd
        def _(pool):
            for i in range(NT):
                norm.pool_tile(pool, i)


DS5, G, GS, NS = 512, 32, 16, 64
TAPS, CT = 31, 4
NJ = G * NS // P
ROUND = 1.5 * 2.0 ** 23
TURN_HI, TURN_LO = 6.28125, 6.283185307179586 - 6.28125
TWO_PI = 6.283185

COLS = {}
for _name, _n in (("b_in", 12), ("b_glu", 4), ("cv_b", 4), ("ln_g", 4), ("ln_b", 4), ("taps", (CT + 1) * TAPS),
                  ("lam_re", NJ), ("lam_im", NJ), ("log_dt", NJ), ("skip", CT)):
    COLS[_name] = (sum(b - a for a, b in COLS.values()), sum(b - a for a, b in COLS.values()) + _n)
NCOLS = COLS["skip"][1]


def even_layout(w):
    col = lambda v: np.ascontiguousarray(v.reshape(-1, P).T)
    state = lambda v: v.reshape(NJ, P).T
    parts = [col(w["ev_b_in"][0]), col(w["s5_b_glu"][0]), col(w["cv_b"][0]), col(w["cv_ln_g"][0]), col(w["cv_ln_b"][0]),
             w["cv_w"][0].reshape(TAPS, CT, P).transpose(2, 1, 0).reshape(P, CT * TAPS), np.zeros((P, TAPS), np.float32),
             state(w["s5_lam_re"][0]), state(w["s5_lam_im"][0]),
             state(np.repeat(w["s5_log_dt"][0][:, None], NS, 1)), col(w["s5_d"][0])]
    b = np.stack([w["s5_b_re"][0], w["s5_b_im"][0]])
    c = np.stack([w["s5_c_re"][0], w["s5_c_im"][0]])
    b = b.reshape(2, NJ, 2, NS, GS).transpose(2, 4, 1, 0, 3)
    c = c.reshape(2, NJ, 2, GS, NS).transpose(2, 4, 1, 0, 3)
    return np.ascontiguousarray(np.concatenate(parts, axis=1)), np.ascontiguousarray(b), np.ascontiguousarray(c)


def even_mixer(nc, g, w, yT, keep):
    with Part(nc, "even") as outer:
        cols = outer.sb("cols", [P, NCOLS])
        col = {k: cols[:, a:b] for k, (a, b) in COLS.items()}
        u32 = outer.sb("u32", [32, NJ + 1, SEQ])
        hpad = outer.sb("hpad", [P, CT, TAPS - 1 + SEQ])
        uT = outer.sb("uT", [P, CT, SEQ])
        bB = outer.sb("bB", [32, NJ + 1, 2, P])
        cC = outer.sb("cC", [P, NJ, 2, 32])
        even_in_project(nc, g, w, cols, col, u32, uT, hpad, bB, cC)
        s5_and_conv(nc, g, col, u32, hpad, bB, cC, yT)
        even_finish(nc, g, w, col, u32, uT, yT)
    wout = keep.sb("wout", [P, KC, D])
    with Part(nc, "evw") as s:
        landed = s.sem("wout_landed")
        block = s.stack.enter_context(nc.Block())

        @block.sync
        def _(sp):
            sp.dma_start(wout[:], w["ev_w_out"][0].rearrange("(c p) n -> p c n", p=P)).then_inc(landed, 16)
            sp.wait_ge(landed, 16)
    return wout


def even_in_project(nc, g, w, cols, col, u32, uT, hpad, bB, cC):
    with Part(nc, "evin") as s:
        win = s.sb("win", [P, KC, 3 * DS5])
        small_loaded = s.sem("small_loaded")
        sig = s.sb("sig", [P, 2, SEQ])
        bank = [s.ps(f"bank{k}", [P, 512]) for k in range(8)]
        win_landed = [s.sem(f"win_landed{k}") for k in range(3)]
        xt_done, xt_a, xt_v = s.sem("xt_done"), s.sem("xt_copied_act"), s.sem("xt_copied_dve")
        done, u_ready, u_moved = s.sem("product_done"), s.sem("u_ready"), s.sem("u_moved")
        sig_ready, h_ready, cleared = s.sem("sig_ready"), s.sem("h_ready"), s.sem("cleared")
        block = s.stack.enter_context(nc.Block())
        order = [0, 1, 2, 3] + [f for t in range(CT) for f in (8 + t, 4 + t)]

        @block.sync
        def _(sp):
            sp.dma_start(g.const_sb[:], w["const_table"]).then_inc(g.consts_loaded, 16)
            for i in range(NT):
                sp.dma_start(g.x[:, i, :], w["x"][0, i * P:(i + 1) * P, :]).then_inc(g.x_loaded, 16)
            sp.dma_start(cols[:], w["columns"]).then_inc(small_loaded, 16)
            src = w["ev_w_in"][0].rearrange("(p c) f -> p c f", c=KC)
            for k in (0, 2, 1):
                sp.dma_start(win[:, :, k * 512:(k + 1) * 512], src[:, :, k * 512:(k + 1) * 512]).then_inc(win_landed[k], 16)
            sp.wait_ge(cleared, 2)
            for q in range(2):
                sp.dma_start(bB[16 * q:16 * q + 16, 0:NJ, :, NS * q:NS * q + NS], w["b_swapped"][q]).then_inc(small_loaded, 16)
                sp.dma_start(cC[64 * q:64 * q + 64, :, :, GS * q:GS * q + GS], w["c_swapped"][q]).then_inc(small_loaded, 16)
            sp.wait_ge(u_ready, CT)
            for q in range(4):
                sp.dma_start(u32[:, 0:NJ, :].rearrange("h (t q) l -> h t q l", q=4)[:, :, q, :], uT[32 * q:32 * q + 32, :, :]).then_inc(u_moved, 16)
            sp.wait_ge(u_moved, 64)
            sp.wait_ge(small_loaded, 80)

        @block.gpsimd
        def _(pool):
            pool.memset(bB[:], 0.0).then_inc(cleared, 1)
            pool.memset(cC[:], 0.0).then_inc(cleared, 1)
            pool.memset(hpad[:, :, 0:TAPS - 1], 0.0)
            pool.memset(u32[:, NJ, :], 0.0)

        @block.tensor
        def _(pe):
            pe.wait_ge(g.consts_loaded, 16)
            pe.wait_ge(g.x_loaded, 64)
            emit_transposes(pe, g.x, g.c["ident"], bank[0:2], xt_done, (xt_a, xt_v))
            pe.wait_ge(xt_a, 4)
            pe.wait_ge(xt_v, 4)
            for n, f in enumerate(order):
                if n in (0, 4, 5):
                    pe.wait_ge(win_landed[f // 4], 16)
                if 6 <= n < 10:
                    pe.wait_ge(u_ready, n - 5)
                elif n >= 10:
                    pe.wait_ge(h_ready, (n - 8) // 2)
                for k in range(KC):
                    mm = pe.matmul(bank[2 + n % 6][:, :], win[:, k, f * P:(f + 1) * P], g.xT[:, k, :],
                                   start=(k == 0), stop=(k == KC - 1))
                mm.then_inc(done, 1)

        @block.scalar
        def _(act):
            for k in range(0, KC, 2):
                act.wait_ge(xt_done, k + 1)
                act.activation(g.xT[:, k, :], bank[0][:, :], ACT.Copy).then_inc(xt_a, 1)
            act.wait_ge(small_loaded, 16)
            for n, f in enumerate(order):
                if n < 4:
                    act.wait_ge(done, n + 1)
                    act.activation(uT[:, n, :], bank[2 + n][:, :], ACT.Identity, bias=col["b_in"][:, f:f + 1]).then_inc(u_ready, 1)
                elif n % 2 == 0:
                    t = (n - 4) // 2
                    act.wait_ge(done, n + 1)
                    if t >= 2:
                        act.wait_ge(h_ready, t - 1)
                    act.activation(sig[:, t % 2, :], bank[2 + n % 6][:, :], ACT.Sigmoid, bias=col["b_in"][:, f:f + 1]).then_inc(sig_ready, 1)

        @block.vector
        def _(dve):
            for k in range(1, KC, 2):
                dve.wait_ge(xt_done, k + 1)
                dve.tensor_copy(g.xT[:, k, :], bank[1][:, :]).then_inc(xt_v, 1)
            dve.wait_ge(small_loaded, 16)
            for t in range(CT):
                n = 5 + 2 * t
                dve.wait_ge(done, n + 1)
                dve.wait_ge(sig_ready, t + 1)
                dve.scalar_tensor_tensor(hpad[:, t, TAPS - 1:], bank[2 + n % 6][:, :], col["b_in"][:, 4 + t:5 + t],
                                         sig[:, t % 2, :], ALU.add, ALU.mult).then_inc(h_ready, 1)


def s5_and_conv(nc, g, col, u32, hpad, bB, cC, yT):
    with Part(nc, "s5") as s:
        names = ("dt", "ld", "th", "km", "k", "r", "sn", "sh", "cs", "are", "aim", "den", "rden", "fre",
                 "fim", "t1", "t2", "t3", "t4")
        v = {n: s.sb(n, [P, NJ]) for n in names}
        decay, rho = s.sb("decay", [P, NJ]), s.sb("rho", [P, NJ + 1])
        cp = s.sb("cp", [P, NJ + 1, 3, 32])
        ct = s.sb("ct", [P, 2, NJ, 32])
        bst = [s.sb(f"bst{p}", [32, 2 * P]) for p in range(2)]
        cst = [s.sb(f"cst{p}", [P, 3 * 32]) for p in range(2)]
        turns, kround, frac = s.sb("turns", [P, SEQ]), s.sb("kround", [P, SEQ]), s.sb("frac", [P, SEQ])
        sinT = [s.sb(f"sinT{p}", [P, SEQ]) for p in range(2)]
        cosT = [s.sb(f"cosT{p}", [P, SEQ]) for p in range(2)]
        half = s.sb("half", [P, SEQ])
        prod = s.sb("prod", [P, 4, SEQ])
        vin = s.sb("vin", [P, 2, SEQ])
        z = s.sb("z", [P, 2, SEQ])
        back = s.sb("back", [P, 4, SEQ])
        diag = s.sb("diag", [P, 2, 8, P])
        bu = [[s.ps(f"bu{p}{q}", [P, 512]) for q in range(2)] for p in range(2)]
        by, bc = s.ps("by", [P, 512]), s.ps("bc", [P, 512])
        dve_steps = Chain(s.sem("dve_steps"))
        exps_ready, sines_ready, rho_ready, cp_ready = s.sem("exps_ready"), s.sem("sines_ready"), s.sem("rho_ready"), s.sem("cp_ready")
        ld_ready, statics = s.sem("ld_ready"), s.sem("statics_copied")
        table_steps, frac_ready, sin_ready, half_ready, square_ready, cos_ready = (
            s.sem("table_steps"), s.sem("frac_ready"), s.sem("sin_ready"), s.sem("half_ready"), s.sem("square_ready"), s.sem("cos_ready"))
        bu_done, prod_re, prod_im = s.sem("bu_done"), s.sem("prod_re_ready"), s.sem("prod_im_ready")
        vin_re, vin_im, z_re, z_im = s.sem("vin_re_ready"), s.sem("vin_im_ready"), s.sem("z_re_ready"), s.sem("z_im_ready")
        back_v, back_p, y_done, y_copied = s.sem("back_dve"), s.sem("back_pool"), s.sem("y_done"), s.sem("y_copied")
        diag_ready, conv_done, conv_copied = s.sem("diag_ready"), s.sem("conv_quarters_done"), s.sem("conv_copied")
        pads, copied = s.sem("pads_cleared"), s.sem("copies")
        block = s.stack.enter_context(nc.Block())
        taps = col["taps"].rearrange("p (t n) -> p t n", n=TAPS)

        def steps(eng):
            with eng.Fori(0, CT) as t:
                for q in range(4):
                    yield 4 * t + q, t, q, q % 2

        def taps_of(q):
            return range(8 * q, min(8 * q + 8, TAPS))

        @block.scalar
        def _(act):
            for counter in (conv_copied, y_copied,):
                act.sem_inc(counter, 1)
            act.activation(v["dt"][:], col["log_dt"], ACT.Exp).then_inc(exps_ready, 1)
            act.wait_ge(ld_ready, 1)
            act.activation(decay[:], v["ld"][:], ACT.Exp).then_inc(exps_ready, 1)
            act.wait_ge(rho_ready, 1)
            act.activation(v["sn"][:], rho[:, 0:NJ], ACT.Sin, scale=TWO_PI).then_inc(sines_ready, 1)
            act.activation(v["sh"][:], rho[:, 0:NJ], ACT.Sin, scale=TWO_PI / 2).then_inc(sines_ready, 1)

            def table(j, p):
                act.wait_ge(frac_ready, j + 1)
                if p is not None:
                    act.wait_ge(back_v, j - 1 + 1)
                    act.wait_ge(back_p, j - 1 + 1)
                act.activation(sinT[p or 0][:], frac[:], ACT.Sin, scale=-TWO_PI).then_inc(sin_ready, 1)
                if p is not None:
                    act.wait_ge(cos_ready, j)
                act.activation(half[:], frac[:], ACT.Sin, scale=-TWO_PI / 2).then_inc(half_ready, 1)
                act.wait_ge(half_ready, j + 1)
                act.activation(half[:], half[:], ACT.Square).then_inc(square_ready, 1)

            def diagonals(t, q, p, j=None):
                if j is not None:
                    act.wait_ge(conv_done, j - 1 + 1)
                for n in taps_of(q):
                    last = act.activation(diag[:, p, n % 8, :], g.c["ident"], ACT.Copy, scale=taps[:, ds(t, 1), n])
                last.then_inc(diag_ready, 1)

            table(0, None)
            diagonals(0, 0, 0)
            for j, t, q, p in steps(act):
                table(j + 1, 1 - p)
                diagonals(t if q < 3 else t + 1, (q + 1) % 4, 1 - p, j + 1)
                act.wait_ge(y_done, j + 1 + 1)
                act.activation(u32[:, ds(j, 1), :].rearrange("h o l -> h (o l)"), by[0:32, :], ACT.Copy).then_inc(y_copied, 1)
                if q == 3:
                    act.wait_ge(conv_done, j + 1 + 1)
                    act.activation(yT[:, ds(CT + t, 1), :].rearrange("p o l -> p (o l)"), bc[:, :], ACT.Identity,
                                   bias=col["cv_b"][:, ds(t, 1)]).then_inc(conv_copied, 1)

        @block.gpsimd
        def _(pool):
            for counter in (back_p, vin_im,):
                pool.sem_inc(counter, 1)
            def statics_of(j, p, wait):
                if wait:
                    pool.wait_ge(y_done, j - 1 + 1)
                pool.tensor_copy(bst[p][:], bB[:, ds(j, 1)].rearrange("h o k n -> h (o k n)"))
                pool.tensor_copy(cst[p][:], cp[:, ds(j, 1)].rearrange("p o k n -> p (o k n)")).then_inc(statics, 1)

            pool.memset(rho[:, NJ:NJ + 1], 0.0).then_inc(pads, 1)
            pool.memset(cp[:, NJ], 0.0).then_inc(pads, 1)
            pool.wait_ge(pads, 2)
            pool.wait_ge(cp_ready, 1)
            statics_of(0, 0, False)
            for j, t, q, p in steps(pool):
                pool.wait_ge(prod_re, j + 1)
                pool.wait_ge(z_im, j + 1)
                pool.tensor_tensor(vin[:, 0, :], prod[:, 0, :], prod[:, 1, :], ALU.add).then_inc(vin_re, 1)
                pool.wait_ge(prod_im, j + 1 + 1)
                pool.tensor_tensor(vin[:, 1, :], prod[:, 2, :], prod[:, 3, :], ALU.subtract).then_inc(vin_im, 1)
                statics_of(j + 1, 1 - p, True)
                pool.wait_ge(z_re, j + 1)
                pool.wait_ge(cos_ready, j + 1)
                pool.wait_ge(sin_ready, j + 1)
                pool.wait_ge(y_done, j + 1)
                pool.tensor_tensor(back[:, 0, :], z[:, 0, :], cosT[p][:], ALU.mult)
                pool.tensor_tensor(back[:, 2, :], z[:, 0, :], sinT[p][:], ALU.mult).then_inc(back_p, 1)

        @block.tensor
        def _(pe):
            for counter in (conv_done, y_done,):
                pe.sem_inc(counter, 1)
            def inputs(j, p):
                pe.wait_ge(statics, j + 1)
                for k in range(2):
                    mm = pe.matmul(bu[p][k][:, :], bst[p][:, k * P:(k + 1) * P],
                                   u32[:, ds(j, 1), :].rearrange("h o l -> h (o l)"), start=True, stop=True)
                mm.then_inc(bu_done, 1)

            inputs(0, 0)
            for j, t, q, p in steps(pe):
                pe.wait_ge(prod_im, j + 1)
                inputs(j + 1, 1 - p)
                pe.wait_ge(diag_ready, j + 1)
                if q == 0:
                    pe.wait_ge(conv_copied, t + 1)
                for n in taps_of(q):
                    mm = pe.matmul(bc[:, :], diag[:, p, n % 8, :], hpad[:, ds(t, 1), n:n + SEQ].rearrange("p o l -> p (o l)"),
                                   start=(n == 0), stop=(n == TAPS - 1))
                mm.then_inc(conv_done, 1)
                pe.wait_ge(back_v, j + 1 + 1)
                pe.wait_ge(back_p, j + 1 + 1)
                pe.wait_ge(y_copied, j + 1)
                for k, sign in enumerate((0, 1, 2, 2)):
                    mm = pe.matmul(by[0:32, :], cst[p][:, sign * 32:sign * 32 + 32], back[:, k, :], start=(k == 0), stop=(k == 3))
                mm.then_inc(y_done, 1)

        @block.vector
        def _(dve):
            for counter in (back_v, z_im, prod_im,):
                dve.sem_inc(counter, 1)
            link = lambda ins: dve_steps.link(dve, ins)
            dve.wait_ge(exps_ready, 1)
            dve.tensor_tensor(v["ld"][:], col["lam_re"], v["dt"][:], ALU.mult).then_inc(ld_ready, 1)
            link(dve.tensor_tensor(v["th"][:], col["lam_im"], v["dt"][:], ALU.mult))
            link(dve.tensor_scalar(v["km"][:], v["th"][:], 1.0 / 6.283185307179586, ROUND, ALU.mult, ALU.add))
            link(dve.tensor_scalar(v["k"][:], v["km"][:], -ROUND, None, ALU.add))
            link(dve.scalar_tensor_tensor(v["r"][:], v["k"][:], -TURN_HI, v["th"][:], ALU.mult, ALU.add))
            link(dve.scalar_tensor_tensor(v["r"][:], v["k"][:], -TURN_LO, v["r"][:], ALU.mult, ALU.add))
            link(dve.tensor_scalar(v["r"][:], v["r"][:], 1.0 / 6.283185307179586, 0.5, ALU.mult, ALU.min))
            dve.tensor_scalar(rho[:, 0:NJ], v["r"][:], -0.5, None, ALU.max).then_inc(rho_ready, 1)
            dve.wait_ge(exps_ready, 2)
            dve.wait_ge(sines_ready, 2)
            link(dve.tensor_tensor(v["cs"][:], v["sh"][:], v["sh"][:], ALU.mult))
            link(dve.tensor_scalar(v["cs"][:], v["cs"][:], -2.0, 1.0, ALU.mult, ALU.add))
            link(dve.tensor_tensor(v["are"][:], decay[:], v["cs"][:], ALU.mult))
            link(dve.tensor_tensor(v["aim"][:], decay[:], v["sn"][:], ALU.mult))
            link(dve.tensor_scalar(v["are"][:], v["are"][:], -1.0, None, ALU.add))
            link(dve.tensor_tensor(v["t1"][:], col["lam_re"], col["lam_re"], ALU.mult))
            link(dve.tensor_tensor(v["t2"][:], col["lam_im"], col["lam_im"], ALU.mult))
            link(dve.tensor_tensor(v["den"][:], v["t1"][:], v["t2"][:], ALU.add))
            link(dve.reciprocal(v["rden"][:], v["den"][:]))
            link(dve.tensor_tensor(v["t1"][:], v["are"][:], col["lam_re"], ALU.mult))
            link(dve.tensor_tensor(v["t2"][:], v["aim"][:], col["lam_im"], ALU.mult))
            link(dve.tensor_tensor(v["t1"][:], v["t1"][:], v["t2"][:], ALU.add))
            link(dve.tensor_tensor(v["fre"][:], v["t1"][:], v["rden"][:], ALU.mult))
            link(dve.tensor_tensor(v["t3"][:], v["aim"][:], col["lam_re"], ALU.mult))
            link(dve.tensor_tensor(v["t4"][:], v["are"][:], col["lam_im"], ALU.mult))
            link(dve.tensor_tensor(v["t3"][:], v["t3"][:], v["t4"][:], ALU.subtract))
            link(dve.tensor_tensor(v["fim"][:], v["t3"][:], v["rden"][:], ALU.mult))
            fre, fim = (f[:].unsqueeze(2).to_broadcast([P, NJ, 32]) for f in (v["fre"], v["fim"]))
            link(dve.tensor_tensor(ct[:, 0], cC[:, :, 0, :], fre, ALU.mult))
            link(dve.tensor_tensor(ct[:, 1], cC[:, :, 1, :], fim, ALU.mult))
            link(dve.tensor_tensor(cp[:, 0:NJ, 0, :], ct[:, 0], ct[:, 1], ALU.subtract))
            link(dve.tensor_scalar(cp[:, 0:NJ, 1, :], cp[:, 0:NJ, 0, :], -1.0, None, ALU.mult))
            link(dve.tensor_tensor(ct[:, 0], cC[:, :, 0, :], fim, ALU.mult))
            link(dve.tensor_tensor(ct[:, 1], cC[:, :, 1, :], fre, ALU.mult))
            link(dve.tensor_tensor(ct[:, 0], ct[:, 0], ct[:, 1], ALU.add))
            dve.tensor_scalar(cp[:, 0:NJ, 2, :], ct[:, 0], -1.0, None, ALU.mult).then_inc(cp_ready, 1)
            dve.wait_ge(pads, 2)
            dve.wait_ge(rho_ready, 1)

            def table(j, wait):
                if wait:
                    dve.wait_ge(frac_ready, j)
                r = rho[:, ds(j, 1)]
                dve.tensor_scalar(turns[:], g.c["time"], r, None, ALU.mult).then_inc(table_steps, 1)
                dve.tensor_scalar(kround[:], g.c["time"], r, ROUND, ALU.mult, ALU.add).then_inc(table_steps, 1)
                dve.wait_ge(table_steps, 2 * j + 2)
                if wait:
                    dve.wait_ge(square_ready, j)
                dve.scalar_tensor_tensor(frac[:], kround[:], -ROUND, turns[:], ALU.add, ALU.subtract).then_inc(frac_ready, 1)

            def cosine(j, p, wait):
                dve.wait_ge(square_ready, j + 1)
                if wait:
                    dve.wait_ge(back_p, j - 1 + 1)
                dve.tensor_scalar(cosT[p][:], half[:], -2.0, 1.0, ALU.mult, ALU.add).then_inc(cos_ready, 1)

            table(0, False)
            cosine(0, 0, False)
            for j, t, q, p in steps(dve):
                dve.wait_ge(bu_done, j + 1)
                dve.wait_ge(cos_ready, j + 1)
                dve.wait_ge(sin_ready, j + 1)
                dve.wait_ge(vin_im, j + 1)
                dve.tensor_tensor(prod[:, 0, :], bu[p][0][:, :], cosT[p][:], ALU.mult)
                dve.tensor_tensor(prod[:, 1, :], bu[p][1][:, :], sinT[p][:], ALU.mult).then_inc(prod_re, 1)
                dve.tensor_tensor(prod[:, 2, :], bu[p][1][:, :], cosT[p][:], ALU.mult)
                dve.tensor_tensor(prod[:, 3, :], bu[p][0][:, :], sinT[p][:], ALU.mult).then_inc(prod_im, 1)
                table(j + 1, True)
                d = decay[:, ds(j, 1)].to_broadcast([P, SEQ])
                dve.wait_ge(vin_re, j + 1)
                dve.wait_ge(back_p, j + 1)
                dve.tensor_tensor_scan(z[:, 0, :], d, vin[:, 0, :], 0.0, ALU.mult, ALU.add).then_inc(z_re, 1)
                dve.wait_ge(vin_im, j + 1 + 1)
                dve.wait_ge(back_v, j + 1)
                dve.tensor_tensor_scan(z[:, 1, :], d, vin[:, 1, :], 0.0, ALU.mult, ALU.add).then_inc(z_im, 1)
                dve.wait_ge(z_im, j + 1 + 1)
                dve.wait_ge(y_done, j + 1)
                dve.tensor_tensor(back[:, 1, :], z[:, 1, :], sinT[p][:], ALU.mult)
                dve.tensor_tensor(back[:, 3, :], z[:, 1, :], cosT[p][:], ALU.mult).then_inc(back_v, 1)
                cosine(j + 1, 1 - p, True)


def even_finish(nc, g, w, col, u32, uT, yT):
    with Part(nc, "evfin") as s:
        wglu = s.sb("wglu", [P, CT, DS5])
        gl, sg, cen = s.sb("gl", [P, CT, SEQ]), s.sb("sg", [P, 2, SEQ]), s.sb("cen", [P, CT, SEQ])
        sq, std, rstd, eps = s.sb("sq", [P, CT, SEQ]), s.sb("std", [P, SEQ]), s.sb("rstd", [P, SEQ]), s.sb("eps", [P, 1])
        bank = [s.ps(f"bank{k}", [P, 512]) for k in range(4)]
        bM, bV = s.ps("bM", [P, 512]), s.ps("bV", [P, 512])
        wglu_landed, y_moved = s.sem("wglu_landed"), s.sem("y_moved")
        y_ready, gl_ready, glu_done, sg_ready, ya_ready = s.sem("y_ready"), s.sem("gl_ready"), s.sem("glu_done"), s.sem("sg_ready"), s.sem("ya_ready")
        mean_done, cen_ready, sq_ready, var_done, std_ready, rstd_ready, norm_ready = (
            s.sem("mean_done"), s.sem("cen_ready"), s.sem("sq_ready"), s.sem("var_done"), s.sem("std_ready"), s.sem("rstd_ready"), s.sem("norm_ready"))
        eps_ready = s.sem("eps_ready")
        block = s.stack.enter_context(nc.Block())

        @block.sync
        def _(sp):
            for q in range(4):
                sp.dma_start(yT[32 * q:32 * q + 32, 0:CT, :], u32[:, 0:NJ, :].rearrange("h (t q) l -> h t q l", q=4)[:, :, q, :]).then_inc(y_moved, 16)
            sp.dma_start(wglu[:], w["s5_w_glu"][0].rearrange("(c p) f -> p c f", p=P)).then_inc(wglu_landed, 16)

        @block.tensor
        def _(pe):
            for k in range(CT):
                mm = pe.matmul(bM[:, :], g.c["ones"], yT[:, CT + k, :], start=(k == 0), stop=(k == CT - 1))
            mm.then_inc(mean_done, 1)
            pe.wait_ge(wglu_landed, 16)
            pe.wait_ge(gl_ready, CT)
            for f in range(CT):
                if f == 1:
                    pe.wait_ge(sq_ready, CT)
                    for k in range(CT):
                        mm = pe.matmul(bV[:, :], g.c["ones"], sq[:, k, :], start=(k == 0), stop=(k == CT - 1))
                    mm.then_inc(var_done, 1)
                for k in range(CT):
                    mm = pe.matmul(bank[f][:, :], wglu[:, k, f * P:(f + 1) * P], gl[:, k, :], start=(k == 0), stop=(k == CT - 1))
                mm.then_inc(glu_done, 1)

        @block.vector
        def _(dve):
            dve.memset(eps[:], EPS).then_inc(eps_ready, 1)
            dve.wait_ge(y_moved, 64)
            for k in range(CT):
                dve.scalar_tensor_tensor(yT[:, k, :], uT[:, k, :], col["skip"][:, k:k + 1], yT[:, k, :], ALU.mult, ALU.add).then_inc(y_ready, 1)
            dve.wait_ge(mean_done, 1)
            for k in range(CT):
                dve.scalar_tensor_tensor(cen[:, k, :], bM[:, :], -1.0 / DS5, yT[:, CT + k, :], ALU.mult, ALU.add).then_inc(cen_ready, 1)
            dve.wait_ge(std_ready, 1)
            dve.reciprocal(rstd[:], std[:]).then_inc(rstd_ready, 1)
            dve.wait_ge(rstd_ready, 1)
            dve.wait_ge(cen_ready, CT)
            dve.wait_ge(sq_ready, CT)
            for k in range(CT):
                dve.tensor_tensor(cen[:, k, :], cen[:, k, :], rstd[:], ALU.mult).then_inc(norm_ready, 1)
            for f in range(CT):
                dve.wait_ge(sg_ready, f + 1)
                dve.tensor_tensor(yT[:, f, :], gl[:, f, :], sg[:, f % 2, :], ALU.mult).then_inc(ya_ready, 1)

        @block.scalar
        def _(act):
            for k in range(CT):
                act.wait_ge(y_ready, k + 1)
                act.activation(gl[:, k, :], yT[:, k, :], ACT.Gelu_apprx_tanh).then_inc(gl_ready, 1)
            for k in range(CT):
                act.wait_ge(cen_ready, k + 1)
                act.activation(sq[:, k, :], cen[:, k, :], ACT.Square).then_inc(sq_ready, 1)
            act.wait_ge(var_done, 1)
            act.wait_ge(eps_ready, 1)
            act.activation(std[:], bV[:, :], ACT.Sqrt, bias=eps[:, 0:1], scale=1.0 / DS5).then_inc(std_ready, 1)
            for f in range(CT):
                act.wait_ge(glu_done, f + 1)
                if f >= 2:
                    act.wait_ge(ya_ready, f - 1)
                act.activation(sg[:, f % 2, :], bank[f][:, :], ACT.Sigmoid, bias=col["b_glu"][:, f:f + 1]).then_inc(sg_ready, 1)
            for k in range(CT):
                act.wait_ge(norm_ready, k + 1)
                act.activation(yT[:, CT + k, :], cen[:, k, :], ACT.Silu, scale=col["ln_g"][:, k:k + 1], bias=col["ln_b"][:, k:k + 1])


NU, NP2 = 4, 2
QCOL, KC_COL, VC_COL, KS_COL, VS_COL, KW_COL, VW_COL, GL_COL, ODD_IN = 0, 1024, 1280, 1536, 1792, 2048, 2304, 2560, 2608
SCALE = HD ** -0.5


def odd_layout(w):
    heads = lambda m: np.moveaxis(m.reshape(m.shape[0], NP2, 2, NU, HD), 2, 3).reshape(m.shape[0], NH * HD)
    win = np.concatenate([heads(w["od_w_in"][0][:, :KC_COL]), w["od_w_in"][0][:, KC_COL:]], axis=1)
    wout = np.ascontiguousarray(heads(np.ascontiguousarray(w["od_w_out"][0].T)).T)
    tables = np.concatenate([np.tile(w[k][0].T, (2, 1)) for k in ("cmp_pe_k", "cmp_pe_v")], axis=1)
    return np.ascontiguousarray(win), wout, np.ascontiguousarray(tables)


def odd_mixer(nc, g, w, yT):
    with Part(nc, "odd") as outer:
        a = Names()
        a.qT = outer.sb("qT", [P, 2 * NU, SEQ])
        a.kT = {k: outer.sb(k + "T", [P, NP2, SEQ]) for k in ("kc", "ks", "kw", "vc")}
        a.v = outer.sb("v", [P, NT, 2, 2 * P])
        a.gates = outer.sb("gates", [P, NT, 3 * NH])
        a.kcmp = outer.sb("kcmp", [P, NP2, 32])
        a.vcmp = outer.sb("vcmp", [NCMP, NP2, P])
        odd_in_project(nc, g, w, a)
        compress(nc, g, w, a)
        attention(nc, g, a, yT)


def odd_in_project(nc, g, w, a):
    with Part(nc, "oddin") as s:
        win = s.sb("win", [P, KC, ODD_IN])
        raw, turned = s.sb("raw", [P, 2, SEQ]), s.sb("turned", [P, 2, 2, SEQ])
        bank = [s.ps(f"bank{k}", [P, 512]) for k in range(8)]
        landed = [s.sem(f"landed{k}") for k in range(3)]
        xt_done, xt_a, xt_v = s.sem("xt_done"), s.sem("xt_copied_act"), s.sem("xt_copied_dve")
        done, raw_ready, rot_done, turned_ready, roped = s.sem("product_done"), s.sem("raw_ready"), s.sem("rot_done"), s.sem("turned_ready"), s.sem("roped")
        v_done, v_ready, vc_ready = s.sem("v_done"), s.sem("v_ready"), s.sem("vc_ready")
        block = s.stack.enter_context(nc.Block())
        roped_tiles = [(win[:, :, P * u:P * u + P], a.qT[:, u, :]) for u in range(2 * NU)]
        for k, at in (("kc", KC_COL), ("ks", KS_COL), ("kw", KW_COL)):
            roped_tiles += [(win[:, :, at + P * u:at + P * u + P], a.kT[k][:, u, :]) for u in range(NP2)]
        NR = len(roped_tiles)
        part_of = lambda n: 0 if n < 8 else 1 if n < 10 else 2

        @block.sync
        def _(sp):
            src = w["od_w_in_heads"].rearrange("(p c) f -> p c f", c=KC)
            for k, (lo, hi) in enumerate(((QCOL, KC_COL), (KC_COL, KS_COL), (KS_COL, ODD_IN))):
                sp.dma_start(win[:, :, lo:hi], src[:, :, lo:hi]).then_inc(landed[k], 16)

        @block.tensor
        def _(pe):
            emit_transposes(pe, g.x, g.c["ident"], bank[0:2], xt_done, (xt_a, xt_v))
            pe.wait_ge(xt_a, 4)
            pe.wait_ge(xt_v, 4)

            def rotate(n):
                pe.wait_ge(raw_ready, n + 1)
                if n >= 2:
                    pe.wait_ge(turned_ready, n - 1)
                pe.matmul(bank[4 + n % 2][:, :], g.c["rot"], raw[:, n % 2, :], start=True, stop=True).then_inc(rot_done, 1)

            for n in range(NR):
                cols, _ = roped_tiles[n]
                pe.wait_ge(landed[part_of(n)], 16)
                if n >= 2:
                    pe.wait_ge(raw_ready, n - 1)
                for k in range(KC):
                    mm = pe.matmul(bank[2 + n % 2][:, :], cols[:, k], g.xT[:, k, :], start=(k == 0), stop=(k == KC - 1))
                mm.then_inc(done, 1)
                if n >= 1:
                    rotate(n - 1)
            rotate(NR - 1)
            for u in range(NP2):
                for k in range(KC):
                    mm = pe.matmul(bank[6 + u][:, :], win[:, k, VC_COL + P * u:VC_COL + P * u + P], g.xT[:, k, :],
                                   start=(k == 0), stop=(k == KC - 1))
                mm.then_inc(v_done, 1)
            for i in range(NT):
                if i >= 2:
                    pe.wait_ge(v_ready, i - 1)
                for b, col in enumerate((VS_COL, VW_COL)):
                    for k in range(KC):
                        mm = pe.matmul(bank[i % 2][:, b * 256:(b + 1) * 256], g.xT[:, k, i * P:(i + 1) * P],
                                       win[:, k, col:col + 256], start=(k == 0), stop=(k == KC - 1))
                mm.then_inc(v_done, 1)
            pe.wait_ge(raw_ready, NR)
            for i in range(NT):
                for k in range(KC):
                    mm = pe.matmul(bank[2][:, i * 48:(i + 1) * 48], g.xT[:, k, i * P:(i + 1) * P], win[:, k, GL_COL:ODD_IN],
                                   start=(k == 0), stop=(k == KC - 1))
            mm.then_inc(v_done, 1)

        @block.scalar
        def _(act):
            for k in range(0, KC, 2):
                act.wait_ge(xt_done, k + 1)
                act.activation(g.xT[:, k, :], bank[0][:, :], ACT.Copy).then_inc(xt_a, 1)
            for n in range(NR):
                act.wait_ge(done, n + 1)
                if n >= 2:
                    act.wait_ge(turned_ready, n - 1)
                act.activation(raw[:, n % 2, :], bank[2 + n % 2][:, :], ACT.Copy).then_inc(raw_ready, 1)
            for u in range(NP2):
                act.wait_ge(v_done, u + 1)
                act.activation(a.kT["vc"][:, u, :], bank[6 + u][:, :], ACT.Copy).then_inc(vc_ready, 1)
            for i in range(NT):
                act.wait_ge(v_done, NP2 + i + 1)
                act.activation(a.v[:, i].rearrange("p b d -> p (b d)"), bank[i % 2][:, :], ACT.Copy).then_inc(v_ready, 1)
            act.wait_ge(v_done, NP2 + NT + 1)
            act.activation(a.gates[:].rearrange("p i h -> p (i h)"), bank[2][:, 0:NT * 48], ACT.Sigmoid).then_inc(vc_ready, 1)

        @block.vector
        def _(dve):
            for k in range(1, KC, 2):
                dve.wait_ge(xt_done, k + 1)
                dve.tensor_copy(g.xT[:, k, :], bank[1][:, :]).then_inc(xt_v, 1)
            for n in range(NR):
                dve.wait_ge(raw_ready, n + 1)
                if n >= 2:
                    dve.wait_ge(roped, n - 1)
                dve.tensor_tensor(turned[:, n % 2, 0, :], raw[:, n % 2, :], g.c["cos"], ALU.mult)
                dve.wait_ge(rot_done, n + 1)
                dve.tensor_tensor(turned[:, n % 2, 1, :], bank[4 + n % 2][:, :], g.c["sin"], ALU.mult).then_inc(turned_ready, 1)

        @block.gpsimd
        def _(pool):
            for n in range(NR):
                pool.wait_ge(turned_ready, n + 1)
                pool.tensor_tensor(roped_tiles[n][1], turned[:, n % 2, 0, :], turned[:, n % 2, 1, :], ALU.add).then_inc(roped, 1)


def compress(nc, g, w, a):
    with Part(nc, "cmp") as s:
        cw = [s.sb(f"cw{k}", [P, CLEN, HD]) for k in range(2)]
        pe_cols = s.sb("pe_cols", [P, 2 * CLEN])
        shift = s.sb("shift", [P, 2])
        vT = s.sb("vT", [P, NP2, 32])
        bank = [s.ps(f"bank{k}", [P, 512]) for k in range(5)]
        landed, pe_landed = [s.sem(f"landed{k}") for k in range(2)], s.sem("pe_landed")
        shifts_done, shift_ready, done, ready, vt_done, v_ready = (
            s.sem("shifts_done"), s.sem("shift_ready"), s.sem("products_done"), s.sem("ready"), s.sem("vt_done"), s.sem("v_ready"))
        block = s.stack.enter_context(nc.Block())

        @block.sync
        def _(sp):
            sp.dma_start(pe_cols[:], w["pe_columns"]).then_inc(pe_landed, 16)
            for k, name in enumerate(("cmp_w_k", "cmp_w_v")):
                for half in range(2):
                    sp.dma_start(cw[k][64 * half:64 * half + 64], w[name][0].rearrange("l d e -> d l e")).then_inc(landed[k], 16)

        @block.tensor
        def _(pe):
            pe.wait_ge(pe_landed, 16)
            for k, name in enumerate(("kc", "vc")):
                pe.wait_ge(landed[k], 32)
                for half in range(2):
                    rows = slice(64 * half, 64 * half + 64)
                    for n in range(CLEN):
                        mm = pe.matmul(bank[4][rows, k:k + 1], cw[k][rows, n, :], pe_cols[rows, k * CLEN + n:k * CLEN + n + 1],
                                       start=(n == 0), stop=(n == CLEN - 1))
                    for n in range(CLEN):
                        mm = pe.matmul(bank[k][rows, 0:NP2 * NCMP], cw[k][rows, n, :],
                                       a.kT[name][rows, :, n:n + CSTRIDE * (NCMP - 1) + 1:CSTRIDE],
                                       start=(n == 0), stop=(n == CLEN - 1))
            mm.then_inc(done, 1)
            pe.wait_ge(ready, 2)
            for u in range(NP2):
                mm = pe.transpose(bank[2][0:NCMP, u * P:(u + 1) * P], vT[:, u, 0:NCMP], g.c["ident"])
            mm.then_inc(vt_done, 1)

        @block.vector
        def _(dve):
            dve.wait_ge(done, 1)
            dve.tensor_copy(shift[:], bank[4][:, 0:2]).then_inc(shift_ready, 1)
            dve.wait_ge(shift_ready, 1)
            for k, out in enumerate((a.kcmp, vT)):
                dve.tensor_scalar(out[:, :, 0:NCMP], bank[k][:, 0:NP2 * NCMP].rearrange("p (u n) -> p u n", u=NP2),
                                  shift[:, k:k + 1], None, ALU.add).then_inc(ready, 1)
            dve.wait_ge(vt_done, 1)
            dve.tensor_copy(a.vcmp[:].rearrange("n u d -> n (u d)"), bank[2][0:NCMP, 0:NP2 * P]).then_inc(v_ready, 1)


def attention(nc, g, a, yT):
    with Part(nc, "att") as s:
        qs = [s.sb(f"qs{p}", [P, SEQ]) for p in range(2)]
        prob = s.sb("prob", [P, 2, SEQ])
        pT = [s.sb(f"pT{b}", [P, NT, SEQ]) for b in range(2)]
        mx, neg = s.sb("mx", [P, 2]), [s.sb(f"neg{p}", [P, 2]) for p in range(2)]
        total, inv, coef = s.sb("total", [P, 2]), s.sb("inv", [P, 2]), s.sb("coef", [P, 2])
        cmx, csum, cinv, ccoef = (s.sb(k, [P, NT]) for k in ("cmx", "csum", "cinv", "ccoef"))
        cp = s.sb("cprob", [P, NT, 32])
        cpT = s.sb("cprobT", [NCMP, SEQ])
        bS = [[s.ps(f"bS{p}{b}", [P, 512]) for b in range(2)] for p in range(2)]
        bT = [s.ps(f"bT{b}", [P, 512]) for b in range(2)]
        bC, bO = s.ps("bC", [P, 512]), s.ps("bO", [P, 512])
        staged = [s.sem(f"q_staged{p}") for p in range(2)]
        s_done, mx_ready, neg_ready, exp_ready = s.sem("scores_done"), s.sem("mx_ready"), s.sem("neg_ready"), s.sem("exp_ready")
        inv_ready, coef_ready, p_sel, p_win = s.sem("inv_ready"), s.sem("coef_ready"), s.sem("p_sel_ready"), s.sem("p_win_ready")
        t_done, pT_v, pT_a, pv_done, o_copied = s.sem("t_done"), s.sem("pT_sel_ready"), s.sem("pT_win_ready"), s.sem("pv_done"), s.sem("o_copied")
        c_done, c_steps, c_shifted, c_exp, pc_ready, ct_done, cT_ready = (
            s.sem("c_done"), s.sem("c_steps"), s.sem("c_shifted"), s.sem("c_exp"), s.sem("pc_ready"), s.sem("ct_done"), s.sem("cT_ready"))
        block = s.stack.enter_context(nc.Block())
        gates = a.gates[:].rearrange("p i (P a j b) -> p i P a j b", P=NP2, a=2, b=3)

        def heads(eng):
            with eng.Fori(0, NU) as j:
                for pair in range(NP2):
                    for half in range(2):
                        yield 4 * j + 2 * pair + half, j, pair, half

        def following(pair, half):
            return ((pair, 1) if half == 0 else (1, 0) if pair == 0 else (0, 0)), int(pair == 1 and half == 1)

        @block.gpsimd
        def _(pool):
            for counter in (p_win,):
                pool.sem_inc(counter, 1)
            pool.tensor_copy(qs[0][:], a.qT[:, 0, :]).then_inc(staged[0], 1)
            for h, j, pair, half in heads(pool):
                if half == 0:
                    pool.wait_ge(s_done, 4 * h + 1)
                    pool.wait_ge(c_done, h + 1)
                    if pair == 0:
                        pool.tensor_copy(qs[1][:], a.qT[:, ds(NU + j, 1), :].rearrange("p o l -> p (o l)")).then_inc(staged[1], 1)
                    else:
                        pool.tensor_copy(qs[0][:], a.qT[:, ds(j + 1, 1), :].rearrange("p o l -> p (o l)")).then_inc(staged[0], 1)
                for i in range(NT):
                    n = 4 * h + i
                    pool.wait_ge(coef_ready, n + 1)
                    pool.tensor_tensor(prob[:, 1, 0:(i + 1) * P], prob[:, 1, 0:(i + 1) * P],
                                       coef[:, 1:2].to_broadcast([P, (i + 1) * P]), ALU.mult).then_inc(p_win, 1)

        @block.tensor
        def _(pe):
            for counter in (s_done, c_done, t_done, pv_done, ct_done,):
                pe.sem_inc(counter, 1)
            def scores(n, i, pair, half):
                rows = slice(64 * half, 64 * half + 64)
                if type(n) is not int:
                    pe.wait_ge(exp_ready, 2 * n - 2 + 1)
                for b, k in enumerate(("ks", "kw")):
                    out = bS[i % 2][b]
                    pe.matmul(out[:, 0:(i + 1) * P], qs[pair][rows, i * P:(i + 1) * P], a.kT[k][rows, pair, 0:(i + 1) * P],
                              start=True, stop=False)
                    mm = pe.matmul(out[:, i * P:(i + 1) * P], g.c["ident"], g.c["causal"], start=False, stop=True)
                mm.then_inc(s_done, 1)

            def compressed_scores(pair, half):
                rows = slice(64 * half, 64 * half + 64)
                for i in range(NT):
                    pe.matmul(bC[:, i * 32:i * 32 + NCMP], qs[pair][rows, i * P:(i + 1) * P], a.kcmp[rows, pair, 0:NCMP],
                              start=True, stop=False)
                    mm = pe.matmul(bC[:, i * 32:i * 32 + NCMP], g.c["ident"], g.c["cmpmask"][:, i * 32:i * 32 + NCMP], start=False, stop=True)
                mm.then_inc(c_done, 1)

            pe.wait_ge(staged[0], 1)
            compressed_scores(0, 0)
            scores(0, 0, 0, 0)
            for h, j, pair, half in heads(pe):
                (next_pair, next_half), more = following(pair, half)
                for i in range(NT):
                    n = 4 * h + i
                    if i < 3:
                        scores(n + 1, i + 1, pair, half)
                    else:
                        scores(n + 1, 0, next_pair, next_half)
                    pe.wait_ge(p_sel, n + 1)
                    pe.wait_ge(p_win, n + 1 + 1)
                    pe.wait_ge(pT_v, n + 1)
                    pe.wait_ge(pT_a, n + 1)
                    for b in range(2):
                        for k in range(i + 1):
                            mm = pe.transpose(bT[b][:, k * P:(k + 1) * P], prob[:, b, k * P:(k + 1) * P], g.c["ident"])
                    mm.then_inc(t_done, 1)
                    if i == 1:
                        pe.wait_ge(pc_ready, h + 1)
                        for k in range(NT):
                            mm = pe.transpose(bC[0:NCMP, k * P:(k + 1) * P], cp[:, k, 0:NCMP], g.c["ident"])
                        mm.then_inc(ct_done, 1)
                    if i == 2:
                        if half == 1:
                            pe.wait_ge(staged[next_pair], j + 1 + more)
                        pe.wait_ge(cT_ready, h + 1)
                        compressed_scores(next_pair, next_half)
                rows = slice(64 * half, 64 * half + 64)
                dims = slice(P * pair + 64 * half, P * pair + 64 * half + 64)
                pe.wait_ge(pT_v, 4 * h + 4 + 1)
                pe.wait_ge(pT_a, 4 * h + 4 + 1)
                pe.wait_ge(o_copied, 2 * j + pair + 1)
                for k in range(NT):
                    for b in range(2):
                        pe.matmul(bO[rows, k * P:SEQ], a.v[:, k, b, dims], pT[b][:, k, k * P:SEQ], start=(k == 0 and b == 0), stop=False)
                pe.matmul(bO[rows, :], a.vcmp[:, pair, 64 * half:64 * half + 64], cpT[:, :], start=False, stop=True).then_inc(pv_done, 1)

        @block.scalar
        def _(act):
            for counter in (exp_ready, pT_a, o_copied,):
                act.sem_inc(counter, 1)
            for h, j, pair, half in heads(act):
                act.wait_ge(c_shifted, h + 1)
                act.activation(cp[:, :, 0:NCMP], cp[:, :, 0:NCMP], ACT.Exp, scale=SCALE).then_inc(c_exp, 1)
                for i in range(NT):
                    n = 4 * h + i
                    act.wait_ge(neg_ready, n + 1)
                    act.wait_ge(t_done, n + 1)
                    act.wait_ge(inv_ready, n + 1)
                    for b in range(2):
                        act.activation(prob[:, b, 0:(i + 1) * P], bS[i % 2][b][:, 0:(i + 1) * P], ACT.Exp, scale=SCALE,
                                       bias=neg[i % 2][:, b:b + 1], accum_out=total[:, b:b + 1]).then_inc(exp_ready, 1)
                    act.wait_ge(t_done, n + 1 + 1)
                    if i == 0:
                        act.wait_ge(pv_done, h + 1)
                    act.activation(pT[1][:, 0:i + 1, i * P:(i + 1) * P], bT[1][:, 0:(i + 1) * P].rearrange("k (c q) -> k c q", q=P),
                                   ACT.Copy).then_inc(pT_a, 1)
                    if i == 1:
                        act.wait_ge(ct_done, h + 1 + 1)
                        act.wait_ge(pv_done, h + 1)
                        act.activation(cpT[:, :], bC[0:NCMP, :], ACT.Copy).then_inc(cT_ready, 1)
                if half == 1:
                    act.wait_ge(pv_done, h + 1 + 1)
                    act.activation(yT[:, ds(NU * pair + j, 1), :].rearrange("p o l -> p (o l)"), bO[:, :], ACT.Copy).then_inc(o_copied, 1)

        @block.vector
        def _(dve):
            for counter in (pT_v, inv_ready,):
                dve.sem_inc(counter, 1)
            def maxima(n, i):
                dve.wait_ge(s_done, n + 1 + 1)
                for b in range(2):
                    last = dve.tensor_reduce(mx[:, b:b + 1], bS[i % 2][b][:, 0:(i + 1) * P], AX.X, ALU.max)
                    last.then_inc(mx_ready, 1)
                dve.wait_ge(mx_ready, 2 * n + 2)
                if type(n) is not int:
                    dve.wait_ge(exp_ready, 2 * n - 2 + 1)
                dve.tensor_scalar(neg[i % 2][:], mx[:], -SCALE, None, ALU.mult).then_inc(neg_ready, 1)

            maxima(0, 0)
            for h, j, pair, half in heads(dve):
                dve.wait_ge(c_done, h + 1 + 1)
                dve.wait_ge(ct_done, h + 1)
                scores = bC[:, 0:NT * 32].rearrange("p (i n) -> p i n", n=32)[:, :, 0:NCMP]
                dve.tensor_reduce(cmx[:], scores, AX.X, ALU.max).then_inc(c_steps, 1)
                dve.wait_ge(c_steps, 5 * h + 1)
                dve.tensor_tensor(cp[:, :, 0:NCMP], scores, cmx[:].unsqueeze(2).to_broadcast([P, NT, NCMP]), ALU.subtract).then_inc(c_shifted, 1)
                for i in range(NT):
                    n = 4 * h + i
                    dve.wait_ge(exp_ready, 2 * n + 2 + 1)
                    dve.reciprocal(inv[:], total[:]).then_inc(inv_ready, 1)
                    dve.wait_ge(inv_ready, n + 1 + 1)
                    dve.wait_ge(p_win, n + 1)
                    dve.tensor_tensor(coef[:], inv[:], gates[:, i, pair, half, ds(j, 1), 1:3].rearrange("p o b -> p (o b)"),
                                      ALU.mult).then_inc(coef_ready, 1)
                    dve.wait_ge(coef_ready, n + 1)
                    dve.tensor_scalar(prob[:, 0, 0:(i + 1) * P], prob[:, 0, 0:(i + 1) * P], coef[:, 0:1], None, ALU.mult).then_inc(p_sel, 1)
                    if i == 0:
                        dve.wait_ge(c_exp, h + 1)
                        dve.tensor_reduce(csum[:], cp[:, :, 0:NCMP], AX.X, ALU.add).then_inc(c_steps, 1)
                        dve.wait_ge(c_steps, 5 * h + 2)
                        dve.reciprocal(cinv[:], csum[:]).then_inc(c_steps, 1)
                        dve.wait_ge(c_steps, 5 * h + 3)
                        dve.tensor_tensor(ccoef[:], cinv[:], gates[:, :, pair, half, ds(j, 1), 0:1].rearrange("p i o b -> p (i o b)"),
                                          ALU.mult).then_inc(c_steps, 1)
                        dve.wait_ge(c_steps, 5 * h + 4)
                        dve.tensor_tensor(ccoef[:, 0:1], ccoef[:, 0:1], g.c["anycmp"], ALU.mult).then_inc(c_steps, 1)
                        dve.wait_ge(c_steps, 5 * h + 5)
                        dve.tensor_tensor(cp[:, :, 0:NCMP], cp[:, :, 0:NCMP], ccoef[:].unsqueeze(2).to_broadcast([P, NT, NCMP]),
                                          ALU.mult).then_inc(pc_ready, 1)
                    maxima(n + 1, (i + 1) % NT)
                    dve.wait_ge(t_done, n + 1 + 1)
                    if i == 0:
                        dve.wait_ge(pv_done, h + 1)
                    dve.tensor_copy(pT[0][:, 0:i + 1, i * P:(i + 1) * P],
                                    bT[0][:, 0:(i + 1) * P].rearrange("k (c q) -> k c q", q=P)).then_inc(pT_v, 1)


def load_odd_out(nc, w, keep):
    wout = keep.sb("wout", [P, KC, D])
    with Part(nc, "oddw") as s:
        landed = s.sem("wout_landed")
        block = s.stack.enter_context(nc.Block())

        @block.sync
        def _(sp):
            sp.dma_start(wout[:], w["od_w_out_heads"].rearrange("(c p) n -> p c n", p=P)).then_inc(landed, 16)
            sp.wait_ge(landed, 16)
    return wout


def program(nc, w, out, where):
    g = Names()
    g.h_dram = [nc.dram_tensor(f"h{layer}", (SEQ, D), F32, kind="Internal").ap() for layer in range(2)]
    g.acc_dram = [nc.dram_tensor(f"acc{layer}", (SEQ + P, D), F32, kind="Internal").ap() for layer in range(2)]
    load_constants(nc, g, w["const_table"], where)
    g.x = nc.alloc_sbuf_tensor("x_sb", [P, NT, D], F32)
    g.xT = nc.alloc_sbuf_tensor("xT", [P, KC, SEQ], F32)
    g.consts_loaded, g.x_loaded = nc.alloc_semaphore("consts_loaded"), nc.alloc_semaphore("x_loaded")
    with Part(nc, "mixer0") as s:
        yT = s.sb("yT", [P, KC, SEQ])
        wout = even_mixer(nc, g, w, yT, s)
        out_project_norm(nc, "out0", g, yT, wout, w["ln1_g"][0], w["ln1_b"][0])
    moe_layer(nc, g, w, 0)
    with Part(nc, "mixer1") as s:
        yT = s.sb("yT", [P, KC, SEQ])
        odd_mixer(nc, g, w, yT)
        wout = load_odd_out(nc, w, s)
        out_project_norm(nc, "out1", g, yT, wout, w["ln1_g"][1], w["ln1_b"][1])
    moe_layer(nc, g, w, 1, out[0])


AS_THEY_ARE = ["x", "ev_w_in", "s5_w_glu", "ev_w_out", "cmp_w_k", "cmp_w_v", "ln1_g", "ln1_b", "ln2_g", "ln2_b", "router_w",
               "router_b", "ex_w_gate", "ex_w_up", "ex_w_down", "sh_w_gate", "sh_w_up", "sh_w_down"]


def kernel(**inputs):
    import concourse.bacc as bacc
    from concourse.bass_utils import run_bass_kernel_spmd

    w = {k: np.asarray(v) for k, v in inputs.items()}
    arrays = {k: np.ascontiguousarray(w[k]) for k in AS_THEY_ARE}
    arrays["const_table"], where = constant_table()
    arrays["columns"], arrays["b_swapped"], arrays["c_swapped"] = even_layout(w)
    arrays["od_w_in_heads"], arrays["od_w_out_heads"], arrays["pe_columns"] = odd_layout(w)
    nc = bacc.Bacc("TRN2", target_bir_lowering=False, num_devices=1)
    ins = {k: nc.dram_tensor(f"in_{k}", v.shape, mybir.dt.from_np(v.dtype), kind="ExternalInput").ap() for k, v in arrays.items()}
    out = nc.dram_tensor("out", (1, SEQ, D), F32, kind="ExternalOutput").ap()
    program(nc, ins, out, where)
    r = run_bass_kernel_spmd(nc, [{f"in_{k}": v for k, v in arrays.items()}], core_ids=[0])
    return r.results[0]["out"]
```

```python
from contextlib import ExitStack

import numpy as np
from concourse import mybir
from concourse.bass import IndirectOffsetOnAxis, ds

BF16 = mybir.dt.bfloat16
F32, F32R, U32, I32 = mybir.dt.float32, mybir.dt.float32r, mybir.dt.uint32, mybir.dt.int32
ALU, ACT, AX = mybir.AluOpType, mybir.ActivationFunctionType, mybir.AxisListType


class Names:
    pass
P = 128
SEQ, D, NT = 512, 1024, 4
KC = D // P
E, TOPK, DE = 64, 8, 256
HC = DE // P
ALPHA, EPS, ROUTE_SCALE = 4.0 ** 0.25, 1e-5, 2.5
NB = SEQ * TOPK // P + E
TABLES = 5
NBT = NB + 4


class Part:

    def __init__(self, nc, name):
        self.nc, self.name, self.stack, self.sems = nc, name, ExitStack(), []

    def __enter__(self):
        return self

    def __exit__(self, *exc):
        done = self.stack.__exit__(*exc)
        if exc[0] is None and self.sems:
            self.nc.clear_and_free_semaphores(self.sems)
            self.nc.all_engine_barrier()
        return done

    def sb(self, name, shape, dtype=F32):
        return self.stack.enter_context(self.nc.sbuf_tensor(f"{self.name}_{name}", shape, dtype))

    def ps(self, name, shape, dtype=F32):
        return self.stack.enter_context(self.nc.psum_tensor(f"{self.name}_{name}", shape, dtype))

    def sem(self, name):
        self.sems.append(self.nc.alloc_semaphore(f"{self.name}_{name}"))
        return self.sems[-1]


class Chain:

    def __init__(self, sem):
        self.sem, self.count = sem, 0

    def mark(self, instruction):
        instruction.then_inc(self.sem, 1)
        self.count += 1
        return self.count

    def link(self, engine, instruction):
        engine.wait_ge(self.sem, self.mark(instruction))


def emit_transposes(pe, x_sb, ident, banks, done, evacuated):
    for c in range(KC):
        if c >= 2:
            pe.wait_ge(evacuated[c % 2], c // 2)
        for i in range(NT):
            mm = pe.transpose(banks[c % 2][:, i * P:(i + 1) * P],
                              x_sb[:, i, :].rearrange("t (k c) -> t c k", c=KC)[:, c, :], ident)
        mm.then_inc(done, 1)


def moe_route(nc, name, g, moe, w, layer):
    with Part(nc, name) as s:
        rw = s.sb("rw", [P, KC, E])
        rb = s.sb("rb", [P, E])
        sgu = s.sb("sgu", [P, 2, KC, DE])
        sdn = s.sb("sdn", [P, HC, D])
        scores = s.sb("scores", [P, NT, E])
        biased = s.sb("biased", [P, NT, E])
        top = s.sb("top", [P, NT, 8])
        rest = s.sb("rest", [P, NT, E])
        sel = s.sb("sel", [P, NT, E])
        gate = s.sb("gate", [P, NT, E])
        gsum = s.sb("gsum", [P, NT])
        ginv = s.sb("ginv", [P, NT])
        pos = s.sb("pos", [P, NT, E])
        posT = s.sb("posT", [E, SEQ])
        gateT = s.sb("gateT", [E, SEQ])
        cnt = s.sb("cnt", [E, 1])
        over = s.sb("over", [E, 4])
        nblk = s.sb("nblk", [E, 1])
        incl = s.sb("incl", [E, 1])
        excl = s.sb("excl", [E, 1])
        owner = s.sb("owner", [E, NBT])
        base = s.sb("base", [E, NBT])
        ownbase = s.sb("ownbase", [E, NBT])
        gleft, gpart = s.sb("gleft", [P, NT, NBT]), s.sb("gpart", [P, NT, NBT])
        sil = s.sb("sil", [P, DE])
        hid = s.sb("hid", [P, DE])
        hidT = s.sb("hidT", [P, HC, P])
        accsb = s.sb("accsb", [P, 2, D])
        bank = [s.ps(f"bank{k}", [P, 512]) for k in range(8)]
        bT, bL, bG, bH, bY = bank[0:2], bank[2], bank[3], bank[4], bank[5:7]
        bS = bank[7]
        loaded, shared_loaded = s.sem("loaded"), s.sem("shared_loaded")
        xt_done, xt_a, xt_v = s.sem("xt_done"), s.sem("xt_copied_act"), s.sem("xt_copied_dve")
        logits_done, scores_ready = s.sem("logits_done"), s.sem("scores_ready")
        sel_ready, gate_ready, pos_done, pos_ready = s.sem("sel_ready"), s.sem("gate_ready"), s.sem("pos_done"), s.sem("pos_ready")
        nblk_ready, incl_done, owner_ready = s.sem("nblk_ready"), s.sem("incl_done"), s.sem("owner_ready")
        tt_done, tt_ready, tab_done, tab_ready = s.sem("tt_done"), s.sem("tt_ready"), s.sem("tab_done"), s.sem("tab_ready")
        gu_done, silu_ready, hid_ready, hidT_done, hidT_ready = (
            s.sem("gu_done"), s.sem("silu_ready"), s.sem("hid_ready"), s.sem("hidT_done"), s.sem("hidT_ready"))
        dn_done, acc_ready = s.sem("dn_done"), s.sem("acc_ready")
        base_written = [s.sem(f"base_written{p}") for p in range(2)]
        dve_steps = Chain(s.sem("dve_steps"))
        c = g.c
        block = s.stack.enter_context(nc.Block())

        @block.sync
        def _(sp):
            sp.dma_start(rw[:], w["router_w"][layer].rearrange("(p c) e -> p c e", c=KC)).then_inc(loaded, 16)
            sp.dma_start(rb[:], w["router_b"][layer].partition_broadcast(P)).then_inc(loaded, 16)
            sp.dma_start(sgu[:, 0], w["sh_w_gate"][layer].rearrange("(p c) f -> p c f", c=KC)).then_inc(shared_loaded, 16)
            sp.dma_start(sgu[:, 1], w["sh_w_up"][layer].rearrange("(p c) f -> p c f", c=KC)).then_inc(shared_loaded, 16)
            sp.dma_start(sdn[:], w["sh_w_down"][layer].rearrange("(p c) n -> p c n", c=HC)).then_inc(shared_loaded, 16)
            for i in range(NT):
                sp.dma_start(moe.h_dram[i * P:(i + 1) * P, :], g.x[:, i, :]).then_inc(moe.h_written, 16)
            moe.norm.load(sp)
            if layer == 0:
                g.load_wide(sp, w["od_w_in_heads"].rearrange("(p c) f -> p c f", c=KC)[:, :, 0:D])
            for i in range(NT):
                if i == 2:
                    sp.wait_ge(moe.tables, 2)
                    for b in range(2):
                        e = sp.value_load(moe.owner_id[0:1, b:b + 1], min_val=0, max_val=E - 1)
                        moe.load_gu(sp, e, b)
                        moe.load_dn(sp, e, b)
                sp.wait_ge(acc_ready, i + 1)
                sp.dma_start(moe.acc_dram[i * P:(i + 1) * P, :], accsb[:, i % 2, :]).then_inc(base_written[i % 2], 16)
            for p in range(2):
                sp.wait_ge(base_written[p], 16 * NT // 2)
            sp.wait_ge(moe.h_written, 16 * NT)

        @block.gpsimd
        def _(pool):
            for p in range(2):
                pool.memset(moe.xg[p][:], 0.0)

        @block.tensor
        def _(pe):
            emit_transposes(pe, g.x, c["ident"], bT, xt_done, (xt_a, xt_v))
            pe.wait_ge(loaded, 32)
            pe.wait_ge(xt_a, 4)
            pe.wait_ge(xt_v, 4)
            for i in range(NT):
                for k in range(KC):
                    mm = pe.matmul(bL[:, i * E:(i + 1) * E], g.xT[:, k, i * P:(i + 1) * P], rw[:, k, :],
                                   start=(k == 0), stop=(k == KC - 1))
            mm.then_inc(logits_done, 1)
            pe.wait_ge(shared_loaded, 48)

            def gate_up(i):
                if i:
                    pe.wait_ge(hid_ready, i)
                for k in range(KC):
                    mm = pe.matmul(bG[:, :], g.xT[:, k, i * P:(i + 1) * P], sgu[:, :, k, :],
                                   start=(k == 0), stop=(k == KC - 1))
                mm.then_inc(gu_done, 1)

            def hidden_transposes(i):
                pe.wait_ge(hid_ready, i + 1)
                if i:
                    pe.wait_ge(hidT_ready, i)
                for k in range(HC):
                    mm = pe.transpose(bH[:, k * P:(k + 1) * P],
                                      hid[:].rearrange("t (k c) -> t c k", c=HC)[:, k, :], c["ident"])
                mm.then_inc(hidT_done, 1)

            def down(i):
                pe.wait_ge(hidT_ready, i + 1)
                if i:
                    pe.wait_ge(acc_ready, i)
                for h in range(2):
                    for k in range(HC):
                        mm = pe.matmul(bY[h][:, :], hidT[:, k, :], sdn[:, k, h * 512:(h + 1) * 512],
                                       start=(k == 0), stop=(k == HC - 1))
                mm.then_inc(dn_done, 1)

            gate_up(0)
            pe.wait_ge(sel_ready, 1)
            for i in range(NT):
                pe.matmul(bS[:, i * E:(i + 1) * E], c["upto"], sel[:, i, :], start=True, stop=(i == 0))
                for j in range(i):
                    pe.matmul(bS[:, i * E:(i + 1) * E], c["ones"], sel[:, j, :], start=False, stop=(j == i - 1))
            for i in range(NT):
                mm = pe.matmul(bS[0:E, 256:257], sel[:, i, :], c["ones"][:, 0:1], start=(i == 0), stop=(i == NT - 1))
            mm.then_inc(pos_done, 1)
            hidden_transposes(0)
            gate_up(1)
            pe.wait_ge(nblk_ready, 1)
            pe.wait_ge(pos_ready, 1)
            pe.matmul(bS[0:E, 260:261], c["upto"][0:E, 0:E], nblk[:], start=True, stop=True)
            pe.matmul(bS[:, 264:265], c["ones"][0:E, :], nblk[:], start=True, stop=True).then_inc(incl_done, 1)
            down(0)
            pe.wait_ge(pos_ready, 1)
            pe.wait_ge(gate_ready, 1)
            for i in range(NT):
                pe.transpose(bT[0][0:E, i * P:(i + 1) * P], pos[:, i, :], c["ident"])
                mm = pe.transpose(bT[1][0:E, i * P:(i + 1) * P], gate[:, i, :], c["ident"])
            mm.then_inc(tt_done, 1)
            hidden_transposes(1)
            gate_up(2)
            down(1)
            pe.wait_ge(owner_ready, 1)
            pe.wait_ge(tt_ready, 2)
            for i in range(NT):
                pe.matmul(bT[0][:, i * NBT:(i + 1) * NBT], posT[:, i * P:(i + 1) * P], owner[:], start=True, stop=False)
                pe.matmul(bT[0][:, i * NBT:(i + 1) * NBT], c["negones"][0:E, :], ownbase[:], start=False, stop=True)
                pe.matmul(bT[1][:, i * NBT:(i + 1) * NBT], gateT[:, i * P:(i + 1) * P], owner[:], start=True, stop=True)
            pe.matmul(bS[:, 300:300 + NBT], c["rowno"][0:E, :], owner[:], start=True, stop=True).then_inc(tab_done, 1)
            hidden_transposes(2)
            gate_up(3)
            down(2)
            hidden_transposes(3)
            down(3)

        @block.scalar
        def _(act):
            for k in range(0, KC, 2):
                act.wait_ge(xt_done, k + 1)
                act.activation(g.xT[:, k, :], bT[0][:, :], ACT.Copy).then_inc(xt_a, 1)
            act.wait_ge(logits_done, 1)
            act.activation(scores[:].rearrange("p i e -> p (i e)"), bL[:, 0:NT * E], ACT.Sigmoid).then_inc(scores_ready, 1)
            for i in range(NT):
                act.wait_ge(gu_done, i + 1)
                if i:
                    act.wait_ge(hid_ready, i)
                act.activation(sil[:], bG[:, 0:DE], ACT.Silu).then_inc(silu_ready, 1)
                act.wait_ge(hidT_done, i + 1)
                if i:
                    act.wait_ge(dn_done, i)
                act.activation(hidT[:].rearrange("p c t -> p (c t)"), bH[:, 0:DE], ACT.Copy).then_inc(hidT_ready, 1)

        @block.vector
        def _(dve):
            for k in range(1, KC, 2):
                dve.wait_ge(xt_done, k + 1)
                dve.tensor_copy(g.xT[:, k, :], bT[1][:, :]).then_inc(xt_v, 1)

            def shared_hidden(i):
                dve.wait_ge(silu_ready, i + 1)
                if i:
                    dve.wait_ge(hidT_done, i)
                dve.tensor_tensor(hid[:], sil[:], bG[:, DE:2 * DE], ALU.mult).then_inc(hid_ready, 1)

            def shared_sum(i):
                dve.wait_ge(dn_done, i + 1)
                if i >= 2:
                    dve.wait_ge(base_written[i % 2], 16 * (i // 2))
                for h in range(2):
                    cols = slice(h * 512, (h + 1) * 512)
                    last = dve.scalar_tensor_tensor(accsb[:, i % 2, cols], g.x[:, i, cols], ALPHA, bY[h][:, :],
                                                    ALU.mult, ALU.add)
                last.then_inc(acc_ready, 1)

            link = lambda ins: dve_steps.link(dve, ins)
            dve.wait_ge(loaded, 32)
            dve.wait_ge(scores_ready, 1)
            link(dve.tensor_tensor(biased[:], scores[:], rb[:].unsqueeze(1).to_broadcast([P, NT, E]), ALU.add))
            for i in range(NT):
                last = dve_steps.mark(dve.max(top[:, i, :], biased[:, i, :]))
            dve.wait_ge(dve_steps.sem, last)
            for i in range(NT):
                last = dve_steps.mark(dve.match_replace(rest[:, i, :], top[:, i, :], biased[:, i, :], -3e38))
            dve.wait_ge(dve_steps.sem, last)
            dve.tensor_tensor(sel[:], rest[:], biased[:], ALU.not_equal).then_inc(sel_ready, 1)
            shared_hidden(0)
            dve.wait_ge(sel_ready, 1)
            link(dve.tensor_tensor(gate[:], scores[:], sel[:], ALU.mult))
            link(dve.tensor_reduce(gsum[:], gate[:], AX.X, ALU.add))
            link(dve.reciprocal(ginv[:], gsum[:]))
            for i in range(NT):
                last = dve.tensor_scalar(gate[:, i, :], gate[:, i, :], ginv[:, i:i + 1], ROUTE_SCALE, ALU.mult, ALU.mult)
            last.then_inc(gate_ready, 1)
            dve.wait_ge(pos_done, 1)
            link(dve.tensor_copy(cnt[:], bS[0:E, 256:257]))
            link(dve.tensor_scalar(over[:], c["thresholds"][0:E, :], cnt[:, 0:1], None, ALU.is_lt))
            dve.tensor_reduce(nblk[:], over[:], AX.X, ALU.add).then_inc(nblk_ready, 1)
            dve.tensor_tensor(pos[:].rearrange("p i e -> p (i e)"), bS[:, 0:NT * E],
                              sel[:].rearrange("p i e -> p (i e)"), ALU.mult).then_inc(pos_ready, 1)
            shared_hidden(1)
            dve.wait_ge(incl_done, 1)
            dve.wait_ge(nblk_ready, 1)
            link(dve.tensor_copy(incl[:], bS[0:E, 260:261]))
            link(dve.tensor_tensor(excl[:], incl[:], nblk[:], ALU.subtract))
            dve.tensor_scalar(moe.trips[0:1, 0:1], bS[0:1, 264:265], 0.5, 0.5, ALU.add, ALU.mult).then_inc(moe.tables, 1)
            link(dve.tensor_scalar(owner[:], c["blockno"][0:E, 0:NBT], excl[:, 0:1], None, ALU.is_ge))
            link(dve.scalar_tensor_tensor(owner[:], c["blockno"][0:E, 0:NBT], incl[:, 0:1], owner[:], ALU.is_lt, ALU.mult))
            link(dve.tensor_scalar(base[:], c["blockno"][0:E, 0:NBT], excl[:, 0:1], float(P), ALU.subtract, ALU.mult))
            dve.tensor_tensor(ownbase[:], base[:], owner[:], ALU.mult).then_inc(owner_ready, 1)
            shared_sum(0)
            dve.wait_ge(tt_done, 1)
            dve.tensor_copy(posT[:], bT[0][0:E, :]).then_inc(tt_ready, 1)
            dve.tensor_copy(gateT[:], bT[1][0:E, :]).then_inc(tt_ready, 1)
            shared_hidden(2)
            shared_sum(1)
            dve.wait_ge(tab_done, 1)
            dve.tensor_copy(moe.owner_id[0:1, :], bS[0:1, 300:300 + NBT]).then_inc(moe.tables, 1)
            dve.tensor_copy(moe.posb[:].rearrange("p i b -> p (i b)"), bT[0][:, 0:NT * NBT]).then_inc(moe.tables, 1)
            link(dve.tensor_copy(gleft[:], bT[1][:, 0:NT * NBT].rearrange("p (i b) -> p i b", i=NT)))
            for k in range(3):
                link(dve.tensor_copy(moe.entry[:, :, :, 3 + k], gleft[:]))
                if k < 2:
                    link(dve.tensor_copy(gpart[:], moe.entry[:, :, :, 3 + k]))
                    link(dve.tensor_tensor(gleft[:], gleft[:], gpart[:], ALU.subtract))
            dve.memset(moe.entry[:, :, :, 2], 0.0)
            dve.memset(moe.entry[:, :, :, 6], 1.0).then_inc(moe.tables, 1)
            dve.tensor_copy(moe.entry[:, :, :, 0], c["tokhi"].unsqueeze(2).to_broadcast([P, NT, NBT]))
            dve.tensor_copy(moe.entry[:, :, :, 1], c["toklo"].unsqueeze(2).to_broadcast([P, NT, NBT])).then_inc(moe.tables, 1)
            shared_hidden(3)
            shared_sum(2)
            shared_sum(3)


def moe_experts(nc, name, g, moe, w, layer):
    with Part(nc, name) as s:
        wgu, wdn, gu_landed, dn_landed = moe.wgu, moe.wdn, moe.gu_landed, moe.dn_landed
        hot = s.sb("hot", [P, NT, P], BF16)
        free1 = s.sb("free1", [P, 1])
        listed = [s.sb(f"listed{p}", [P, 2]) for p in range(2)]
        idx = [s.sb(f"idx{p}", [P, 1], U32) for p in range(2)]
        kidx = [s.sb(f"kidx{p}", [P, 1], U32) for p in range(2)]
        sgate = [s.sb(f"sgate{p}", [P, 1]) for p in range(2)]
        sidx = [s.sb(f"sidx{p}", [P, 1], U32) for p in range(2)]
        xgT = s.sb("xgT", [P, KC, P])
        sil = s.sb("sil", [P, DE])
        hid = s.sb("hid", [P, DE])
        hidT = s.sb("hidT", [P, HC, P])
        y = [s.sb(f"y{p}", [P, D]) for p in range(2)]
        bX = [s.ps(f"bX{k}", [P, 512]) for k in range(2)]
        bG, bH, bL = s.ps("bG", [P, 512]), s.ps("bH", [P, 512]), s.ps("bL", [P, 512])
        bY = [s.ps(f"bY{k}", [P, 512]) for k in range(2)]
        hot_ready, list_done, idx_ready = s.sem("hot_ready"), s.sem("list_done"), s.sem("idx_ready")
        kept, sidx_ready, gathered, xT_done = s.sem("kept"), s.sem("sidx_ready"), [s.sem(f"gathered{p}") for p in range(2)], s.sem("xT_done")
        xT_a, xT_v = s.sem("xT_copied_act"), s.sem("xT_copied_dve")
        gu_done, silu_ready, hid_ready = s.sem("gu_done"), s.sem("silu_ready"), s.sem("hid_ready")
        hidT_done, hidT_ready, dn_done = s.sem("hidT_done"), s.sem("hidT_ready"), s.sem("dn_done")
        y_a, y_v, listed_ready = s.sem("y_act"), s.sem("y_dve"), s.sem("listed_ready")
        scattered, sending = s.sem("scattered"), s.sem("sending")
        gathering, loading = s.sem("gathering"), s.sem("loading")
        c = g.c
        block = s.stack.enter_context(nc.Block())

        def trips(eng):
            eng.wait_ge(moe.tables, TABLES)
            return eng.value_load(moe.trips[0:1, 0:1], min_val=NB // 2 - E // 2, max_val=NB // 2)

        def pairs(eng, but=0):
            n = trips(eng)
            with eng.Fori(0, eng.snap(n - but) if but else n) as i:
                for p in range(2):
                    yield 2 * i + p, i, p

        @block.sync
        def _(sp):
            def owner_of(b):
                sp.wait_ge(moe.tables, TABLES)
                return sp.value_load(moe.owner_id[0:1, ds(b, 1)], min_val=0, max_val=E - 1)

            sp.wait_ge(gu_done, 1)
            moe.load_gu(sp, owner_of(2), 0)
            for b, i, p in pairs(sp, but=1):
                sp.wait_ge(gu_done, b + 2)
                sp.sem_inc(loading, 1)
                moe.load_gu(sp, owner_of(b + 3), 1 - p)
                sp.wait_ge(dn_done, b + 1)
                sp.sem_inc(loading, 1)
                moe.load_dn(sp, owner_of(b + 2), p)
            n = sp.snap(trips(sp))
            sp.wait_ge(gu_landed[0], 32 * n + 32)
            sp.sem_inc(loading, 1)

        @block.gpsimd
        def _(pool):
            for counter in (sending,):
                pool.sem_inc(counter, 1)
            def gather(b, p):
                pool.wait_ge(idx_ready, b + 1)
                if type(b) is not int or b >= 2:
                    pool.wait_ge(xT_done, b - 1)
                pool.sem_inc(gathering, 1)
                pool.indirect_dma_start(out=moe.xg[p][:], out_offset=None, in_=moe.h_dram[0:SEQ, :],
                                        in_offset=IndirectOffsetOnAxis(ap=idx[p][:, 0:1], axis=0),
                                        bounds_check=SEQ - 1, oob_is_err=False).then_inc(gathered[p], 16)

            pool.dma_start(moe.acc_dram[SEQ:SEQ + P, :], moe.xg[0][:]).then_inc(scattered, 16)
            pool.wait_ge(scattered, 16)
            for b in range(3):
                gather(b, b % 2)
            for b, i, p in pairs(pool):
                gather(b + 3, 1 - p)
                pool.wait_ge(y_a, b + 1 + 1)
                pool.wait_ge(y_v, b + 1 + 1)
                pool.wait_ge(sidx_ready, b + 1)
                pool.wait_ge(scattered, 16 * b + 16)
                pool.sem_inc(sending, 1)
                pool.indirect_dma_start(out=moe.acc_dram[:, :], out_offset=IndirectOffsetOnAxis(ap=sidx[p][:, 0:1], axis=0),
                                        in_=y[p][:], in_offset=None, compute_op=ALU.add).then_inc(scattered, 16)
            n = pool.snap(trips(pool))
            pool.wait_ge(scattered, 32 * n + 16)
            pool.wait_ge(gathered[0], 16 * n + 32)
            pool.wait_ge(gathered[1], 16 * n + 16)
            pool.sem_inc(gathering, 1)

        @block.tensor
        def _(pe):
            def slot_list(b):
                pe.wait_ge(hot_ready, b + 1)
                pe.wait_ge(idx_ready, b)
                for i in range(NT):
                    mm = pe.matmul(bL[:, 0:7], hot[:, i, :], moe.entry[:, i, ds(b, 1), :].rearrange("p o k -> p (o k)"),
                                   start=(i == 0), stop=(i == NT - 1))
                mm.then_inc(list_done, 1)

            def rows_transposes(b, p, turn):
                pe.wait_ge(gathered[p], 16 * turn + 16)
                pe.wait_ge(xT_a, b)
                pe.wait_ge(xT_v, b)
                for k in range(KC):
                    mm = pe.transpose(bX[k // 4][:, (k % 4) * P:(k % 4 + 1) * P],
                                      moe.xg[p][:].rearrange("t (k c) -> t c k", c=KC)[:, k, :], c["ident"])
                mm.then_inc(xT_done, 1)

            def gate_up(b, p, turn):
                pe.wait_ge(gu_landed[p], 32 * turn + 32)
                pe.wait_ge(xT_a, b + 1)
                pe.wait_ge(xT_v, b + 1)
                pe.wait_ge(hid_ready, b)
                for k in range(KC):
                    mm = pe.matmul(bG[:, :], xgT[:, k, :], wgu[p][:, :, k, :], start=(k == 0), stop=(k == KC - 1))
                mm.then_inc(gu_done, 1)

            for b in range(2):
                slot_list(b)
            rows_transposes(0, 0, 0)
            slot_list(2)
            gate_up(0, 0, 0)
            rows_transposes(1, 1, 0)
            for b, i, p in pairs(pe):
                pe.wait_ge(hid_ready, b + 1)
                pe.wait_ge(hidT_ready, b + 1)
                for k in range(HC):
                    mm = pe.transpose(bH[:, k * P:(k + 1) * P],
                                      hid[:].rearrange("t (k c) -> t c k", c=HC)[:, k, :], c["ident"])
                mm.then_inc(hidT_done, 1)
                slot_list(b + 3)
                gate_up(b + 1, 1 - p, i + p)
                rows_transposes(b + 2, p, i + 1)
                pe.wait_ge(dn_landed[p], 16 * i + 16)
                pe.wait_ge(hidT_ready, b + 1 + 1)
                pe.wait_ge(y_a, b + 1)
                pe.wait_ge(y_v, b + 1)
                for h in range(2):
                    for k in range(HC):
                        mm = pe.matmul(bY[h][:, :], hidT[:, k, :], wdn[p][:, k, h * 512:(h + 1) * 512],
                                       start=(k == 0), stop=(k == HC - 1))
                mm.then_inc(dn_done, 1)

        @block.scalar
        def _(act):
            for counter in (hidT_ready, y_a,):
                act.sem_inc(counter, 1)
            def copy_rows(b):
                act.wait_ge(xT_done, b + 1)
                act.activation(xgT[:, 0:4, :].rearrange("p k t -> p (k t)"), bX[0][:, :], ACT.Copy).then_inc(xT_a, 1)

            def silu(b):
                act.wait_ge(gu_done, b + 1)
                act.wait_ge(hid_ready, b)
                act.activation(sil[:], bG[:, 0:DE], ACT.Silu).then_inc(silu_ready, 1)

            copy_rows(0)
            silu(0)
            copy_rows(1)
            for b, i, p in pairs(act):
                act.wait_ge(hidT_done, b + 1)
                act.activation(hidT[:].rearrange("p c t -> p (c t)"), bH[:, 0:DE], ACT.Copy).then_inc(hidT_ready, 1)
                silu(b + 1)
                copy_rows(b + 2)
                act.wait_ge(dn_done, b + 1)
                act.wait_ge(sidx_ready, b + 1)
                act.activation(y[p][:, 0:512], bY[0][:, :], ACT.Copy, scale=sgate[p][:, 0:1]).then_inc(y_a, 1)

        @block.vector
        def _(dve):
            for counter in (y_v,):
                dve.sem_inc(counter, 1)
            def one_hot(b):
                dve.wait_ge(list_done, b)
                dve.tensor_tensor(hot[:], c["slotno"].unsqueeze(1).to_broadcast([P, NT, P]),
                                  moe.posb[:, :, ds(b, 1)].to_broadcast([P, NT, P]), ALU.is_equal).then_inc(hot_ready, 1)

            def take_list(b, p):
                dve.wait_ge(list_done, b + 1)
                dve.tensor_reduce(listed[p][:], bL[:, 0:6].rearrange("p (v k) -> p v k", k=3), AX.X, ALU.add)
                dve.tensor_scalar(free1[:], bL[:, 6:7], 1.0, c["negtrash"], ALU.subtract, ALU.mult).then_inc(listed_ready, 1)
                dve.wait_ge(listed_ready, b + 1)
                dve.tensor_tensor(idx[p][:], listed[p][:, 0:1], free1[:], ALU.add).then_inc(idx_ready, 1)

            def keep(b, p):
                dve.wait_ge(idx_ready, b + 1)
                dve.tensor_copy(kidx[p][:], idx[p][:])
                dve.tensor_copy(sgate[p][:], listed[p][:, 1:2]).then_inc(kept, 1)

            def copy_rows(b):
                dve.wait_ge(xT_done, b + 1)
                dve.tensor_copy(xgT[:, 4:8, :].rearrange("p k t -> p (k t)"), bX[1][:, :]).then_inc(xT_v, 1)

            def hidden(b):
                dve.wait_ge(silu_ready, b + 1)
                dve.wait_ge(hidT_done, b)
                dve.tensor_tensor(hid[:], sil[:], bG[:, DE:2 * DE], ALU.mult).then_inc(hid_ready, 1)

            one_hot(0)
            for b in range(2):
                one_hot(b + 1)
                take_list(b, b)
            keep(0, 0)
            copy_rows(0)
            one_hot(3)
            dve.wait_ge(kept, 1)
            take_list(2, 0)
            hidden(0)
            copy_rows(1)
            for b, i, p in pairs(dve):
                dve.wait_ge(sending, b + 1)
                dve.wait_ge(kept, b + 1)
                dve.tensor_copy(sidx[p][:], kidx[p][:]).then_inc(sidx_ready, 1)
                dve.wait_ge(y_a, b + 1)
                dve.wait_ge(y_v, b + 1)
                dve.wait_ge(sidx_ready, b + 1)
                keep(b + 1, 1 - p)
                dve.wait_ge(kept, b + 2)
                take_list(b + 3, 1 - p)
                hidden(b + 1)
                copy_rows(b + 2)
                one_hot(b + 4)
                dve.wait_ge(dn_done, b + 1)
                dve.tensor_scalar(y[p][:, 512:1024], bY[1][:, :], sgate[p][:, 0:1], None, ALU.mult).then_inc(y_v, 1)


def moe_layer(nc, g, w, layer, out=None):
    with Part(nc, f"moe{layer}") as s:
        m = Names()
        m.h_dram, m.acc_dram = g.h_dram[layer], g.acc_dram[layer]
        m.posb = s.sb("posb", [P, NT, NBT])
        m.entry = s.sb("entry", [P, NT, NBT, 7], BF16)
        m.owner_id = s.sb("owner_id", [1, NBT], I32)
        m.trips = s.sb("trips", [1, 1], I32)
        m.xg = [s.sb(f"xg{p}", [P, D]) for p in range(2)]
        m.wgu = [s.sb(f"wgu{p}", [P, 2, KC, DE]) for p in range(2)]
        m.wdn = [s.sb(f"wdn{p}", [P, HC, D]) for p in range(2)]
        m.gu_landed = [s.sem(f"gu_landed{p}") for p in range(2)]
        m.dn_landed = [s.sem(f"dn_landed{p}") for p in range(2)]
        m.h_written = s.sem("h_written")
        m.tables = s.sem("tables_ready")

        def load_gu(sp, e, p):
            for k, src in enumerate((w["ex_w_gate"], w["ex_w_up"])):
                sp.dma_start(m.wgu[p][:, k], src[layer, ds(e, 1)].rearrange("o (p c) f -> p (o c) f", c=KC)).then_inc(m.gu_landed[p], 16)

        def load_dn(sp, e, p):
            sp.dma_start(m.wdn[p][:], w["ex_w_down"][layer, ds(e, 1)].rearrange("o (p c) n -> p (o c) n", c=HC)).then_inc(m.dn_landed[p], 16)

        m.load_gu, m.load_dn = load_gu, load_dn
        m.norm = Norm(s, g, w["ln2_g"][layer], w["ln2_b"][layer])
        moe_route(nc, f"route{layer}", g, m, w, layer)
        moe_experts(nc, f"experts{layer}", g, m, w, layer)
        norm_from_dram(nc, f"norm{layer}", g, m.acc_dram, m.norm, out)
HD, NH = 64, 16
NCMP, CSTRIDE, CLEN = (SEQ - 32) // 16 + 1, 16, 32


def constant_table():
    p = np.arange(P)
    half = HD // 2
    inv = np.float32(10000.0) ** (-np.arange(half, dtype=np.float32) / np.float32(half))
    ang = np.arange(SEQ, dtype=np.float32)[None, :] * inv[p % half][:, None]
    rot = np.zeros((P, P), np.float32)
    for m in range(P):
        rot[m + half if m % HD < half else m - half, m] = -1.0 if m % HD < half else 1.0
    ends = np.arange(32) * CSTRIDE + CLEN - 1
    t = np.arange(NT)[None, :, None] * P + p[:, None, None]
    parts = {
        "ident": np.eye(P), "upto": p[:, None] <= p[None, :], "ones": np.ones((P, P)), "negones": -np.ones((P, P)),
        "rowno": np.repeat(p[:, None], P, 1), "slotno": np.repeat(p[None, :] + 1, P, 0),
        "thresholds": np.repeat(np.arange(4)[None, :] * P, P, 0), "blockno": np.repeat(np.arange(NBT)[None, :], P, 0),
        "tokhi": np.arange(NT)[None, :] * P + p[:, None] // 16 * 16, "toklo": np.repeat(p[:, None] % 16, NT, 1), "negtrash": -(SEQ + p[:, None]),
        "time": np.repeat(np.arange(SEQ)[None, :], P, 0), "cos": np.cos(ang), "sin": np.sin(ang), "rot": rot,
        "causal": np.where(p[None, :] > p[:, None], -1e30, 0.0),
        "cmpmask": np.where(ends[None, None, :] > t, -1e30, 0.0).reshape(P, -1),
        "anycmp": (p[:, None] >= CLEN - 1),
    }
    table = np.concatenate([np.asarray(v, np.float32) for v in parts.values()], axis=1)
    at, where = 0, {}
    for k, v in parts.items():
        where[k] = (at, at + v.shape[1])
        at += v.shape[1]
    return np.ascontiguousarray(table), where


def load_constants(nc, g, const_dram, where):
    cs = nc.alloc_sbuf_tensor("const_sb", [P, const_dram.shape[1]], F32)
    g.c = {k: cs[:, a:b] for k, (a, b) in where.items()}
    g.const_sb = cs


def make_wide(nc, g):
    g.wide = nc.alloc_sbuf_tensor("wide", [P, KC, D], F32)
    g.wide_landed = nc.alloc_semaphore("wide_landed")
    loads = []

    def load_wide(sp, source):
        loads.append(source)
        sp.dma_start(g.wide[:], source).then_inc(g.wide_landed, 16)

    def wait_wide(pe):
        pe.wait_ge(g.wide_landed, 16 * len(loads))

    g.load_wide, g.wait_wide = load_wide, wait_wide


class Norm:

    def __init__(self, s, g, gamma, beta):
        self.g = g
        self.gamma, self.beta = s.sb("ln_g", [P, D]), s.sb("ln_b", [P, D])
        self.gamma_dram, self.beta_dram = gamma, beta
        self.stats, self.mv = s.sb("ln_stats", [P, NT, 2, 6]), s.sb("ln_mv", [P, NT, 2])
        self.std, self.rstd, self.eps = s.sb("ln_std", [P, NT]), s.sb("ln_rstd", [P, NT]), s.sb("ln_eps", [P, 1])
        self.loaded, self.eps_ready = s.sem("ln_loaded"), s.sem("ln_eps_ready")
        self.mv_ready, self.std_ready, self.rstd_ready = s.sem("ln_mv_ready"), s.sem("ln_std_ready"), s.sem("ln_rstd_ready")
        self.centred, self.scaled = s.sem("ln_centred"), s.sem("ln_scaled")
        self.done, self.last_done = s.sem("ln_done"), s.sem("ln_last_done")
        self.steps = Chain(s.sem("ln_dve_steps"))

    def load(self, sp):
        sp.dma_start(self.gamma[:], self.gamma_dram.partition_broadcast(P)).then_inc(self.loaded, 16)
        sp.dma_start(self.beta[:], self.beta_dram.partition_broadcast(P)).then_inc(self.loaded, 16)

    def wait_tile(self, engine, i):
        if i < NT - 1:
            engine.wait_ge(self.done, i + 1)
        else:
            engine.wait_ge(self.last_done, 1)

    def dve_begin(self, dve):
        dve.memset(self.eps[:], EPS).then_inc(self.eps_ready, 1)
        dve.wait_ge(self.loaded, 32)

    def dve_tile(self, dve, i):
        for h in range(2):
            last = self.steps.mark(dve.bn_stats(self.stats[:, i, h, :], self.g.x[:, i, h * 512:(h + 1) * 512]))
        dve.wait_ge(self.steps.sem, last)
        dve.bn_aggr(self.mv[:, i, :], self.stats[:, i, :, :]).then_inc(self.mv_ready, 1)
        dve.wait_ge(self.mv_ready, i + 1)
        dve.scalar_tensor_tensor(self.g.x[:, i, :], self.g.x[:, i, :], self.mv[:, i, 0:1], self.gamma[:],
                                 ALU.subtract, ALU.mult).then_inc(self.centred, 1)
        dve.wait_ge(self.std_ready, i + 1)
        dve.reciprocal(self.rstd[:, i:i + 1], self.std[:, i:i + 1]).then_inc(self.rstd_ready, 1)
        if i == NT - 1:
            dve.wait_ge(self.centred, i + 1)
            dve.wait_ge(self.rstd_ready, i + 1)
            dve.scalar_tensor_tensor(self.g.x[:, i, :], self.g.x[:, i, :], self.rstd[:, i:i + 1], self.beta[:],
                                     ALU.mult, ALU.add).then_inc(self.last_done, 1)

    def act_tile(self, act, i):
        act.wait_ge(self.eps_ready, 1)
        act.wait_ge(self.mv_ready, i + 1)
        act.activation(self.std[:, i:i + 1], self.mv[:, i, 1:2], ACT.Sqrt, bias=self.eps[:, 0:1]).then_inc(self.std_ready, 1)
        if i < NT - 1:
            act.wait_ge(self.centred, i + 1)
            act.wait_ge(self.rstd_ready, i + 1)
            act.activation(self.g.x[:, i, :], self.g.x[:, i, :], ACT.Copy, scale=self.rstd[:, i:i + 1]).then_inc(self.scaled, 1)

    def pool_tile(self, pool, i):
        if i < NT - 1:
            pool.wait_ge(self.loaded, 32)
            pool.wait_ge(self.scaled, i + 1)
            pool.tensor_tensor(self.g.x[:, i, :], self.g.x[:, i, :], self.beta[:], ALU.add).then_inc(self.done, 1)


def norm_from_dram(nc, name, g, acc_dram, norm, out=None):
    with Part(nc, name) as s:
        landed, stored = [s.sem(f"landed{i}") for i in range(NT)], s.sem("stored")
        block = s.stack.enter_context(nc.Block())

        @block.sync
        def _(sp):
            for i in range(NT):
                sp.dma_start(g.x[:, i, :], acc_dram[i * P:(i + 1) * P, :]).then_inc(landed[i], 16)
            if out is not None:
                for i in range(NT):
                    norm.wait_tile(sp, i)
                    sp.dma_start(out[i * P:(i + 1) * P, :], g.x[:, i, :]).then_inc(stored, 16)
                sp.wait_ge(stored, 16 * NT)

        @block.vector
        def _(dve):
            norm.dve_begin(dve)
            for i in range(NT):
                dve.wait_ge(landed[i], 16)
                norm.dve_tile(dve, i)

        @block.scalar
        def _(act):
            for i in range(NT):
                norm.act_tile(act, i)

        @block.gpsimd
        def _(pool):
            for i in range(NT):
                norm.pool_tile(pool, i)


def out_project_norm(nc, name, g, yT, gamma, beta):
    with Part(nc, name) as s:
        norm = Norm(s, g, gamma, beta)
        bank = [s.ps(f"bank{k}", [P, 512]) for k in range(4)]
        done, summed = s.sem("product_done"), s.sem("summed")
        block = s.stack.enter_context(nc.Block())

        @block.sync
        def _(sp):
            norm.load(sp)

        @block.tensor
        def _(pe):
            g.wait_wide(pe)
            for n in range(2 * NT):
                i, h = n // 2, n % 2
                if n >= 4:
                    pe.wait_ge(summed, n - 3)
                for k in range(KC):
                    mm = pe.matmul(bank[n % 4][:, :], yT[:, k, i * P:(i + 1) * P], g.wide[:, k, h * 512:(h + 1) * 512],
                                   start=(k == 0), stop=(k == KC - 1))
                mm.then_inc(done, 1)

        @block.vector
        def _(dve):
            norm.dve_begin(dve)
            for i in range(NT):
                for h in range(2):
                    n, cols = 2 * i + h, slice(h * 512, (h + 1) * 512)
                    dve.wait_ge(done, n + 1)
                    dve.scalar_tensor_tensor(g.x[:, i, cols], g.x[:, i, cols], ALPHA, bank[n % 4][:, :],
                                             ALU.mult, ALU.add).then_inc(summed, 1)
                dve.wait_ge(summed, 2 * i + 2)
                norm.dve_tile(dve, i)

        @block.scalar
        def _(act):
            for i in range(NT):
                norm.act_tile(act, i)

        @block.gpsimd
        def _(pool):
            for i in range(NT):
                norm.pool_tile(pool, i)


DS5, G, GS, NS = 512, 32, 16, 64
TAPS, CT = 31, 4
NJ = G * NS // P
ROUND = 1.5 * 2.0 ** 23
TURN_HI, TURN_LO = 6.28125, 6.283185307179586 - 6.28125
TWO_PI = 6.283185

COLS = {}
for _name, _n in (("b_in", 12), ("b_glu", 4), ("cv_b", 4), ("ln_g", 4), ("ln_b", 4), ("taps", (CT + 1) * TAPS),
                  ("lam_re", NJ), ("lam_im", NJ), ("log_dt", NJ), ("skip", CT)):
    COLS[_name] = (sum(b - a for a, b in COLS.values()), sum(b - a for a, b in COLS.values()) + _n)
NCOLS = COLS["skip"][1]


def even_layout(w):
    col = lambda v: np.ascontiguousarray(v.reshape(-1, P).T)
    state = lambda v: v.reshape(NJ, P).T
    parts = [col(w["ev_b_in"][0]), col(w["s5_b_glu"][0]), col(w["cv_b"][0]), col(w["cv_ln_g"][0]), col(w["cv_ln_b"][0]),
             w["cv_w"][0].reshape(TAPS, CT, P).transpose(2, 1, 0).reshape(P, CT * TAPS), np.zeros((P, TAPS), np.float32),
             state(w["s5_lam_re"][0]), state(w["s5_lam_im"][0]),
             state(np.repeat(w["s5_log_dt"][0][:, None], NS, 1)), col(w["s5_d"][0])]
    b = np.stack([w["s5_b_re"][0], w["s5_b_im"][0]])
    c = np.stack([w["s5_c_re"][0], w["s5_c_im"][0]])
    b = b.reshape(2, NJ, 2, NS, GS).transpose(2, 4, 1, 0, 3)
    c = c.reshape(2, NJ, 2, GS, NS).transpose(2, 4, 1, 0, 3)
    return np.ascontiguousarray(np.concatenate(parts, axis=1)), np.ascontiguousarray(b), np.ascontiguousarray(c)


def even_mixer(nc, g, w, yT):
    with Part(nc, "even") as outer:
        cols = outer.sb("cols", [P, NCOLS])
        col = {k: cols[:, a:b] for k, (a, b) in COLS.items()}
        u32 = outer.sb("u32", [32, NJ + 1, SEQ])
        hpad = outer.sb("hpad", [P, CT, TAPS - 1 + SEQ])
        uT = outer.sb("uT", [P, CT, SEQ])
        bB = outer.sb("bB", [32, NJ + 1, 2, P])
        cC = outer.sb("cC", [P, NJ, 2, 32])
        even_in_project(nc, g, w, cols, col, u32, uT, hpad, bB, cC)
        s5_and_conv(nc, g, col, u32, hpad, bB, cC, yT)
        even_finish(nc, g, w, col, u32, uT, yT)


def even_in_project(nc, g, w, cols, col, u32, uT, hpad, bB, cC):
    with Part(nc, "evin") as s:
        gates_in = s.sb("win", [P, KC, DS5])
        win = [g.wide[:, :, 0:DS5], g.wide[:, :, DS5:2 * DS5], gates_in[:, :, :]]
        cols_loaded, small_loaded = s.sem("cols_loaded"), s.sem("small_loaded")
        sig = s.sb("sig", [P, 2, SEQ])
        bank = [s.ps(f"bank{k}", [P, 512]) for k in range(8)]
        win_landed = [s.sem(f"win_landed{k}") for k in range(3)]
        xt_done, xt_a, xt_v = s.sem("xt_done"), s.sem("xt_copied_act"), s.sem("xt_copied_dve")
        done, u_ready, u_moved = s.sem("product_done"), s.sem("u_ready"), s.sem("u_moved")
        sig_ready, h_ready, cleared = s.sem("sig_ready"), s.sem("h_ready"), s.sem("cleared")
        block = s.stack.enter_context(nc.Block())
        order = [0, 1, 2, 3] + [f for t in range(CT) for f in (8 + t, 4 + t)]

        @block.sync
        def _(sp):
            sp.dma_start(g.const_sb[:, 0:P], w["const_table"][:, 0:P]).then_inc(g.ident_loaded, 16)
            for i in range(NT):
                sp.dma_start(g.x[:, i, :], w["x"][0, i * P:(i + 1) * P, :]).then_inc(g.x_loaded, 16)
            src = w["ev_w_in"][0].rearrange("(p c) f -> p c f", c=KC)
            for k in (0, 2, 1):
                sp.dma_start(win[k], src[:, :, k * 512:(k + 1) * 512]).then_inc(win_landed[k], 16)
                if k == 0:
                    sp.dma_start(cols[:], w["columns"]).then_inc(cols_loaded, 16)
            sp.dma_start(g.const_sb[:, P:], w["const_table"][:, P:]).then_inc(g.consts_loaded, 16)
            sp.wait_ge(cleared, 2)
            for q in range(2):
                sp.dma_start(bB[16 * q:16 * q + 16, 0:NJ, :, NS * q:NS * q + NS], w["b_swapped"][q]).then_inc(small_loaded, 16)
                sp.dma_start(cC[64 * q:64 * q + 64, :, :, GS * q:GS * q + GS], w["c_swapped"][q]).then_inc(small_loaded, 16)
            sp.wait_ge(u_ready, CT)
            for q in range(4):
                sp.dma_start(u32[:, 0:NJ, :].rearrange("h (t q) l -> h t q l", q=4)[:, :, q, :], uT[32 * q:32 * q + 32, :, :]).then_inc(u_moved, 16)
            sp.wait_ge(u_moved, 64)
            sp.wait_ge(small_loaded, 64)
            sp.wait_ge(g.consts_loaded, 16)

        @block.gpsimd
        def _(pool):
            pool.memset(bB[:], 0.0).then_inc(cleared, 1)
            pool.memset(cC[:], 0.0).then_inc(cleared, 1)
            pool.memset(hpad[:, :, 0:TAPS - 1], 0.0)
            pool.memset(u32[:, NJ, :], 0.0)

        @block.tensor
        def _(pe):
            pe.wait_ge(g.ident_loaded, 16)
            pe.wait_ge(g.x_loaded, 64)
            emit_transposes(pe, g.x, g.c["ident"], bank[0:2], xt_done, (xt_a, xt_v))
            pe.wait_ge(xt_a, 4)
            pe.wait_ge(xt_v, 4)
            for n, f in enumerate(order):
                if n in (0, 4, 5):
                    pe.wait_ge(win_landed[f // 4], 16)
                if 6 <= n < 10:
                    pe.wait_ge(u_ready, n - 5)
                elif n >= 10:
                    pe.wait_ge(h_ready, (n - 8) // 2)
                for k in range(KC):
                    mm = pe.matmul(bank[2 + n % 6][:, :], win[f // 4][:, k, f % 4 * P:(f % 4 + 1) * P], g.xT[:, k, :],
                                   start=(k == 0), stop=(k == KC - 1))
                mm.then_inc(done, 1)

        @block.scalar
        def _(act):
            for k in range(0, KC, 2):
                act.wait_ge(xt_done, k + 1)
                act.activation(g.xT[:, k, :], bank[0][:, :], ACT.Copy).then_inc(xt_a, 1)
            act.wait_ge(cols_loaded, 16)
            for n, f in enumerate(order):
                if n < 4:
                    act.wait_ge(done, n + 1)
                    act.activation(uT[:, n, :], bank[2 + n][:, :], ACT.Identity, bias=col["b_in"][:, f:f + 1]).then_inc(u_ready, 1)
                elif n % 2 == 0:
                    t = (n - 4) // 2
                    act.wait_ge(done, n + 1)
                    if t >= 2:
                        act.wait_ge(h_ready, t - 1)
                    act.activation(sig[:, t % 2, :], bank[2 + n % 6][:, :], ACT.Sigmoid, bias=col["b_in"][:, f:f + 1]).then_inc(sig_ready, 1)

        @block.vector
        def _(dve):
            for k in range(1, KC, 2):
                dve.wait_ge(xt_done, k + 1)
                dve.tensor_copy(g.xT[:, k, :], bank[1][:, :]).then_inc(xt_v, 1)
            dve.wait_ge(cols_loaded, 16)
            for t in range(CT):
                n = 5 + 2 * t
                dve.wait_ge(done, n + 1)
                dve.wait_ge(sig_ready, t + 1)
                dve.scalar_tensor_tensor(hpad[:, t, TAPS - 1:], bank[2 + n % 6][:, :], col["b_in"][:, 4 + t:5 + t],
                                         sig[:, t % 2, :], ALU.add, ALU.mult).then_inc(h_ready, 1)


def s5_and_conv(nc, g, col, u32, hpad, bB, cC, yT):
    with Part(nc, "s5") as s:
        names = ("dt", "ld", "th", "km", "k", "r", "sn", "sh", "cs", "are", "aim", "den", "rden", "fre",
                 "fim", "t1", "t2", "t3", "t4")
        v = {n: s.sb(n, [P, NJ]) for n in names}
        decay, rho = s.sb("decay", [P, NJ]), s.sb("rho", [P, NJ + 1])
        cp = s.sb("cp", [P, NJ + 1, 3, 32])
        ct = s.sb("ct", [P, 2, NJ, 32])
        bst = [s.sb(f"bst{p}", [32, 2 * P]) for p in range(2)]
        cst = [s.sb(f"cst{p}", [P, 3 * 32]) for p in range(2)]
        turns, kround, frac = s.sb("turns", [P, SEQ]), s.sb("kround", [P, SEQ]), s.sb("frac", [P, SEQ])
        sinT = [s.sb(f"sinT{p}", [P, SEQ]) for p in range(2)]
        cosT = [s.sb(f"cosT{p}", [P, SEQ]) for p in range(2)]
        half = s.sb("half", [P, SEQ])
        prod, back = (g.wide[:, k:k + 2, :].rearrange("p c (h l) -> p (c h) l", l=SEQ) for k in (0, 2))
        vin = s.sb("vin", [P, 2, SEQ])
        z = s.sb("z", [P, 2, SEQ])
        diag = s.sb("diag", [P, 2, 8, P])
        bu = [[s.ps(f"bu{p}{q}", [P, 512]) for q in range(2)] for p in range(2)]
        by, bc = s.ps("by", [P, 512]), s.ps("bc", [P, 512])
        dve_steps = Chain(s.sem("dve_steps"))
        exps_ready, sines_ready, rho_ready, cp_ready = s.sem("exps_ready"), s.sem("sines_ready"), s.sem("rho_ready"), s.sem("cp_ready")
        ld_ready, statics = s.sem("ld_ready"), s.sem("statics_copied")
        table_steps, frac_ready, sin_ready, half_ready, square_ready, cos_ready = (
            s.sem("table_steps"), s.sem("frac_ready"), s.sem("sin_ready"), s.sem("half_ready"), s.sem("square_ready"), s.sem("cos_ready"))
        bu_done, prod_re, prod_im = s.sem("bu_done"), s.sem("prod_re_ready"), s.sem("prod_im_ready")
        vin_re, vin_im, z_re, z_im = s.sem("vin_re_ready"), s.sem("vin_im_ready"), s.sem("z_re_ready"), s.sem("z_im_ready")
        back_v, back_p, y_done, y_copied = s.sem("back_dve"), s.sem("back_pool"), s.sem("y_done"), s.sem("y_copied")
        diag_ready, conv_done, conv_copied = s.sem("diag_ready"), s.sem("conv_quarters_done"), s.sem("conv_copied")
        pads, copied = s.sem("pads_cleared"), s.sem("copies")
        block = s.stack.enter_context(nc.Block())
        taps = col["taps"].rearrange("p (t n) -> p t n", n=TAPS)

        def steps(eng):
            with eng.Fori(0, CT) as t:
                for q in range(4):
                    yield 4 * t + q, t, q, q % 2

        def taps_of(q):
            return range(8 * q, min(8 * q + 8, TAPS))

        @block.scalar
        def _(act):
            for counter in (conv_copied, y_copied,):
                act.sem_inc(counter, 1)
            act.activation(v["dt"][:], col["log_dt"], ACT.Exp).then_inc(exps_ready, 1)
            act.wait_ge(ld_ready, 1)
            act.activation(decay[:], v["ld"][:], ACT.Exp).then_inc(exps_ready, 1)
            act.wait_ge(rho_ready, 1)
            act.activation(v["sn"][:], rho[:, 0:NJ], ACT.Sin, scale=TWO_PI).then_inc(sines_ready, 1)
            act.activation(v["sh"][:], rho[:, 0:NJ], ACT.Sin, scale=TWO_PI / 2).then_inc(sines_ready, 1)

            def table(j, p):
                act.wait_ge(frac_ready, j + 1)
                if p is not None:
                    act.wait_ge(back_v, j - 1 + 1)
                    act.wait_ge(back_p, j - 1 + 1)
                act.activation(sinT[p or 0][:], frac[:], ACT.Sin, scale=-TWO_PI).then_inc(sin_ready, 1)
                if p is not None:
                    act.wait_ge(cos_ready, j)
                act.activation(half[:], frac[:], ACT.Sin, scale=-TWO_PI / 2).then_inc(half_ready, 1)
                act.wait_ge(half_ready, j + 1)
                act.activation(half[:], half[:], ACT.Square).then_inc(square_ready, 1)

            def diagonals(t, q, p, j=None):
                if j is not None:
                    act.wait_ge(conv_done, j - 1 + 1)
                for n in taps_of(q):
                    last = act.activation(diag[:, p, n % 8, :], g.c["ident"], ACT.Copy, scale=taps[:, ds(t, 1), n])
                last.then_inc(diag_ready, 1)

            table(0, None)
            diagonals(0, 0, 0)
            for j, t, q, p in steps(act):
                table(j + 1, 1 - p)
                diagonals(t if q < 3 else t + 1, (q + 1) % 4, 1 - p, j + 1)
                act.wait_ge(y_done, j + 1 + 1)
                act.activation(u32[:, ds(j, 1), :].rearrange("h o l -> h (o l)"), by[0:32, :], ACT.Copy).then_inc(y_copied, 1)
                if q == 3:
                    act.wait_ge(conv_done, j + 1 + 1)
                    act.activation(yT[:, ds(CT + t, 1), :].rearrange("p o l -> p (o l)"), bc[:, :], ACT.Identity,
                                   bias=col["cv_b"][:, ds(t, 1)]).then_inc(conv_copied, 1)

        @block.gpsimd
        def _(pool):
            for counter in (back_p, vin_im,):
                pool.sem_inc(counter, 1)
            def statics_of(j, p, wait):
                if wait:
                    pool.wait_ge(y_done, j - 1 + 1)
                pool.tensor_copy(bst[p][:], bB[:, ds(j, 1)].rearrange("h o k n -> h (o k n)"))
                pool.tensor_copy(cst[p][:], cp[:, ds(j, 1)].rearrange("p o k n -> p (o k n)")).then_inc(statics, 1)

            pool.memset(rho[:, NJ:NJ + 1], 0.0).then_inc(pads, 1)
            pool.memset(cp[:, NJ], 0.0).then_inc(pads, 1)
            pool.wait_ge(pads, 2)
            pool.wait_ge(cp_ready, 1)
            statics_of(0, 0, False)
            for j, t, q, p in steps(pool):
                pool.wait_ge(prod_re, j + 1)
                pool.wait_ge(z_im, j + 1)
                pool.tensor_tensor(vin[:, 0, :], prod[:, 0, :], prod[:, 1, :], ALU.add).then_inc(vin_re, 1)
                pool.wait_ge(prod_im, j + 1 + 1)
                pool.tensor_tensor(vin[:, 1, :], prod[:, 2, :], prod[:, 3, :], ALU.subtract).then_inc(vin_im, 1)
                statics_of(j + 1, 1 - p, True)
                pool.wait_ge(z_re, j + 1)
                pool.wait_ge(cos_ready, j + 1)
                pool.wait_ge(sin_ready, j + 1)
                pool.wait_ge(y_done, j + 1)
                pool.tensor_tensor(back[:, 0, :], z[:, 0, :], cosT[p][:], ALU.mult)
                pool.tensor_tensor(back[:, 2, :], z[:, 0, :], sinT[p][:], ALU.mult).then_inc(back_p, 1)

        @block.tensor
        def _(pe):
            for counter in (conv_done, y_done,):
                pe.sem_inc(counter, 1)
            def inputs(j, p):
                pe.wait_ge(statics, j + 1)
                for k in range(2):
                    mm = pe.matmul(bu[p][k][:, :], bst[p][:, k * P:(k + 1) * P],
                                   u32[:, ds(j, 1), :].rearrange("h o l -> h (o l)"), start=True, stop=True)
                mm.then_inc(bu_done, 1)

            inputs(0, 0)
            for j, t, q, p in steps(pe):
                pe.wait_ge(prod_im, j + 1)
                inputs(j + 1, 1 - p)
                pe.wait_ge(diag_ready, j + 1)
                if q == 0:
                    pe.wait_ge(conv_copied, t + 1)
                for n in taps_of(q):
                    mm = pe.matmul(bc[:, :], diag[:, p, n % 8, :], hpad[:, ds(t, 1), n:n + SEQ].rearrange("p o l -> p (o l)"),
                                   start=(n == 0), stop=(n == TAPS - 1))
                mm.then_inc(conv_done, 1)
                pe.wait_ge(back_v, j + 1 + 1)
                pe.wait_ge(back_p, j + 1 + 1)
                pe.wait_ge(y_copied, j + 1)
                for k, sign in enumerate((0, 1, 2, 2)):
                    mm = pe.matmul(by[0:32, :], cst[p][:, sign * 32:sign * 32 + 32], back[:, k, :], start=(k == 0), stop=(k == 3))
                mm.then_inc(y_done, 1)

        @block.vector
        def _(dve):
            for counter in (back_v, z_im, prod_im,):
                dve.sem_inc(counter, 1)
            link = lambda ins: dve_steps.link(dve, ins)
            dve.wait_ge(exps_ready, 1)
            dve.tensor_tensor(v["ld"][:], col["lam_re"], v["dt"][:], ALU.mult).then_inc(ld_ready, 1)
            link(dve.tensor_tensor(v["th"][:], col["lam_im"], v["dt"][:], ALU.mult))
            link(dve.tensor_scalar(v["km"][:], v["th"][:], 1.0 / 6.283185307179586, ROUND, ALU.mult, ALU.add))
            link(dve.tensor_scalar(v["k"][:], v["km"][:], -ROUND, None, ALU.add))
            link(dve.scalar_tensor_tensor(v["r"][:], v["k"][:], -TURN_HI, v["th"][:], ALU.mult, ALU.add))
            link(dve.scalar_tensor_tensor(v["r"][:], v["k"][:], -TURN_LO, v["r"][:], ALU.mult, ALU.add))
            link(dve.tensor_scalar(v["r"][:], v["r"][:], 1.0 / 6.283185307179586, 0.5, ALU.mult, ALU.min))
            dve.tensor_scalar(rho[:, 0:NJ], v["r"][:], -0.5, None, ALU.max).then_inc(rho_ready, 1)
            dve.wait_ge(exps_ready, 2)
            dve.wait_ge(sines_ready, 2)
            link(dve.tensor_tensor(v["cs"][:], v["sh"][:], v["sh"][:], ALU.mult))
            link(dve.tensor_scalar(v["cs"][:], v["cs"][:], -2.0, 1.0, ALU.mult, ALU.add))
            link(dve.tensor_tensor(v["are"][:], decay[:], v["cs"][:], ALU.mult))
            link(dve.tensor_tensor(v["aim"][:], decay[:], v["sn"][:], ALU.mult))
            link(dve.tensor_scalar(v["are"][:], v["are"][:], -1.0, None, ALU.add))
            link(dve.tensor_tensor(v["t1"][:], col["lam_re"], col["lam_re"], ALU.mult))
            link(dve.tensor_tensor(v["t2"][:], col["lam_im"], col["lam_im"], ALU.mult))
            link(dve.tensor_tensor(v["den"][:], v["t1"][:], v["t2"][:], ALU.add))
            link(dve.reciprocal(v["rden"][:], v["den"][:]))
            link(dve.tensor_tensor(v["t1"][:], v["are"][:], col["lam_re"], ALU.mult))
            link(dve.tensor_tensor(v["t2"][:], v["aim"][:], col["lam_im"], ALU.mult))
            link(dve.tensor_tensor(v["t1"][:], v["t1"][:], v["t2"][:], ALU.add))
            link(dve.tensor_tensor(v["fre"][:], v["t1"][:], v["rden"][:], ALU.mult))
            link(dve.tensor_tensor(v["t3"][:], v["aim"][:], col["lam_re"], ALU.mult))
            link(dve.tensor_tensor(v["t4"][:], v["are"][:], col["lam_im"], ALU.mult))
            link(dve.tensor_tensor(v["t3"][:], v["t3"][:], v["t4"][:], ALU.subtract))
            link(dve.tensor_tensor(v["fim"][:], v["t3"][:], v["rden"][:], ALU.mult))
            fre, fim = (f[:].unsqueeze(2).to_broadcast([P, NJ, 32]) for f in (v["fre"], v["fim"]))
            link(dve.tensor_tensor(ct[:, 0], cC[:, :, 0, :], fre, ALU.mult))
            link(dve.tensor_tensor(ct[:, 1], cC[:, :, 1, :], fim, ALU.mult))
            link(dve.tensor_tensor(cp[:, 0:NJ, 0, :], ct[:, 0], ct[:, 1], ALU.subtract))
            link(dve.tensor_scalar(cp[:, 0:NJ, 1, :], cp[:, 0:NJ, 0, :], -1.0, None, ALU.mult))
            link(dve.tensor_tensor(ct[:, 0], cC[:, :, 0, :], fim, ALU.mult))
            link(dve.tensor_tensor(ct[:, 1], cC[:, :, 1, :], fre, ALU.mult))
            link(dve.tensor_tensor(ct[:, 0], ct[:, 0], ct[:, 1], ALU.add))
            dve.tensor_scalar(cp[:, 0:NJ, 2, :], ct[:, 0], -1.0, None, ALU.mult).then_inc(cp_ready, 1)
            dve.wait_ge(pads, 2)
            dve.wait_ge(rho_ready, 1)

            def table(j, wait):
                if wait:
                    dve.wait_ge(frac_ready, j)
                r = rho[:, ds(j, 1)]
                dve.tensor_scalar(turns[:], g.c["time"], r, None, ALU.mult).then_inc(table_steps, 1)
                dve.tensor_scalar(kround[:], g.c["time"], r, ROUND, ALU.mult, ALU.add).then_inc(table_steps, 1)
                dve.wait_ge(table_steps, 2 * j + 2)
                if wait:
                    dve.wait_ge(square_ready, j)
                dve.scalar_tensor_tensor(frac[:], kround[:], -ROUND, turns[:], ALU.add, ALU.subtract).then_inc(frac_ready, 1)

            def cosine(j, p, wait):
                dve.wait_ge(square_ready, j + 1)
                if wait:
                    dve.wait_ge(back_p, j - 1 + 1)
                dve.tensor_scalar(cosT[p][:], half[:], -2.0, 1.0, ALU.mult, ALU.add).then_inc(cos_ready, 1)

            table(0, False)
            cosine(0, 0, False)
            for j, t, q, p in steps(dve):
                dve.wait_ge(bu_done, j + 1)
                dve.wait_ge(cos_ready, j + 1)
                dve.wait_ge(sin_ready, j + 1)
                dve.wait_ge(vin_im, j + 1)
                dve.tensor_tensor(prod[:, 0, :], bu[p][0][:, :], cosT[p][:], ALU.mult)
                dve.tensor_tensor(prod[:, 1, :], bu[p][1][:, :], sinT[p][:], ALU.mult).then_inc(prod_re, 1)
                dve.tensor_tensor(prod[:, 2, :], bu[p][1][:, :], cosT[p][:], ALU.mult)
                dve.tensor_tensor(prod[:, 3, :], bu[p][0][:, :], sinT[p][:], ALU.mult).then_inc(prod_im, 1)
                table(j + 1, True)
                d = decay[:, ds(j, 1)].to_broadcast([P, SEQ])
                dve.wait_ge(vin_re, j + 1)
                dve.wait_ge(back_p, j + 1)
                dve.tensor_tensor_scan(z[:, 0, :], d, vin[:, 0, :], 0.0, ALU.mult, ALU.add).then_inc(z_re, 1)
                dve.wait_ge(vin_im, j + 1 + 1)
                dve.wait_ge(back_v, j + 1)
                dve.tensor_tensor_scan(z[:, 1, :], d, vin[:, 1, :], 0.0, ALU.mult, ALU.add).then_inc(z_im, 1)
                dve.wait_ge(z_im, j + 1 + 1)
                dve.wait_ge(y_done, j + 1)
                dve.tensor_tensor(back[:, 1, :], z[:, 1, :], sinT[p][:], ALU.mult)
                dve.tensor_tensor(back[:, 3, :], z[:, 1, :], cosT[p][:], ALU.mult).then_inc(back_v, 1)
                cosine(j + 1, 1 - p, True)


def even_finish(nc, g, w, col, u32, uT, yT):
    with Part(nc, "evfin") as s:
        wglu = s.sb("wglu", [P, CT, DS5])
        gl, sg, cen = s.sb("gl", [P, CT, SEQ]), s.sb("sg", [P, 2, SEQ]), s.sb("cen", [P, CT, SEQ])
        sq, std, rstd, eps = s.sb("sq", [P, CT, SEQ]), s.sb("std", [P, SEQ]), s.sb("rstd", [P, SEQ]), s.sb("eps", [P, 1])
        bank = [s.ps(f"bank{k}", [P, 512]) for k in range(4)]
        bM, bV = s.ps("bM", [P, 512]), s.ps("bV", [P, 512])
        wglu_landed, y_moved = s.sem("wglu_landed"), s.sem("y_moved")
        y_ready, gl_ready, glu_done, sg_ready, ya_ready = s.sem("y_ready"), s.sem("gl_ready"), s.sem("glu_done"), s.sem("sg_ready"), s.sem("ya_ready")
        mean_done, cen_ready, sq_ready, var_done, std_ready, rstd_ready, norm_ready = (
            s.sem("mean_done"), s.sem("cen_ready"), s.sem("sq_ready"), s.sem("var_done"), s.sem("std_ready"), s.sem("rstd_ready"), s.sem("norm_ready"))
        eps_ready = s.sem("eps_ready")
        block = s.stack.enter_context(nc.Block())

        @block.sync
        def _(sp):
            for q in range(4):
                sp.dma_start(yT[32 * q:32 * q + 32, 0:CT, :], u32[:, 0:NJ, :].rearrange("h (t q) l -> h t q l", q=4)[:, :, q, :]).then_inc(y_moved, 16)
            sp.dma_start(wglu[:], w["s5_w_glu"][0].rearrange("(c p) f -> p c f", p=P)).then_inc(wglu_landed, 16)
            g.load_wide(sp, w["ev_w_out"][0].rearrange("(c p) n -> p c n", p=P))

        @block.tensor
        def _(pe):
            for k in range(CT):
                mm = pe.matmul(bM[:, :], g.c["ones"], yT[:, CT + k, :], start=(k == 0), stop=(k == CT - 1))
            mm.then_inc(mean_done, 1)
            pe.wait_ge(wglu_landed, 16)
            pe.wait_ge(gl_ready, CT)
            for f in range(CT):
                if f == 1:
                    pe.wait_ge(sq_ready, CT)
                    for k in range(CT):
                        mm = pe.matmul(bV[:, :], g.c["ones"], sq[:, k, :], start=(k == 0), stop=(k == CT - 1))
                    mm.then_inc(var_done, 1)
                for k in range(CT):
                    mm = pe.matmul(bank[f][:, :], wglu[:, k, f * P:(f + 1) * P], gl[:, k, :], start=(k == 0), stop=(k == CT - 1))
                mm.then_inc(glu_done, 1)

        @block.vector
        def _(dve):
            dve.memset(eps[:], EPS).then_inc(eps_ready, 1)
            dve.wait_ge(y_moved, 64)
            for k in range(CT):
                dve.scalar_tensor_tensor(yT[:, k, :], uT[:, k, :], col["skip"][:, k:k + 1], yT[:, k, :], ALU.mult, ALU.add).then_inc(y_ready, 1)
            dve.wait_ge(mean_done, 1)
            for k in range(CT):
                dve.scalar_tensor_tensor(cen[:, k, :], bM[:, :], -1.0 / DS5, yT[:, CT + k, :], ALU.mult, ALU.add).then_inc(cen_ready, 1)
            dve.wait_ge(std_ready, 1)
            dve.reciprocal(rstd[:], std[:]).then_inc(rstd_ready, 1)
            dve.wait_ge(rstd_ready, 1)
            dve.wait_ge(cen_ready, CT)
            dve.wait_ge(sq_ready, CT)
            for k in range(CT):
                dve.tensor_tensor(cen[:, k, :], cen[:, k, :], rstd[:], ALU.mult).then_inc(norm_ready, 1)
            for f in range(CT):
                dve.wait_ge(sg_ready, f + 1)
                dve.tensor_tensor(yT[:, f, :], gl[:, f, :], sg[:, f % 2, :], ALU.mult).then_inc(ya_ready, 1)

        @block.scalar
        def _(act):
            for k in range(CT):
                act.wait_ge(y_ready, k + 1)
                act.activation(gl[:, k, :], yT[:, k, :], ACT.Gelu_apprx_tanh).then_inc(gl_ready, 1)
            for k in range(CT):
                act.wait_ge(cen_ready, k + 1)
                act.activation(sq[:, k, :], cen[:, k, :], ACT.Square).then_inc(sq_ready, 1)
            act.wait_ge(var_done, 1)
            act.wait_ge(eps_ready, 1)
            act.activation(std[:], bV[:, :], ACT.Sqrt, bias=eps[:, 0:1], scale=1.0 / DS5).then_inc(std_ready, 1)
            for f in range(CT):
                act.wait_ge(glu_done, f + 1)
                if f >= 2:
                    act.wait_ge(ya_ready, f - 1)
                act.activation(sg[:, f % 2, :], bank[f][:, :], ACT.Sigmoid, bias=col["b_glu"][:, f:f + 1]).then_inc(sg_ready, 1)
            for k in range(CT):
                act.wait_ge(norm_ready, k + 1)
                act.activation(yT[:, CT + k, :], cen[:, k, :], ACT.Silu, scale=col["ln_g"][:, k:k + 1], bias=col["ln_b"][:, k:k + 1])


NU, NP2 = 4, 2
QCOL, KC_COL, VC_COL, KS_COL, VS_COL, KW_COL, VW_COL, GL_COL, ODD_IN = 0, 1024, 1280, 1536, 1792, 2048, 2304, 2560, 2608
SCALE = HD ** -0.5


def odd_layout(w):
    heads = lambda m: np.moveaxis(m.reshape(m.shape[0], NP2, 2, NU, HD), 2, 3).reshape(m.shape[0], NH * HD)
    win = np.concatenate([heads(w["od_w_in"][0][:, :KC_COL]), w["od_w_in"][0][:, KC_COL:]], axis=1)
    wout = np.ascontiguousarray(heads(np.ascontiguousarray(w["od_w_out"][0].T)).T)
    tables = np.concatenate([np.tile(w[k][0].T, (2, 1)) for k in ("cmp_pe_k", "cmp_pe_v")], axis=1)
    return np.ascontiguousarray(win), wout, np.ascontiguousarray(tables)


def odd_mixer(nc, g, w, yT):
    with Part(nc, "odd") as outer:
        a = Names()
        a.qT = outer.sb("qT", [P, 2 * NU, SEQ])
        a.kT = {k: outer.sb(k + "T", [P, NP2, SEQ]) for k in ("kc", "ks", "kw", "vc")}
        a.v = outer.sb("v", [P, NT, 2, 2 * P])
        a.gates = outer.sb("gates", [P, NT, 3 * NH])
        a.kcmp = outer.sb("kcmp", [P, NP2, 32])
        a.vcmp = outer.sb("vcmp", [NCMP, NP2, P])
        odd_in_project(nc, g, w, a)
        compress(nc, g, w, a)
        attention(nc, g, w, a, yT)


def odd_in_project(nc, g, w, a):
    with Part(nc, "oddin") as s:
        win = s.sb("win", [P, KC, ODD_IN - KC_COL])
        raw, turned = s.sb("raw", [P, 2, SEQ]), s.sb("turned", [P, 2, 2, SEQ])
        bank = [s.ps(f"bank{k}", [P, 512]) for k in range(8)]
        landed = [s.sem(f"landed{k}") for k in range(2)]
        xt_done, xt_a, xt_v = s.sem("xt_done"), s.sem("xt_copied_act"), s.sem("xt_copied_dve")
        done, raw_ready, rot_done, turned_ready, roped = s.sem("product_done"), s.sem("raw_ready"), s.sem("rot_done"), s.sem("turned_ready"), s.sem("roped")
        v_done, v_ready, vc_ready = s.sem("v_done"), s.sem("v_ready"), s.sem("vc_ready")
        block = s.stack.enter_context(nc.Block())
        roped_tiles = [(g.wide[:, :, P * u:P * u + P], a.qT[:, u, :]) for u in range(2 * NU)]
        for k, at in (("kc", KC_COL), ("ks", KS_COL), ("kw", KW_COL)):
            roped_tiles += [(win[:, :, at - KC_COL + P * u:at - KC_COL + P * u + P], a.kT[k][:, u, :]) for u in range(NP2)]
        NR = len(roped_tiles)

        @block.sync
        def _(sp):
            src = w["od_w_in_heads"].rearrange("(p c) f -> p c f", c=KC)
            for k, (lo, hi) in enumerate(((KC_COL, KS_COL), (KS_COL, ODD_IN))):
                sp.dma_start(win[:, :, lo - KC_COL:hi - KC_COL], src[:, :, lo:hi]).then_inc(landed[k], 16)

        @block.tensor
        def _(pe):
            emit_transposes(pe, g.x, g.c["ident"], bank[0:2], xt_done, (xt_a, xt_v))
            g.wait_wide(pe)
            pe.wait_ge(xt_a, 4)
            pe.wait_ge(xt_v, 4)

            def rotate(n):
                pe.wait_ge(raw_ready, n + 1)
                if n >= 2:
                    pe.wait_ge(turned_ready, n - 1)
                pe.matmul(bank[4 + n % 2][:, :], g.c["rot"], raw[:, n % 2, :], start=True, stop=True).then_inc(rot_done, 1)

            for n in range(NR):
                cols, _ = roped_tiles[n]
                if n >= 2 * NU:
                    pe.wait_ge(landed[0 if n < 2 * NU + NP2 else 1], 16)
                if n >= 2:
                    pe.wait_ge(raw_ready, n - 1)
                for k in range(KC):
                    mm = pe.matmul(bank[2 + n % 2][:, :], cols[:, k], g.xT[:, k, :], start=(k == 0), stop=(k == KC - 1))
                mm.then_inc(done, 1)
                if n >= 1:
                    rotate(n - 1)
            rotate(NR - 1)
            for u in range(NP2):
                for k in range(KC):
                    mm = pe.matmul(bank[6 + u][:, :], win[:, k, VC_COL - KC_COL + P * u:VC_COL - KC_COL + P * u + P], g.xT[:, k, :],
                                   start=(k == 0), stop=(k == KC - 1))
                mm.then_inc(v_done, 1)
            for i in range(NT):
                if i >= 2:
                    pe.wait_ge(v_ready, i - 1)
                for b, col in enumerate((VS_COL, VW_COL)):
                    for k in range(KC):
                        mm = pe.matmul(bank[i % 2][:, b * 256:(b + 1) * 256], g.xT[:, k, i * P:(i + 1) * P],
                                       win[:, k, col - KC_COL:col - KC_COL + 256], start=(k == 0), stop=(k == KC - 1))
                mm.then_inc(v_done, 1)
            pe.wait_ge(raw_ready, NR)
            for i in range(NT):
                for k in range(KC):
                    mm = pe.matmul(bank[2][:, i * 48:(i + 1) * 48], g.xT[:, k, i * P:(i + 1) * P], win[:, k, GL_COL - KC_COL:ODD_IN - KC_COL],
                                   start=(k == 0), stop=(k == KC - 1))
            mm.then_inc(v_done, 1)

        @block.scalar
        def _(act):
            for k in range(0, KC, 2):
                act.wait_ge(xt_done, k + 1)
                act.activation(g.xT[:, k, :], bank[0][:, :], ACT.Copy).then_inc(xt_a, 1)
            for n in range(NR):
                act.wait_ge(done, n + 1)
                if n >= 2:
                    act.wait_ge(turned_ready, n - 1)
                act.activation(raw[:, n % 2, :], bank[2 + n % 2][:, :], ACT.Copy).then_inc(raw_ready, 1)
            for u in range(NP2):
                act.wait_ge(v_done, u + 1)
                act.activation(a.kT["vc"][:, u, :], bank[6 + u][:, :], ACT.Copy).then_inc(vc_ready, 1)
            for i in range(NT):
                act.wait_ge(v_done, NP2 + i + 1)
                act.activation(a.v[:, i].rearrange("p b d -> p (b d)"), bank[i % 2][:, :], ACT.Copy).then_inc(v_ready, 1)
            act.wait_ge(v_done, NP2 + NT + 1)
            act.activation(a.gates[:].rearrange("p i h -> p (i h)"), bank[2][:, 0:NT * 48], ACT.Sigmoid).then_inc(vc_ready, 1)

        @block.vector
        def _(dve):
            for k in range(1, KC, 2):
                dve.wait_ge(xt_done, k + 1)
                dve.tensor_copy(g.xT[:, k, :], bank[1][:, :]).then_inc(xt_v, 1)
            for n in range(NR):
                dve.wait_ge(raw_ready, n + 1)
                if n >= 2:
                    dve.wait_ge(roped, n - 1)
                dve.tensor_tensor(turned[:, n % 2, 0, :], raw[:, n % 2, :], g.c["cos"], ALU.mult)
                dve.wait_ge(rot_done, n + 1)
                dve.tensor_tensor(turned[:, n % 2, 1, :], bank[4 + n % 2][:, :], g.c["sin"], ALU.mult).then_inc(turned_ready, 1)

        @block.gpsimd
        def _(pool):
            for n in range(NR):
                pool.wait_ge(turned_ready, n + 1)
                pool.tensor_tensor(roped_tiles[n][1], turned[:, n % 2, 0, :], turned[:, n % 2, 1, :], ALU.add).then_inc(roped, 1)


def compress(nc, g, w, a):
    with Part(nc, "cmp") as s:
        cw = [s.sb(f"cw{k}", [P, CLEN, HD]) for k in range(2)]
        pe_cols = s.sb("pe_cols", [P, 2 * CLEN])
        shift = s.sb("shift", [P, 2])
        vT = s.sb("vT", [P, NP2, 32])
        bank = [s.ps(f"bank{k}", [P, 512]) for k in range(5)]
        landed, pe_landed = [s.sem(f"landed{k}") for k in range(2)], s.sem("pe_landed")
        shifts_done, shift_ready, done, ready, vt_done, v_ready = (
            s.sem("shifts_done"), s.sem("shift_ready"), s.sem("products_done"), s.sem("ready"), s.sem("vt_done"), s.sem("v_ready"))
        block = s.stack.enter_context(nc.Block())

        @block.sync
        def _(sp):
            sp.dma_start(pe_cols[:], w["pe_columns"]).then_inc(pe_landed, 16)
            for k, name in enumerate(("cmp_w_k", "cmp_w_v")):
                for half in range(2):
                    sp.dma_start(cw[k][64 * half:64 * half + 64], w[name][0].rearrange("l d e -> d l e")).then_inc(landed[k], 16)

        @block.tensor
        def _(pe):
            pe.wait_ge(pe_landed, 16)
            for k, name in enumerate(("kc", "vc")):
                pe.wait_ge(landed[k], 32)
                for half in range(2):
                    rows = slice(64 * half, 64 * half + 64)
                    for n in range(CLEN):
                        mm = pe.matmul(bank[4][rows, k:k + 1], cw[k][rows, n, :], pe_cols[rows, k * CLEN + n:k * CLEN + n + 1],
                                       start=(n == 0), stop=(n == CLEN - 1))
                    for n in range(CLEN):
                        mm = pe.matmul(bank[k][rows, 0:NP2 * NCMP], cw[k][rows, n, :],
                                       a.kT[name][rows, :, n:n + CSTRIDE * (NCMP - 1) + 1:CSTRIDE],
                                       start=(n == 0), stop=(n == CLEN - 1))
            mm.then_inc(done, 1)
            pe.wait_ge(ready, 2)
            for u in range(NP2):
                mm = pe.transpose(bank[2][0:NCMP, u * P:(u + 1) * P], vT[:, u, 0:NCMP], g.c["ident"])
            mm.then_inc(vt_done, 1)

        @block.vector
        def _(dve):
            dve.wait_ge(done, 1)
            dve.tensor_copy(shift[:], bank[4][:, 0:2]).then_inc(shift_ready, 1)
            dve.wait_ge(shift_ready, 1)
            for k, out in enumerate((a.kcmp, vT)):
                dve.tensor_scalar(out[:, :, 0:NCMP], bank[k][:, 0:NP2 * NCMP].rearrange("p (u n) -> p u n", u=NP2),
                                  shift[:, k:k + 1], None, ALU.add).then_inc(ready, 1)
            dve.wait_ge(vt_done, 1)
            dve.tensor_copy(a.vcmp[:].rearrange("n u d -> n (u d)"), bank[2][0:NCMP, 0:NP2 * P]).then_inc(v_ready, 1)


def attention(nc, g, w, a, yT):
    with Part(nc, "att") as s:
        qs = [s.sb(f"qs{p}", [P, SEQ]) for p in range(2)]
        prob = [s.sb(f"prob{p}", [P, 2, SEQ]) for p in range(2)]
        pT = [s.sb(f"pT{b}", [P, NT, SEQ]) for b in range(2)]
        mx, neg = [s.sb(f"mx{p}", [P, 2]) for p in range(2)], [s.sb(f"neg{p}", [P, 2]) for p in range(2)]
        total, inv, coef = [s.sb(f"total{p}", [P, 2]) for p in range(2)], s.sb("inv", [P, 2]), s.sb("coef", [P, 2])
        cmx, csum, cinv, ccoef = (s.sb(k, [P, NT]) for k in ("cmx", "csum", "cinv", "ccoef"))
        cp = s.sb("cprob", [P, NT, 32])
        cpT = s.sb("cprobT", [NCMP, SEQ])
        bS = [[s.ps(f"bS{p}{b}", [P, 512]) for b in range(2)] for p in range(2)]
        bT = [s.ps(f"bT{b}", [P, 512]) for b in range(2)]
        bC, bO = s.ps("bC", [P, 512]), s.ps("bO", [P, 512])
        staged = [s.sem(f"q_staged{p}") for p in range(2)]
        s_done, mx_ready, neg_ready, exp_ready = s.sem("scores_done"), s.sem("mx_ready"), s.sem("neg_ready"), s.sem("exp_ready")
        inv_ready, coef_ready, p_sel, p_win = s.sem("inv_ready"), s.sem("coef_ready"), s.sem("p_sel_ready"), s.sem("p_win_ready")
        t_done, pT_v, pT_a, pv_done, o_copied = s.sem("t_done"), s.sem("pT_sel_ready"), s.sem("pT_win_ready"), s.sem("pv_done"), s.sem("o_copied")
        c_done, c_steps, c_shifted, c_exp, pc_ready, ct_done, cT_ready = (
            s.sem("c_done"), s.sem("c_steps"), s.sem("c_shifted"), s.sem("c_exp"), s.sem("pc_ready"), s.sem("ct_done"), s.sem("cT_ready"))
        block = s.stack.enter_context(nc.Block())
        gates = a.gates[:].rearrange("p i (P a j b) -> p i P a j b", P=NP2, a=2, b=3)

        def heads(eng):
            with eng.Fori(0, NU) as j:
                for pair in range(NP2):
                    for half in range(2):
                        yield 4 * j + 2 * pair + half, j, pair, half

        def following(pair, half):
            return ((pair, 1) if half == 0 else (1, 0) if pair == 0 else (0, 0)), int(pair == 1 and half == 1)

        @block.sync
        def _(sp):
            g.load_wide(sp, w["od_w_out_heads"].rearrange("(c p) n -> p c n", p=P))

        @block.gpsimd
        def _(pool):
            for counter in (p_win,):
                pool.sem_inc(counter, 1)
            pool.tensor_copy(qs[0][:], a.qT[:, 0, :]).then_inc(staged[0], 1)
            for h, j, pair, half in heads(pool):
                if half == 0:
                    pool.wait_ge(s_done, 4 * h + 1)
                    pool.wait_ge(c_done, h + 1)
                    if pair == 0:
                        pool.tensor_copy(qs[1][:], a.qT[:, ds(NU + j, 1), :].rearrange("p o l -> p (o l)")).then_inc(staged[1], 1)
                    else:
                        pool.tensor_copy(qs[0][:], a.qT[:, ds(j + 1, 1), :].rearrange("p o l -> p (o l)")).then_inc(staged[0], 1)
                for i in range(NT):
                    n = 4 * h + i
                    pool.wait_ge(coef_ready, n + 1)
                    pool.tensor_tensor(prob[i % 2][:, 1, 0:(i + 1) * P], prob[i % 2][:, 1, 0:(i + 1) * P],
                                       coef[:, 1:2].to_broadcast([P, (i + 1) * P]), ALU.mult).then_inc(p_win, 1)

        @block.tensor
        def _(pe):
            for counter in (s_done, c_done, t_done, pv_done, ct_done,):
                pe.sem_inc(counter, 1)
            def scores(n, i, pair, half):
                rows = slice(64 * half, 64 * half + 64)
                if type(n) is not int:
                    pe.wait_ge(exp_ready, 2 * n - 2 + 1)
                for b, k in enumerate(("ks", "kw")):
                    out = bS[i % 2][b]
                    pe.matmul(out[:, 0:(i + 1) * P], qs[pair][rows, i * P:(i + 1) * P], a.kT[k][rows, pair, 0:(i + 1) * P],
                              start=True, stop=False)
                    mm = pe.matmul(out[:, i * P:(i + 1) * P], g.c["ident"], g.c["causal"], start=False, stop=True)
                mm.then_inc(s_done, 1)

            def compressed_scores(pair, half):
                rows = slice(64 * half, 64 * half + 64)
                for i in range(NT):
                    pe.matmul(bC[:, i * 32:i * 32 + NCMP], qs[pair][rows, i * P:(i + 1) * P], a.kcmp[rows, pair, 0:NCMP],
                              start=True, stop=False)
                    mm = pe.matmul(bC[:, i * 32:i * 32 + NCMP], g.c["ident"], g.c["cmpmask"][:, i * 32:i * 32 + NCMP], start=False, stop=True)
                mm.then_inc(c_done, 1)

            pe.wait_ge(staged[0], 1)
            compressed_scores(0, 0)
            scores(0, 0, 0, 0)
            scores(1, 1, 0, 0)
            for h, j, pair, half in heads(pe):
                (next_pair, next_half), more = following(pair, half)
                for i in range(NT):
                    n = 4 * h + i
                    if i == 2 and half == 1:
                        pe.wait_ge(staged[next_pair], j + 1 + more)
                    if i < 2:
                        scores(n + 2, i + 2, pair, half)
                    else:
                        scores(n + 2, i - 2, next_pair, next_half)
                    pe.wait_ge(p_sel, n + 1)
                    pe.wait_ge(p_win, n + 1 + 1)
                    pe.wait_ge(pT_v, n + 1)
                    pe.wait_ge(pT_a, n + 1)
                    for b in range(2):
                        for k in range(i + 1):
                            mm = pe.transpose(bT[b][:, k * P:(k + 1) * P], prob[i % 2][:, b, k * P:(k + 1) * P], g.c["ident"])
                    mm.then_inc(t_done, 1)
                    if i == 1:
                        pe.wait_ge(pc_ready, h + 1)
                        for k in range(NT):
                            mm = pe.transpose(bC[0:NCMP, k * P:(k + 1) * P], cp[:, k, 0:NCMP], g.c["ident"])
                        mm.then_inc(ct_done, 1)
                    if i == 2:
                        pe.wait_ge(cT_ready, h + 1)
                        compressed_scores(next_pair, next_half)
                rows = slice(64 * half, 64 * half + 64)
                dims = slice(P * pair + 64 * half, P * pair + 64 * half + 64)
                pe.wait_ge(cT_ready, h + 1)
                pe.wait_ge(o_copied, 2 * j + pair + 1)
                pe.wait_ge(pT_v, 4 * h + 3 + 1)
                pe.wait_ge(pT_a, 4 * h + 3 + 1)
                pe.matmul(bO[rows, :], a.vcmp[:, pair, 64 * half:64 * half + 64], cpT[:, :], start=True, stop=False)
                for k in range(NT - 1):
                    for b in range(2):
                        pe.matmul(bO[rows, k * P:SEQ - P], a.v[:, k, b, dims], pT[b][:, k, k * P:SEQ - P], start=False, stop=False)
                pe.wait_ge(pT_v, 4 * h + 4 + 1)
                pe.wait_ge(pT_a, 4 * h + 4 + 1)
                for k in range(NT):
                    for b in range(2):
                        mm = pe.matmul(bO[rows, SEQ - P:SEQ], a.v[:, k, b, dims], pT[b][:, k, SEQ - P:SEQ],
                                       start=False, stop=(k == NT - 1 and b == 1))
                mm.then_inc(pv_done, 1)

        @block.scalar
        def _(act):
            for counter in (exp_ready, pT_a, o_copied,):
                act.sem_inc(counter, 1)
            def exponentials(n, i):
                act.wait_ge(neg_ready, n + 1)
                if type(n) is not int:
                    act.wait_ge(t_done, n - 1 + 1)
                    act.wait_ge(inv_ready, n - 1 + 1)
                for b in range(2):
                    act.activation(prob[i % 2][:, b, 0:(i + 1) * P], bS[i % 2][b][:, 0:(i + 1) * P], ACT.Exp, scale=SCALE,
                                   bias=neg[i % 2][:, b:b + 1], accum_out=total[i % 2][:, b:b + 1]).then_inc(exp_ready, 1)

            exponentials(0, 0)
            for h, j, pair, half in heads(act):
                act.wait_ge(c_shifted, h + 1)
                act.activation(cp[:, :, 0:NCMP], cp[:, :, 0:NCMP], ACT.Exp, scale=SCALE).then_inc(c_exp, 1)
                for i in range(NT):
                    n = 4 * h + i
                    exponentials(n + 1, (i + 1) % NT)
                    act.wait_ge(t_done, n + 1 + 1)
                    if i == 0:
                        act.wait_ge(pv_done, h + 1)
                    act.activation(pT[1][:, 0:i + 1, i * P:(i + 1) * P], bT[1][:, 0:(i + 1) * P].rearrange("k (c q) -> k c q", q=P),
                                   ACT.Copy).then_inc(pT_a, 1)
                    if i == 1:
                        act.wait_ge(ct_done, h + 1 + 1)
                        act.wait_ge(pv_done, h + 1)
                        act.activation(cpT[:, :], bC[0:NCMP, :], ACT.Copy).then_inc(cT_ready, 1)
                if half == 1:
                    act.wait_ge(pv_done, h + 1 + 1)
                    act.activation(yT[:, ds(NU * pair + j, 1), :].rearrange("p o l -> p (o l)"), bO[:, :], ACT.Copy).then_inc(o_copied, 1)

        @block.vector
        def _(dve):
            for counter in (pT_v, inv_ready,):
                dve.sem_inc(counter, 1)
            def maxima(n, i):
                dve.wait_ge(s_done, n + 1 + 1)
                if type(n) is not int:
                    dve.wait_ge(exp_ready, 2 * n - 2 + 1)
                for b in range(2):
                    dve.tensor_reduce(mx[i % 2][:, b:b + 1], bS[i % 2][b][:, 0:(i + 1) * P], AX.X, ALU.max).then_inc(mx_ready, 1)
                dve.wait_ge(mx_ready, 2 * n + 2)
                dve.tensor_scalar(neg[i % 2][:], mx[i % 2][:], -SCALE, None, ALU.mult).then_inc(neg_ready, 1)

            maxima(0, 0)
            maxima(1, 1)
            for h, j, pair, half in heads(dve):
                dve.wait_ge(c_done, h + 1 + 1)
                dve.wait_ge(ct_done, h + 1)
                scores = bC[:, 0:NT * 32].rearrange("p (i n) -> p i n", n=32)[:, :, 0:NCMP]
                dve.tensor_reduce(cmx[:], scores, AX.X, ALU.max).then_inc(c_steps, 1)
                dve.wait_ge(c_steps, 5 * h + 1)
                dve.tensor_tensor(cp[:, :, 0:NCMP], scores, cmx[:].unsqueeze(2).to_broadcast([P, NT, NCMP]), ALU.subtract).then_inc(c_shifted, 1)
                for i in range(NT):
                    n = 4 * h + i
                    dve.wait_ge(exp_ready, 2 * n + 2 + 1)
                    dve.reciprocal(inv[:], total[i % 2][:]).then_inc(inv_ready, 1)
                    dve.wait_ge(inv_ready, n + 1 + 1)
                    dve.wait_ge(p_win, n + 1)
                    dve.tensor_tensor(coef[:], inv[:], gates[:, i, pair, half, ds(j, 1), 1:3].rearrange("p o b -> p (o b)"),
                                      ALU.mult).then_inc(coef_ready, 1)
                    dve.wait_ge(coef_ready, n + 1)
                    dve.tensor_scalar(prob[i % 2][:, 0, 0:(i + 1) * P], prob[i % 2][:, 0, 0:(i + 1) * P], coef[:, 0:1], None, ALU.mult).then_inc(p_sel, 1)
                    if i == 0:
                        dve.wait_ge(c_exp, h + 1)
                        dve.tensor_reduce(csum[:], cp[:, :, 0:NCMP], AX.X, ALU.add).then_inc(c_steps, 1)
                        dve.wait_ge(c_steps, 5 * h + 2)
                        dve.reciprocal(cinv[:], csum[:]).then_inc(c_steps, 1)
                        dve.wait_ge(c_steps, 5 * h + 3)
                        dve.tensor_tensor(ccoef[:], cinv[:], gates[:, :, pair, half, ds(j, 1), 0:1].rearrange("p i o b -> p (i o b)"),
                                          ALU.mult).then_inc(c_steps, 1)
                        dve.wait_ge(c_steps, 5 * h + 4)
                        dve.tensor_tensor(ccoef[:, 0:1], ccoef[:, 0:1], g.c["anycmp"], ALU.mult).then_inc(c_steps, 1)
                        dve.wait_ge(c_steps, 5 * h + 5)
                        dve.tensor_tensor(cp[:, :, 0:NCMP], cp[:, :, 0:NCMP], ccoef[:].unsqueeze(2).to_broadcast([P, NT, NCMP]),
                                          ALU.mult).then_inc(pc_ready, 1)
                    maxima(n + 2, (i + 2) % NT)
                    dve.wait_ge(t_done, n + 1 + 1)
                    if i == 0:
                        dve.wait_ge(pv_done, h + 1)
                    dve.tensor_copy(pT[0][:, 0:i + 1, i * P:(i + 1) * P],
                                    bT[0][:, 0:(i + 1) * P].rearrange("k (c q) -> k c q", q=P)).then_inc(pT_v, 1)


def program(nc, w, out, where):
    g = Names()
    g.h_dram = [nc.dram_tensor(f"h{layer}", (SEQ, D), F32, kind="Internal").ap() for layer in range(2)]
    g.acc_dram = [nc.dram_tensor(f"acc{layer}", (SEQ + P, D), F32, kind="Internal").ap() for layer in range(2)]
    load_constants(nc, g, w["const_table"], where)
    g.x = nc.alloc_sbuf_tensor("x_sb", [P, NT, D], F32)
    g.xT = nc.alloc_sbuf_tensor("xT", [P, KC, SEQ], F32)
    make_wide(nc, g)
    g.ident_loaded, g.consts_loaded, g.x_loaded = (nc.alloc_semaphore(k) for k in ("ident_loaded", "consts_loaded", "x_loaded"))
    even_mixer(nc, g, w, g.xT)
    out_project_norm(nc, "out0", g, g.xT, w["ln1_g"][0], w["ln1_b"][0])
    moe_layer(nc, g, w, 0)
    odd_mixer(nc, g, w, g.xT)
    out_project_norm(nc, "out1", g, g.xT, w["ln1_g"][1], w["ln1_b"][1])
    moe_layer(nc, g, w, 1, out[0])


AS_THEY_ARE = ["x", "ev_w_in", "s5_w_glu", "ev_w_out", "cmp_w_k", "cmp_w_v", "ln1_g", "ln1_b", "ln2_g", "ln2_b", "router_w",
               "router_b", "ex_w_gate", "ex_w_up", "ex_w_down", "sh_w_gate", "sh_w_up", "sh_w_down"]


def kernel(**inputs):
    import concourse.bacc as bacc
    from concourse.bass_utils import run_bass_kernel_spmd

    w = {k: np.asarray(v) for k, v in inputs.items()}
    arrays = {k: np.ascontiguousarray(w[k]) for k in AS_THEY_ARE}
    arrays["const_table"], where = constant_table()
    arrays["columns"], arrays["b_swapped"], arrays["c_swapped"] = even_layout(w)
    arrays["od_w_in_heads"], arrays["od_w_out_heads"], arrays["pe_columns"] = odd_layout(w)
    nc = bacc.Bacc("TRN2", target_bir_lowering=False, num_devices=1)
    ins = {k: nc.dram_tensor(f"in_{k}", v.shape, mybir.dt.from_np(v.dtype), kind="ExternalInput").ap() for k, v in arrays.items()}
    out = nc.dram_tensor("out", (1, SEQ, D), F32, kind="ExternalOutput").ap()
    program(nc, ins, out, where)
    r = run_bass_kernel_spmd(nc, [{f"in_{k}": v for k, v in arrays.items()}], core_ids=[0])
    return r.results[0]["out"]
```
